# Optimizing a Trainium2 kernel written in Bass

```python
import jax, jax.numpy as jnp
from jax import lax
import numpy as np

D_MODEL = 1024
BATCH = 1
SEQ = 256
DEPTH = 1

GRID_W = 64
CTX_LEN = 256

MLA_HEADS = 8
MLA_Q_RANK = 256
MLA_KV_RANK = 256
MLA_NOPE = 64
MLA_ROPE = 32
MLA_V = 64
MLA_SCALE = (MLA_NOPE + MLA_ROPE) ** -0.5
Q_BLOCK = 128

RET_HEADS = 4
RET_DK = 128
RET_DV = 128
RET_CHUNK = 128

D_FF = 2816
CONV_WIDTH = 3

ROPE_BASE = 10000.0
EPS = 1e-6

MLA_WIDTH = MLA_HEADS * MLA_V
RET_WIDTH = RET_HEADS * RET_DV
MIX_WIDTH = MLA_WIDTH + RET_WIDTH
IN_SIZES = (MLA_Q_RANK, MLA_KV_RANK, MLA_ROPE, RET_HEADS * RET_DK, RET_HEADS * RET_DK, RET_WIDTH, RET_WIDTH)
IN_SPLITS = tuple(int(v) for v in np.cumsum(IN_SIZES)[:-1])
IN_COLS = int(sum(IN_SIZES))


def rmsnorm(x, g):
    xf = x.astype(jnp.float32)
    y = xf * lax.rsqrt(jnp.mean(xf * xf, axis=-1, keepdims=True) + EPS)
    return (y * g.astype(jnp.float32)).astype(x.dtype)

def modulate(h, shift, scale):
    return h * (1.0 + scale) + shift

def rope_angles(pos, dim):
    inv = ROPE_BASE ** (-jnp.arange(0, dim, 2, dtype=jnp.float32) / dim)
    return pos.astype(jnp.float32)[:, None] * inv[None, :]

def apply_rope(x, ang):
    x1, x2 = jnp.split(x, 2, axis=-1)
    cos = jnp.cos(ang)[None, :, None, :].astype(x.dtype)
    sin = jnp.sin(ang)[None, :, None, :].astype(x.dtype)
    return jnp.concatenate([x1 * cos - x2 * sin, x1 * sin + x2 * cos], axis=-1)

def axial_rope(x, pos):
    pos_row, pos_col = pos
    half = x.shape[-1] // 2
    xr = apply_rope(x[..., :half], rope_angles(pos_row, half))
    xc = apply_rope(x[..., half:], rope_angles(pos_col, half))
    return jnp.concatenate([xr, xc], axis=-1)

def split_proj(p):
    return jnp.split(p, IN_SPLITS, axis=-1)

def mla_queries(c_q, g_q, w_uq, pos):
    B, S, _ = c_q.shape
    q = (rmsnorm(c_q, g_q) @ w_uq).reshape(B, S, MLA_HEADS, MLA_NOPE + MLA_ROPE)
    q_nope, q_pe = q[..., :MLA_NOPE], q[..., MLA_NOPE:]
    if pos is not None:
        q_pe = axial_rope(q_pe, pos)
    return jnp.concatenate([q_nope, q_pe], axis=-1)

def mla_keys(c_kv, k_pe, g_kv, w_ukv, pos):
    B, S, _ = c_kv.shape
    kv = (rmsnorm(c_kv, g_kv) @ w_ukv).reshape(B, S, MLA_HEADS, MLA_NOPE + MLA_V)
    k_nope, v = kv[..., :MLA_NOPE], kv[..., MLA_NOPE:]
    k_pe = k_pe[:, :, None, :]
    if pos is not None:
        k_pe = axial_rope(k_pe, pos)
    k_pe = jnp.broadcast_to(k_pe, (B, S, MLA_HEADS, MLA_ROPE))
    return jnp.concatenate([k_nope, k_pe], axis=-1), v

def softmax_attention(q, k, v):
    s = jnp.einsum('bqhd,bkhd->bhqk', q, k).astype(jnp.float32) * MLA_SCALE
    p = jax.nn.softmax(s, axis=-1).astype(v.dtype)
    return jnp.einsum('bhqk,bkhd->bqhd', p, v)

def latent_attention(q, k_lat, v_lat, k_ctx, v_ctx):
    k = jnp.concatenate([k_lat, k_ctx], axis=1)
    v = jnp.concatenate([v_lat, v_ctx], axis=1)
    B, S, H, dq = q.shape
    qb = q.reshape(B, S // Q_BLOCK, Q_BLOCK, H, dq).swapaxes(0, 1)
    o = lax.map(lambda qi: softmax_attention(qi, k, v), qb)
    return o.swapaxes(0, 1).reshape(B, S, H * MLA_V)

def retention_inputs(rq, rk, rv, pos):
    B, S, _ = rq.shape
    q = rq.reshape(B, S, RET_HEADS, RET_DK)
    k = rk.reshape(B, S, RET_HEADS, RET_DK) * (RET_DK ** -0.5)
    v = rv.reshape(B, S, RET_HEADS, RET_DV)
    if pos is not None:
        ang = rope_angles(pos, RET_DK)
        q = apply_rope(q, ang)
        k = apply_rope(k, ang)
    return q, k, v

def retention_final_state(k, v, log_gamma, reverse):
    L = k.shape[1]
    j = jnp.arange(L, dtype=jnp.float32)
    expo = j if reverse else (L - 1.0 - j)
    w = jnp.exp(log_gamma[:, None] * expo[None, :])
    return jnp.einsum('bjhd,hj,bjhe->bhde', k.astype(jnp.float32), w, v.astype(jnp.float32))

def retention_chunkwise(q, k, v, log_gamma, init_state, strict):
    B, S, H, dk = q.shape
    dv = v.shape[-1]
    C = RET_CHUNK
    n = S // C
    idx = jnp.arange(C, dtype=jnp.float32)
    diff = idx[:, None] - idx[None, :]
    mask = (diff > 0) if strict else (diff >= 0)
    expo = jnp.where(mask, diff, 0.0)
    lg = log_gamma.astype(jnp.float32)
    decay_in = jnp.where(mask[None], jnp.exp(lg[:, None, None] * expo[None]), 0.0)
    xi = jnp.exp(lg[:, None] * (idx + 1.0)[None, :])[None, :, :, None]
    zeta = jnp.exp(lg[:, None] * (C - 1.0 - idx)[None, :])[None, :, :, None]
    g_chunk = jnp.exp(lg * C)[None, :, None, None]

    def to_chunks(a):
        return a.astype(jnp.float32).reshape(B, n, C, H, a.shape[-1]).transpose(1, 0, 3, 2, 4)

    def step(state, inp):
        qi, ki, vi = inp
        att = jnp.einsum('bhqd,bhkd->bhqk', qi, ki) * decay_in[None]
        inner = jnp.einsum('bhqk,bhke->bhqe', att, vi)
        cross = jnp.einsum('bhqd,bhde->bhqe', qi, state) * xi
        new_state = state * g_chunk + jnp.einsum('bhkd,bhke->bhde', ki * zeta, vi)
        return new_state, inner + cross

    _, out = lax.scan(step, init_state.astype(jnp.float32), (to_chunks(q), to_chunks(k), to_chunks(v)))
    return out.transpose(1, 0, 3, 2, 4).reshape(B, S, H, dv)

def head_groupnorm(y, g):
    B, S, H, dv = y.shape
    mu = jnp.mean(y, axis=-1, keepdims=True)
    var = jnp.mean(jnp.square(y - mu), axis=-1, keepdims=True)
    yn = ((y - mu) * lax.rsqrt(var + EPS)).reshape(B, S, H * dv)
    return yn * g.astype(jnp.float32)

def retention_bidir(q, k, v, gate, log_gamma, state_f, state_b, g_ret):
    flip = lambda a: jnp.flip(a, axis=1)
    y_f = retention_chunkwise(q, k, v, log_gamma[0], state_f, False)
    y_b = flip(retention_chunkwise(flip(q), flip(k), flip(v), log_gamma[1], state_b, True))
    y = head_groupnorm(y_f + y_b, g_ret)
    return (jax.nn.silu(gate.astype(jnp.float32)) * y).astype(v.dtype)

def conv_ffn(h, w_up, conv_w, conv_b, w_down):
    u = h @ w_up
    u = lax.conv_general_dilated(u, conv_w[:, None, :].astype(u.dtype), window_strides=(1,),
                                 padding=((CONV_WIDTH // 2, CONV_WIDTH // 2),),
                                 dimension_numbers=('NWC', 'WIO', 'NWC'),
                                 feature_group_count=u.shape[-1]) + conv_b
    a, g = jnp.split(u, 2, axis=-1)
    return (jax.nn.silu(g) * a) @ w_down

def first_inputs(seed: int = 0) -> dict:
    key = jax.random.key(seed)
    ks = jax.random.split(key, 21)
    nrm = lambda k, shape, scale: jax.random.normal(k, shape, jnp.float32) * scale
    h = jnp.arange(RET_HEADS, dtype=jnp.float32)
    decay_init = jnp.log(-jnp.log(1.0 - 2.0 ** (-5.0 - h)))
    return {
        'x': nrm(ks[0], (BATCH, SEQ, D_MODEL), 1.0),
        'c': nrm(ks[1], (BATCH, D_MODEL), 1.0),
        'ctx': nrm(ks[2], (BATCH, CTX_LEN, D_MODEL), 1.0),
        'c_ctx': nrm(ks[3], (D_MODEL,), 1.0),
        'w_ada': nrm(ks[4], (DEPTH, D_MODEL, 6 * D_MODEL), 0.5 * D_MODEL ** -0.5),
        'b_ada': nrm(ks[5], (DEPTH, 6 * D_MODEL), 0.02),
        'g_norm1': 1.0 + nrm(ks[6], (DEPTH, D_MODEL), 0.02),
        'w_in': nrm(ks[7], (DEPTH, D_MODEL, IN_COLS), D_MODEL ** -0.5),
        'g_q': 1.0 + nrm(ks[8], (DEPTH, MLA_Q_RANK), 0.02),
        'w_uq': nrm(ks[9], (DEPTH, MLA_Q_RANK, MLA_HEADS * (MLA_NOPE + MLA_ROPE)), MLA_Q_RANK ** -0.5),
        'g_kv': 1.0 + nrm(ks[10], (DEPTH, MLA_KV_RANK), 0.02),
        'w_ukv': nrm(ks[11], (DEPTH, MLA_KV_RANK, MLA_HEADS * (MLA_NOPE + MLA_V)), MLA_KV_RANK ** -0.5),
        'ret_decay': decay_init[None, None, :] + nrm(ks[12], (DEPTH, 2, RET_HEADS), 0.05),
        'g_ret': 1.0 + nrm(ks[13], (DEPTH, RET_WIDTH), 0.02),
        'w_out': nrm(ks[14], (DEPTH, MIX_WIDTH, D_MODEL), MIX_WIDTH ** -0.5),
        'g_norm2': 1.0 + nrm(ks[15], (DEPTH, D_MODEL), 0.02),
        'w_up': nrm(ks[16], (DEPTH, D_MODEL, 2 * D_FF), D_MODEL ** -0.5),
        'conv_w': nrm(ks[17], (DEPTH, CONV_WIDTH, 2 * D_FF), CONV_WIDTH ** -0.5),
        'conv_b': nrm(ks[18], (DEPTH, 2 * D_FF), 0.02),
        'w_down': nrm(ks[19], (DEPTH, D_FF, D_MODEL), D_FF ** -0.5),
        'g_final': 1.0 + nrm(ks[20], (D_MODEL,), 0.02),
    }

def first_block(x, c, ctx, c_ctx, w_ada, b_ada, g_norm1, w_in, g_q, w_uq, g_kv, w_ukv,
              ret_decay, g_ret, w_out, g_norm2, w_up, conv_w, conv_b, w_down, g_final):
    B, S, _ = x.shape
    rows = S // GRID_W
    pos_row = jnp.repeat(jnp.arange(rows, dtype=jnp.int32), GRID_W)
    pos_col = jnp.tile(jnp.arange(GRID_W, dtype=jnp.int32), rows)
    pos_grid = (pos_row, pos_col)
    pos_seq = jnp.arange(S, dtype=jnp.int32)

    for l in range(DEPTH):
        last = l == DEPTH - 1
        mod = jax.nn.silu(c) @ w_ada[l] + b_ada[l]
        sh1, sc1, gt1, sh2, sc2, gt2 = jnp.split(mod[:, None, :], 6, axis=-1)
        mod_c = jax.nn.silu(c_ctx) @ w_ada[l] + b_ada[l]
        shc1, scc1, gtc1, shc2, scc2, gtc2 = jnp.split(mod_c, 6)
        log_gamma = -jnp.exp(ret_decay[l].astype(jnp.float32))

        h = modulate(rmsnorm(x, g_norm1[l]), sh1, sc1)
        hc = modulate(rmsnorm(ctx, g_norm1[l]), shc1, scc1)
        cq, ckv, kpe, rq, rk, rv, rg = split_proj(h @ w_in[l])
        cq_c, ckv_c, kpe_c, rq_c, rk_c, rv_c, rg_c = split_proj(hc @ w_in[l])

        k_c, v_c = mla_keys(ckv_c, kpe_c, g_kv[l], w_ukv[l], None)
        qr_c, kr_c, vr_c = retention_inputs(rq_c, rk_c, rv_c, None)
        st_f = retention_final_state(kr_c, vr_c, log_gamma[0], False)
        st_b = retention_final_state(kr_c, vr_c, log_gamma[1], True)

        q = mla_queries(cq, g_q[l], w_uq[l], pos_grid)
        k, v = mla_keys(ckv, kpe, g_kv[l], w_ukv[l], pos_grid)
        o_mla = latent_attention(q, k, v, k_c, v_c)
        qr, kr, vr = retention_inputs(rq, rk, rv, pos_seq)
        o_ret = retention_bidir(qr, kr, vr, rg, log_gamma, st_f, st_b, g_ret[l])
        o = jnp.concatenate([o_mla, o_ret.astype(o_mla.dtype)], axis=-1) @ w_out[l]
        x_new = x + gt1 * o
        x_new = x_new + gt2 * conv_ffn(modulate(rmsnorm(x_new, g_norm2[l]), sh2, sc2),
                                       w_up[l], conv_w[l], conv_b[l], w_down[l])

        if not last:
            q_c = mla_queries(cq_c, g_q[l], w_uq[l], None)
            o_mla_c = softmax_attention(q_c, k_c, v_c).reshape(B, ctx.shape[1], MLA_WIDTH)
            zero_state = jnp.zeros_like(st_f)
            o_ret_c = retention_bidir(qr_c, kr_c, vr_c, rg_c, log_gamma, zero_state, zero_state, g_ret[l])
            o_c = jnp.concatenate([o_mla_c, o_ret_c.astype(o_mla_c.dtype)], axis=-1) @ w_out[l]
            ctx = ctx + gtc1 * o_c
            ctx = ctx + gtc2 * conv_ffn(modulate(rmsnorm(ctx, g_norm2[l]), shc2, scc2),
                                        w_up[l], conv_w[l], conv_b[l], w_down[l])
        x = x_new

    return rmsnorm(x, g_final)


DEPTH_2 = 2

N_A_LAYERS = DEPTH_2 // 2
N_B_LAYERS = DEPTH_2 - N_A_LAYERS
CHUNK = 128
GMLP_WIDTH = 2 * D_MODEL
GMLP_GROUPS = 16
GMLP_GROUP_DIM = GMLP_WIDTH // GMLP_GROUPS
N_HEADS = 16
HEAD_DIM = D_MODEL // N_HEADS
FFN_HIDDEN = -(-8 * D_MODEL // (3 * 256)) * 256


def rms_norm(x, g):
    xf = x.astype(jnp.float32)
    y = xf * lax.rsqrt(jnp.mean(xf * xf, axis=-1, keepdims=True) + EPS)
    return (y * g.astype(jnp.float32)).astype(x.dtype)

def layer_norm(x, g, b):
    xf = x.astype(jnp.float32)
    mu = jnp.mean(xf, axis=-1, keepdims=True)
    xc = xf - mu
    y = xc * lax.rsqrt(jnp.mean(xc * xc, axis=-1, keepdims=True) + EPS)
    return (y * g.astype(jnp.float32) + b.astype(jnp.float32)).astype(x.dtype)

def modulate_2(h, shift, scale):
    return h * (1 + scale[:, None, :]) + shift[:, None, :]

def swiglu(h, w_gu, w_down):
    gu = h @ w_gu
    g, u = jnp.split(gu, 2, axis=-1)
    return (jax.nn.silu(g) * u) @ w_down

def gmlp_mixer(h, w_in, b_in, ln_g, ln_b, w_s, b_s, w_out):
    B, S, _ = h.shape
    z = jax.nn.gelu(h @ w_in + b_in)
    u, v = jnp.split(z, 2, axis=-1)
    v = layer_norm(v, ln_g, ln_b)
    v = v.reshape(B, S // CHUNK, CHUNK, GMLP_GROUPS, GMLP_GROUP_DIM)
    causal = jnp.tril(jnp.ones((CHUNK, CHUNK), dtype=w_s.dtype))
    ws = w_s * causal[None]
    v = jnp.einsum('gts,bnsgc->bntgc', ws, v) + b_s.T[:, :, None]
    y = u * v.reshape(B, S, GMLP_WIDTH)
    return y @ w_out

def shared_kv(x, mod_kv, kv_norm_g, kv_w, kv_b_f, k_norm_g):
    B, S, _ = x.shape
    shift, scale = jnp.split(mod_kv, 2, axis=-1)
    h = modulate_2(rms_norm(x, kv_norm_g), shift, scale)
    kvf = h @ kv_w
    k = kvf[..., :D_MODEL].reshape(B, S, N_HEADS, HEAD_DIM)
    k = rms_norm(k, k_norm_g).transpose(0, 2, 1, 3)
    v = kvf[..., D_MODEL:2 * D_MODEL].reshape(B, S, N_HEADS, HEAD_DIM).transpose(0, 2, 1, 3)
    f_logit = kvf[..., 2 * D_MODEL:].astype(jnp.float32) + kv_b_f.astype(jnp.float32)
    dcum = jnp.cumsum(jax.nn.log_sigmoid(f_logit), axis=1).transpose(0, 2, 1)
    return k, v, dcum

def fox_attention(q, k, v, dcum):
    B, H, S, Dh = q.shape
    nb = S // Q_BLOCK
    qb = q.reshape(B, H, nb, Q_BLOCK, Dh).transpose(2, 0, 1, 3, 4)
    db = dcum.reshape(B, H, nb, Q_BLOCK).transpose(2, 0, 1, 3)
    kpos = jnp.arange(S)
    scale = HEAD_DIM ** -0.5

    def block(args):
        qi, di, i = args
        qpos = i * Q_BLOCK + jnp.arange(Q_BLOCK)
        logits = jnp.einsum('bhqd,bhkd->bhqk', qi, k).astype(jnp.float32) * scale
        logits = logits + di[..., :, None] - dcum[..., None, :]
        logits = jnp.where(kpos[None, :] <= qpos[:, None], logits, -jnp.inf)
        p = jax.nn.softmax(logits, axis=-1)
        return jnp.einsum('bhqk,bhkd->bhqd', p.astype(v.dtype), v)

    o = lax.map(block, (qb, db, jnp.arange(nb)))
    return o.transpose(1, 2, 0, 3, 4).reshape(B, H, S, Dh)

def fox_mixer(h, w_qg, q_norm_g, w_o, k, v, dcum):
    B, S, _ = h.shape
    qg = h @ w_qg
    q = qg[..., :D_MODEL].reshape(B, S, N_HEADS, HEAD_DIM)
    q = rms_norm(q, q_norm_g).transpose(0, 2, 1, 3)
    gate = jax.nn.sigmoid(qg[..., D_MODEL:])
    o = fox_attention(q, k, v, dcum).transpose(0, 2, 1, 3).reshape(B, S, D_MODEL)
    return (o * gate) @ w_o

def second_inputs(seed: int = 0) -> dict:
    key = jax.random.key(seed)
    ks = jax.random.split(key, 26)
    D, F, GW = D_MODEL, FFN_HIDDEN, GMLP_WIDTH

    def nrm(k, shape, scale):
        return jax.random.normal(k, shape, jnp.float32) * scale

    def gain(k, shape):
        return 1.0 + nrm(k, shape, 0.05)

    return {
        "x": nrm(ks[0], (BATCH, SEQ, D), 1.0),
        "c": nrm(ks[1], (BATCH, D), 1.0),
        "ada_w": nrm(ks[2], (DEPTH_2, D, 6 * D), 0.5 * D ** -0.5),
        "ada_b": nrm(ks[3], (DEPTH_2, 6 * D), 0.01),
        "pre_mix_g": gain(ks[4], (DEPTH_2, D)),
        "post_mix_g": gain(ks[5], (DEPTH_2, D)),
        "pre_ffn_g": gain(ks[6], (DEPTH_2, D)),
        "post_ffn_g": gain(ks[7], (DEPTH_2, D)),
        "ffn_w_gu": nrm(ks[8], (DEPTH_2, D, 2 * F), D ** -0.5),
        "ffn_w_down": nrm(ks[9], (DEPTH_2, F, D), F ** -0.5),
        "a_w_in": nrm(ks[10], (N_A_LAYERS, D, 2 * GW), D ** -0.5),
        "a_b_in": nrm(ks[11], (N_A_LAYERS, 2 * GW), 0.01),
        "a_ln_g": gain(ks[12], (N_A_LAYERS, GW)),
        "a_ln_b": nrm(ks[13], (N_A_LAYERS, GW), 0.01),
        "a_w_s": nrm(ks[14], (N_A_LAYERS, GMLP_GROUPS, CHUNK, CHUNK), 0.5 * CHUNK ** -0.5),
        "a_b_s": 1.0 + nrm(ks[15], (N_A_LAYERS, GMLP_GROUPS, CHUNK), 0.1),
        "a_w_out": nrm(ks[16], (N_A_LAYERS, GW, D), GW ** -0.5),
        "kv_ada_w": nrm(ks[17], (D, 2 * D), 0.5 * D ** -0.5),
        "kv_ada_b": nrm(ks[18], (2 * D,), 0.01),
        "kv_norm_g": gain(ks[19], (D,)),
        "kv_w": nrm(ks[20], (D, 2 * D + N_HEADS), D ** -0.5),
        "kv_b_f": jax.random.uniform(ks[21], (N_HEADS,), jnp.float32, 1.0, 5.0),
        "k_norm_g": gain(ks[22], (HEAD_DIM,)),
        "b_w_qg": nrm(ks[23], (N_B_LAYERS, D, 2 * D), D ** -0.5),
        "b_q_norm_g": gain(ks[24], (N_B_LAYERS, HEAD_DIM)),
        "b_w_o": nrm(ks[25], (N_B_LAYERS, D, D), D ** -0.5),
    }

def second_block(x, c, ada_w, ada_b, pre_mix_g, post_mix_g, pre_ffn_g, post_ffn_g,
              ffn_w_gu, ffn_w_down, a_w_in, a_b_in, a_ln_g, a_ln_b, a_w_s, a_b_s,
              a_w_out, kv_ada_w, kv_ada_b, kv_norm_g, kv_w, kv_b_f, k_norm_g,
              b_w_qg, b_q_norm_g, b_w_o):
    c_act = jax.nn.silu(c)
    k = v = dcum = None
    for layer in range(DEPTH_2):
        mod = c_act @ ada_w[layer] + ada_b[layer]
        sh_m, sc_m, g_m, sh_f, sc_f, g_f = jnp.split(mod, 6, axis=-1)
        h = modulate_2(rms_norm(x, pre_mix_g[layer]), sh_m, sc_m)
        if layer < N_A_LAYERS:
            i = layer
            y = gmlp_mixer(h, a_w_in[i], a_b_in[i], a_ln_g[i], a_ln_b[i],
                           a_w_s[i], a_b_s[i], a_w_out[i])
        else:
            j = layer - N_A_LAYERS
            y = fox_mixer(h, b_w_qg[j], b_q_norm_g[j], b_w_o[j], k, v, dcum)
        x = x + g_m[:, None, :] * rms_norm(y, post_mix_g[layer])
        h = modulate_2(rms_norm(x, pre_ffn_g[layer]), sh_f, sc_f)
        y = swiglu(h, ffn_w_gu[layer], ffn_w_down[layer])
        x = x + g_f[:, None, :] * rms_norm(y, post_ffn_g[layer])
        if layer == N_A_LAYERS - 1:
            k, v, dcum = shared_kv(x, c_act @ kv_ada_w + kv_ada_b, kv_norm_g,
                                   kv_w, kv_b_f, k_norm_g)
    return x


def setup_inputs(seed=0):
    out = dict(first_inputs(seed))
    for name, value in second_inputs(seed + 1).items():
        if name != "x":
            out[name + "_2"] = value
    return out


def reference(
    x, c, ctx, c_ctx, w_ada, b_ada, g_norm1, w_in, g_q, w_uq, g_kv, w_ukv, ret_decay, g_ret,
    w_out, g_norm2, w_up, conv_w, conv_b, w_down, g_final, c_2, ada_w_2, ada_b_2, pre_mix_g_2,
    post_mix_g_2, pre_ffn_g_2, post_ffn_g_2, ffn_w_gu_2, ffn_w_down_2, a_w_in_2, a_b_in_2,
    a_ln_g_2, a_ln_b_2, a_w_s_2, a_b_s_2, a_w_out_2, kv_ada_w_2, kv_ada_b_2, kv_norm_g_2,
    kv_w_2, kv_b_f_2, k_norm_g_2, b_w_qg_2, b_q_norm_g_2, b_w_o_2,
):
    x = first_block(
        x, c, ctx, c_ctx, w_ada, b_ada, g_norm1, w_in, g_q, w_uq, g_kv, w_ukv, ret_decay, g_ret,
        w_out, g_norm2, w_up, conv_w, conv_b, w_down, g_final,
    )
    return second_block(
        x, c_2, ada_w_2, ada_b_2, pre_mix_g_2, post_mix_g_2, pre_ffn_g_2, post_ffn_g_2,
        ffn_w_gu_2, ffn_w_down_2, a_w_in_2, a_b_in_2, a_ln_g_2, a_ln_b_2, a_w_s_2, a_b_s_2,
        a_w_out_2, kv_ada_w_2, kv_ada_b_2, kv_norm_g_2, kv_w_2, kv_b_f_2, k_norm_g_2, b_w_qg_2,
        b_q_norm_g_2, b_w_o_2,
    )


_drawn_inputs = setup_inputs


def setup_inputs(seed=0):
    import zlib

    import numpy as np

    out = dict(_drawn_inputs(seed))
    spreads = {}
    factors = {'g_norm1': 8.0,
     'g_q': 8.0,
     'w_uq': 2.672,
     'g_kv': 8.0,
     'g_ret': 8.0,
     'g_norm2': 8.0,
     'conv_b': 8.0,
     'g_final': 2.728,
     'ada_b_2': 2.688,
     'pre_mix_g_2': 3.007,
     'post_ffn_g_2': 2.966,
     'a_b_in_2': 64.0,
     'a_ln_g_2': 56.347,
     'a_ln_b_2': 64.0,
     'kv_ada_b_2': 8.0,
     'kv_norm_g_2': 4.241,
     'k_norm_g_2': 8.0,
     'b_q_norm_g_2': 7.738,
     'post_mix_g_2': 5.688,
     'a_b_s_2': 7.993}
    for name, (base, spread) in spreads.items():
        noise = np.random.default_rng([zlib.crc32(name.encode()), seed]).standard_normal(out[name].shape)
        drawn = base * np.exp(spread * noise) if base else spread * noise
        out[name] = __import__('jax').numpy.asarray(drawn.astype(out[name].dtype))
    for name, factor in factors.items():
        out[name] = (out[name] * factor).astype(out[name].dtype)
    return out
```

```python
from contextlib import ExitStack

import numpy as np

import concourse.bass as bass
from concourse import mybir

ALU = mybir.AluOpType
ACT = mybir.ActivationFunctionType
AX = mybir.AxisListType
F32 = mybir.dt.float32
F32R = mybir.dt.float32r

P = 128
TOK = 256
NT = TOK // P
D = 1024
KD = D // P
EPS = 1e-6
GRID_W = 64

MLA_H, NOPE, ROPE, MLA_V = 8, 64, 32, 64
QK = NOPE + ROPE
MLA_SCALE = QK ** -0.5
RH, RDK = 4, 128
FF = 2816
NFF = FF // P
NBLK = NFF // 2
GW = 2048
NG = 16
FH, FD = 16, 64
FA = FD + 2
NEG = -1.0e30

UNIT = 2048
RAW = 4
HALF = 512

CONST_PARTS = [("ident", 128), ("ones", 128), ("tri", 128), ("neg", 128), ("pick", 512), ("cos_r", 128),
               ("sin_r", 128), ("cos_m", 32), ("sin_m", 32), ("diff", 512)]
CONST_AT = {}
CONST_W = 0
for _name, _w in CONST_PARTS:
    CONST_AT[_name] = CONST_W
    CONST_W += _w


def shape_constants():
    p = np.arange(P)
    tok = np.arange(TOK)
    c = np.zeros((P, CONST_W), np.float32)

    def put(name, value):
        c[:, CONST_AT[name]:CONST_AT[name] + value.shape[1]] = value

    put("ident", np.eye(P, dtype=np.float32))
    put("ones", np.ones((P, P), np.float32))
    put("tri", (p[:, None] <= p[None, :]).astype(np.float32))
    put("neg", np.where(p[None, :] <= p[:, None], 0.0, NEG).astype(np.float32))
    put("pick", np.repeat((p[:, None] == np.arange(4)[None, :]).astype(np.float32), P, axis=1))
    inv = (np.float32(10000.0) ** (-np.arange(0, RDK, 2, dtype=np.float32) / np.float32(RDK))).astype(np.float32)
    ang = (tok.astype(np.float32)[:, None] * inv[None, :]).astype(np.float32)
    for name, f in (("cos_r", np.cos), ("sin_r", np.sin)):
        put(name, f(ang).astype(np.float32).reshape(NT, P, RDK // 2).transpose(1, 0, 2).reshape(P, -1))
    half = ROPE // 2
    inv = (np.float32(10000.0) ** (-np.arange(0, half, 2, dtype=np.float32) / np.float32(half))).astype(np.float32)
    pos = np.stack([tok // GRID_W, tok % GRID_W], 1).astype(np.float32)
    ang = (pos[:, :, None] * inv[None, None, :]).astype(np.float32)
    for name, f in (("cos_m", np.cos), ("sin_m", np.sin)):
        put(name, f(ang).astype(np.float32).reshape(NT, P, half).transpose(1, 0, 2).reshape(P, -1))
    key = (np.arange(NT)[:, None] * P + p[None, :])
    put("diff", (tok[None, None, :] - key[:, :, None]).astype(np.float32).transpose(1, 0, 2).reshape(P, -1))
    return c


VEC_TILES = [
    [("c", 0, 8), ("c_ctx", 0, 8), ("c_2", 0, 8), ("g_norm1", 0, 8), ("g_q", 0, 2), ("g_kv", 0, 2),
     ("g_ret", 0, 4), ("g_norm2", 0, 8), ("conv_b", 0, 44), ("pre_mix_g_2", 0, 16), ("pre_ffn_g_2", 0, 16)],
    [("conv_w", 0, 88), ("a_b_in_2", 0, 16), ("kv_norm_g_2", 0, 8)],
    [("conv_w", 88 * P, 44)],
]
COL = {}
for _t, _rows in enumerate(VEC_TILES):
    _r = 0
    for _n, _e, _k in _rows:
        COL[(_n, _e)] = _t * P + _r
        _r += _k
VEC_ROWS = [sum(k for _, _, k in rows) for rows in VEC_TILES]

W_IN, W_UQ, W_UKV = 0, 11, 12
W_OUT = 13
UP = [17, 74, 128]
DOWN = [39, 96, 150]
GM_V, GM_U = 50, 58
KV, QG, WO = 107, 116, 124
N_UNITS = 161
DIRECT = (W_UQ, W_UKV)


def split_no(u):
    return u if u < W_UQ else u - len(DIRECT)


N_X, N_CTX, N_RET, N_FF0, N_MIX1, N_FF1, N_KV, N_MIX2, N_FOX, N_FF2 = range(10)
GROUPS = [
    ("first",),
    ("gate_shift", N_FF0), ("scale_gate", N_FF0),
    ("shift_scale", N_MIX1), ("gate_shift", N_FF1), ("scale_gate", N_FF1),
    ("shift_scale", N_KV),
    ("shift_scale", N_MIX2), ("gate_shift", N_FF2), ("scale_gate", N_FF2),
]
GATE_SLOT = {1: 0, 2: 1, 4: 0, 5: 1, 8: 0, 9: 1}
POST_G = {4: 1, 5: 2, 8: 3, 9: 4}
EX_STEPS = [0] + [1 if g[0] == "shift_scale" else 3 for g in GROUPS[1:]]
EX_BASE = [sum(EX_STEPS[:g]) for g in range(len(GROUPS) + 1)]
ADA_AFTER = {}


def _spread(group, at):
    for k, u in enumerate(at):
        ADA_AFTER.setdefault(u, []).append(8 * group + k)


_spread(1, [0, 0, 1, 1, 2, 2, 3, 3])
_spread(2, [7, 7, 8, 8, 9, 9, 10, 10])
_spread(3, range(39, 47))
_spread(4, [51, 52, 53, 54, 55, 56, 57, 57])
_spread(5, range(60, 68))
_spread(6, [92, 93, 94, 95, 96, 96, 97, 97])
_spread(7, range(98, 106))
_spread(8, range(107, 115))
_spread(9, range(116, 124))
EXTRACT_AFTER = {6: 1, 51: 3, 59: 4, 75: 5, 98: 6, 107: 7, 116: 8}
EX_BANKS = {1: (6, 7), 2: (2, 3), 3: (4, 5), 4: (6, 7), 5: (4, 5), 6: (4, 5), 7: (4, 5), 8: (6, 7), 9: (6, 7)}
CREDIT = 4

R_X, R_CTX, R_C, R_RET, R_FF0, R_FIN, R_MIX1, R_LN, R_PM1, R_FF1, R_PF1, R_KV, R_KH, R_QH, R_PM2, R_FF2, R_PF2 = range(17)
R_W = [2, 2, 6, 8, 2, 2, 2, 2, 2, 2, 2, 2, 32, 32, 2, 2, 2]
R_AT = [sum(R_W[:r]) for r in range(len(R_W) + 1)]
SQ_N = [2, 2, 6, 0, 2, 2, 2, 0, 4, 2, 4, 2, 0, 0, 4, 2, 4]
SQ_BASE = [sum(SQ_N[:r]) for r in range(len(SQ_N) + 1)]
XN_NEED = [2, 4, 6, 8, 10, 12, 14, 14, 16, 18]


def build(nc, a, out):
    ctx = ExitStack()
    with ctx:
        def sb(name, shape, dt=F32):
            return ctx.enter_context(nc.sbuf_tensor(name, shape, dt))

        def sem(name):
            return ctx.enter_context(nc.semaphore(name))

        con = sb("con", [P, CONST_AT["diff"]])
        col = sb("col", [P, 3 * P])
        raw = sb("raw", [P, RAW, UNIT])
        wh = sb("wh", [P, 2, UNIT], F32R)
        wl = sb("wl", [P, 2, UNIT], F32R)
        au = sb("au", [P, 2, UNIT])
        acc = sb("acc", [P, UNIT])
        brow = sb("brow", [4, HALF])
        x = sb("x", [P, NT, D])
        gate = sb("gate", [P, 2, D])
        postg = sb("postg", [P, D])
        hraw = sb("hraw", [P, 2, HALF])
        junk = hraw[:, :, :].rearrange("p a c -> p (a c)")
        tmp = junk
        cs = sb("cs", [P, 24])
        mod = sb("mod", [P, 10, 2, KD])
        ss = sb("ss", [P, 128])
        ms = sb("ms", [P, 128])
        rt = sb("rt", [P, 128])
        rs = sb("rs", [P, 128])
        lg = sb("lg", [P, 4, 8])
        bns = sb("bns", [P, 8, 6])
        bna = sb("bna", [P, 8, 2])
        nmax = sb("nmax", [P, 32])
        psumr = sb("psumr", [P, 32])
        prec = sb("prec", [P, 32])
        credit = sb("credit", [P, 4])
        bf = sb("bf", [P, FH])
        gq = sb("gq", [P, 2, FD])
        fz = sb("fz", [P, 6, NT, FH])
        dcum = sb("dcum", [P, NT, FH])
        vrow = junk[:, 0:3 * P].rearrange("p (t c) -> p t c", t=3)

        KB = 1024
        h_at = nc.sbuf_base + (-nc.sbuf_base) % 32
        h_area = sb("h_area", [P, 16 * KB // 4])
        r_at = nc.sbuf_base + (-nc.sbuf_base) % 32
        r_area = sb("r_area", [P, 64 * KB // 4])

        def in_h(name, kb, shape, dt=F32):
            return nc.alloc_sbuf_tensor_at(name, shape, dt, offset=h_at + int(kb * KB))

        def in_r(name, kb, shape, dt=F32):
            return nc.alloc_sbuf_tensor_at(name, shape, dt, offset=r_at + int(kb * KB))

        hh = in_h("hh", 0, [P, KD, TOK], F32R)
        hl = in_h("hl", 8, [P, KD, TOK], F32R)
        m1 = in_h("m1", 0, [2, UNIT])
        xn = in_r("xn", 52, [P, NT, D])
        ch = in_r("ch", 0, [P, KD, TOK], F32R)
        cl = in_r("cl", 8, [P, KD, TOK], F32R)
        cx = in_r("cx", 16, [P, NT, D])
        xn_c = in_r("xn_c", 24, [P, NT, D])
        cqkv = in_r("cqkv", 32, [P, 6, 256])
        kpe = in_r("kpe", 38, [P, 4, ROPE])
        rk = in_r("rk", 40, [P, 4, HALF])
        rv = in_r("rv", 48, [P, 4, HALF])
        rq = in_r("rq", 56, [P, NT, HALF])
        rg = in_r("rg", 60, [P, NT, HALF])
        rtmp = hraw[:, 0, :]
        rtmp_pool = hraw[:, 1, :]
        kt_m = in_r("kt_m", 0, [QK, MLA_H, 2 * TOK])
        qt_m = in_r("qt_m", 16, [QK, MLA_H, TOK])
        v_m = in_r("v_m", 24, [P, 4, MLA_H, MLA_V])
        o = in_r("o", 32, [P, NT, D])
        cn = in_h("cn", 0, [P, 6, 256])
        cqt = in_h("cqt", 6, [P, 2, TOK])
        ckt = in_h("ckt", 8, [P, 2, 2 * TOK])
        qk_st = in_h("qk_st", 0, [P, 2, MLA_H, QK])
        prob = in_h("prob", 8, [P, 2, HALF])
        prob_t = in_h("prob_t", 12, [P, 2, HALF])
        rqt = in_r("rqt", 0, [P, RH, TOK])
        rkt = in_r("rkt", 4, [P, RH, 2 * TOK])
        mask = in_r("mask", 12, [P, RH, 4, TOK])
        mt = in_r("mt", 28, [P, 2, TOK])
        diff = in_r("diff", 30, [P, NT, TOK])
        pr = in_h("pr", 0, [P, 2, 4, TOK])
        gh = in_r("gh", 0, [P, NFF, TOK], F32R)
        gl = in_r("gl", 22, [P, NFF, TOK], F32R)
        hu = in_r("hu", 44, [P, 2, 2, TOK])
        sl = in_r("sl", 48, [P, 2, TOK])
        hid = in_r("hid", 50, [P, 2, TOK])
        vg = in_r("vg", 0, [P, NT, GW])
        wsr = in_r("wsr", 16, [P, NG, P])
        yh = in_r("yh", 16, [P, 2, 4, TOK], F32R)
        yl = in_r("yl", 24, [P, 2, 4, TOK], F32R)
        wst = in_r("wst", 32, [P, NG, P])
        bc = in_r("bc", 40, [P, 4, HALF])
        ub = in_r("ub", 48, [P, 4, TOK])
        yr = in_r("yr", 52, [P, 4, TOK])
        kt_f = in_r("kt_f", 0, [FA, FH, TOK])
        qt_f = in_r("qt_f", 16, [FA, FH, TOK])
        v_f = in_r("v_f", 32, [P, NT, D])
        k_st = in_r("k_st", 40, [P, NT, D])
        ka = in_r("ka", 16, [P, NT, FH, FA])
        ksq = in_r("ksq", 25, [P, D])
        q_st = in_r("q_st", 48, [P, NT, D])
        qa = in_h("qa", 0, [P, NT, FH, FA])
        qsq = in_h("qsq", 9, [P, D])
        prob_f = in_h("prob_f", 0, [P, 2, 384])
        prob_ft = in_h("prob_ft", 3, [P, 2, 384])
        sg = in_r("sg", 56, [P, NT, D])
        o_f = in_r("o_f", 40, [P, NT, D])

        ps = ctx.enter_context(nc.psum_tensor("ps", [P, 8, HALF], F32))

        def const(name):
            at = CONST_AT[name]
            return con[:, at:at + dict(CONST_PARTS)[name]]

        ident, ones = const("ident"), const("ones")
        tri, neg = const("tri"), const("neg")
        pick = const("pick").rearrange("p (r c) -> p r c", r=4)
        cos_r = const("cos_r").rearrange("p (t c) -> p t c", t=NT)
        sin_r = const("sin_r").rearrange("p (t c) -> p t c", t=NT)
        cos_m = const("cos_m").rearrange("p (t a c) -> p t a c", t=NT, a=2)
        sin_m = const("sin_m").rearrange("p (t a c) -> p t a c", t=NT, a=2)

        def column(name, first=0, k=0):
            at = COL[(name, first)] + k
            return col[:, at:at + 1]

        def columns(name, k, n, first=0):
            at = COL[(name, first)] + k
            return col[:, at:at + n]

        def bcast(ap, at, n):
            ap = ap.unsqueeze(at)
            shape = list(ap.shape)
            shape[at] = n
            return ap.broadcast_to(tuple(shape))

        in_const = sem("in_const")
        in_rows = sem("in_rows")
        in_x = sem("in_x")
        in_ctx = sem("in_ctx")
        in_small = sem("in_small")
        raw_loaded = [sem(f"raw_loaded{i}") for i in range(RAW)]
        au_loaded = [sem(f"au_loaded{i}") for i in range(2)]
        brow_loaded = sem("brow_loaded")
        postg_loaded = sem("postg_loaded")
        bc_loaded = [sem(f"bc_loaded{i}") for i in range(4)]
        ws_loaded = sem("ws_loaded")
        hi_done = sem("hi_done")
        lo_done = sem("lo_done")
        w_used = sem("w_used")
        acc_step = sem("acc_step")
        ex_done = sem("ex_done")
        ex_taken = sem("ex_taken")
        cols_turned = sem("cols_turned")
        cols_ready = sem("cols_ready")
        cs_ready = sem("cs_ready")
        mod1_used = sem("mod1_used")
        m1_ready = sem("m1_ready")
        m1_turned = sem("m1_turned")
        mod1_ready = sem("mod1_ready")
        lg_exp = sem("lg_exp")
        lg_ready = sem("lg_ready")
        sq_done = sem("sq_done")
        ms_ready = sem("ms_ready")
        rt_ready = sem("rt_ready")
        xn_ready = sem("xn_ready")
        x_ready = sem("x_ready")
        turned = sem("turned")
        t_raw = sem("t_raw")
        t_hi = sem("t_hi")
        t_lo = sem("t_lo")
        evac = sem("evac")
        dve_step = sem("dve_step")
        act_step = sem("act_step")
        pool_step = sem("pool_step")
        cn_ready = sem("cn_ready")
        c_turned = sem("c_turned")
        ct_ready = sem("ct_ready")
        q_proj = sem("q_proj")
        q_evac = sem("q_evac")
        q_roped = sem("q_roped")
        q_turned = sem("q_turned")
        qt_ready = sem("qt_ready")
        kv_proj = sem("kv_proj")
        k_evac = sem("k_evac")
        v_evac = sem("v_evac")
        kpe_roped = sem("kpe_roped")
        k_full = sem("k_full")
        diff_loaded = sem("diff_loaded")
        k_turned = sem("k_turned")
        kt_ready = sem("kt_ready")
        score = sem("score")
        max_ready = sem("max_ready")
        p_ready = sem("p_ready")
        p_turned = sem("p_turned")
        pt_ready = sem("pt_ready")
        pv_done = sem("pv_done")
        ret_roped = sem("ret_roped")
        r_turned = sem("r_turned")
        rt_evac = sem("rt_evac")
        arg_ready = sem("arg_ready")
        mask_exp = sem("mask_exp")
        mask_ready = sem("mask_ready")
        att_done = sem("att_done")
        pr_ready = sem("pr_ready")
        y_done = sem("y_done")
        up_done = sem("up_done")
        conv_base = sem("conv_base")
        conv_mid = sem("conv_mid")
        silu_done = sem("silu_done")
        hid_pool = sem("hid_pool")
        hid_dve = sem("hid_dve")
        gh_done = sem("gh_done")
        gl_done = sem("gl_done")
        v_added = sem("v_added")
        v_gelu = sem("v_gelu")
        affine = sem("affine")
        ws_turned = sem("ws_turned")
        wst_ready = sem("wst_ready")
        ub_ready = sem("ub_ready")
        sp_done = sem("sp_done")
        yr_ready = sem("yr_ready")
        yh_ready = sem("yh_ready")
        yl_ready = sem("yl_ready")
        f_act = sem("f_act")
        f_pre = sem("f_pre")
        ls_ready = sem("ls_ready")
        cum_done = sem("cum_done")
        ka_ready = sem("ka_ready")
        qa_ready = sem("qa_ready")
        f_turned = sem("f_turned")
        ft_evac = sem("ft_evac")
        fs_done = sem("fs_done")
        fm_ready = sem("fm_ready")
        fp_ready = sem("fp_ready")
        fp_turned = sem("fp_turned")
        fpt_ready = sem("fpt_ready")
        fpv_done = sem("fpv_done")
        fo_ready = sem("fo_ready")
        out_sent = sem("out_sent")

        def k_major(w, k0, k1, c0, c1):
            return w[k0 * P:k1 * P, c0:c1].rearrange("(k p) n -> p k n", p=P)

        def pair_blocks(w, b, h):
            v = w.rearrange("(k p) (s n) -> p k s n", p=P, s=2)
            return v[:, 4 * h:4 * h + 4, :, bass.ds(b * 256, 256)]

        w_in = a["w_in"][0]
        units = []
        for c0 in (0, 544 + 512, 544 + 1024, 544, 544 + 1536):
            units += [k_major(w_in, 4 * h, 4 * h + 4, c0, c0 + 512) for h in range(2)]
        units.append(k_major(w_in, 0, KD, 512, 544))
        units.append(k_major(a["w_uq"][0], 0, 2, 0, MLA_H * QK))
        units.append(k_major(a["w_ukv"][0], 0, 2, 0, 1024))
        units += [k_major(a["w_out"][0], 2 * j, 2 * j + 2, 0, D) for j in range(4)]
        up_w = [a["w_up"][0], a["ffn_w_gu_2"][0], a["ffn_w_gu_2"][1]]
        down_w = [a["w_down"][0], a["ffn_w_down_2"][0], a["ffn_w_down_2"][1]]

        def ffn_units(f):
            got = [("up", f, b, h) for b in range(NBLK) for h in range(2)]
            return got + [k_major(down_w[f], 2 * j, 2 * j + 2, 0, D) for j in range(NBLK)]

        units += ffn_units(0)
        a_in, a_out = a["a_w_in_2"][0], a["a_w_out_2"][0]
        for b in range(4):
            units += [k_major(a_in, 4 * h, 4 * h + 4, GW + b * 512, GW + b * 512 + 512) for h in range(2)]
        for b in range(5):
            if b < 4:
                units += [k_major(a_in, 4 * h, 4 * h + 4, b * 512, b * 512 + 512) for h in range(2)]
            if b > 0:
                units += [k_major(a_out, 4 * (b - 1) + 2 * h, 4 * (b - 1) + 2 * h + 2, 0, D) for h in range(2)]
        units += ffn_units(1)
        for b in range(4):
            units += [k_major(a["kv_w_2"], 4 * h, 4 * h + 4, b * 512, b * 512 + 512) for h in range(2)]
        units.append(k_major(a["kv_w_2"], 0, KD, 2048, 2048 + FH))
        for b in range(4):
            units += [k_major(a["b_w_qg_2"][0], 4 * h, 4 * h + 4, b * 512, b * 512 + 512) for h in range(2)]
        units += [k_major(a["b_w_o_2"][0], 2 * j, 2 * j + 2, 0, D) for j in range(4)]
        units += ffn_units(2)
        assert len(units) == N_UNITS

        def width(u):
            if isinstance(units[u], tuple):
                return UNIT
            return units[u].shape[1] * units[u].shape[2]

        ada = []
        for g in range(10):
            if g < 3:
                w, bias, c0 = a["w_ada"][0], a["b_ada"][0], g * 2048
            elif g < 6:
                w, bias, c0 = a["ada_w_2"][0], a["ada_b_2"][0], (g - 3) * 2048
            elif g == 6:
                w, bias, c0 = a["kv_ada_w_2"], a["kv_ada_b_2"], 0
            else:
                w, bias, c0 = a["ada_w_2"][1], a["ada_b_2"][1], (g - 7) * 2048
            ada.append((w[:, c0:c0 + 2048], bias[c0:c0 + 2048].rearrange("(r c) -> r c", r=4)))

        taken = []

        block = ctx.enter_context(nc.Block())

        @block.vector
        def _(dve):
            steps = [0]

            def link(ins):
                steps[0] += 1
                ins.then_inc(dve_step, 1)
                dve.wait_ge(dve_step, steps[0])

            def lo_part(u, s, i=None):
                more = 0 if i is None else 4 * i
                dve.wait_ge(hi_done, s + 1 + more)
                n = width(u)
                nc.vector.tensor_tensor(wl[:, s % 2, 0:n], raw[:, u % RAW, 0:n], wh[:, s % 2, 0:n].bitcast(F32),
                                        ALU.subtract).then_inc(lo_done, 1)

            def ada_part(v):
                g, k = v // 8, v % 8
                dve.wait_ge(au_loaded[v % 2], 16 * (v // 2 + 1))
                at = (16 if g > 2 else 0) + k
                if k == 0:
                    if g > 1:
                        dve.wait_ge(ex_done, EX_BASE[g])
                    nc.vector.tensor_scalar(acc[:, :], au[:, v % 2, :], cs[:, at:at + 1], None,
                                            ALU.mult).then_inc(acc_step, 1)
                else:
                    dve.wait_ge(acc_step, v - 8)
                    nc.vector.scalar_tensor_tensor(acc[:, :], au[:, v % 2, :], cs[:, at:at + 1], acc[:, :],
                                                   ALU.mult, ALU.add).then_inc(acc_step, 1)
                taken.append(("a", v))

            def extract(g, ba, bb):
                kind, n = GROUPS[g]
                e = EX_BASE[g]
                dve.wait_ge(ex_done, e + 1)
                gains = {N_FF0: ("g_norm2", 0), N_MIX1: ("pre_mix_g_2", 0), N_FF1: ("pre_ffn_g_2", 0),
                         N_KV: ("kv_norm_g_2", 0), N_MIX2: ("pre_mix_g_2", 8), N_FF2: ("pre_ffn_g_2", 8)}[n]
                gain = columns(gains[0], gains[1], KD)
                if kind == "shift_scale":
                    nc.vector.tensor_copy(mod[:, n, 1, :], ps[:, ba, 0:8])
                    nc.vector.scalar_tensor_tensor(mod[:, n, 0, :], ps[:, ba, 8:16], 1.0, gain, ALU.add,
                                                   ALU.mult).then_inc(ex_taken, 1)
                    return
                if kind == "gate_shift":
                    nc.vector.tensor_copy(mod[:, n, 1, :], ps[:, ba, 0:8]).then_inc(ex_taken, 1)
                else:
                    nc.vector.scalar_tensor_tensor(mod[:, n, 0, :], ps[:, ba, 0:8], 1.0, gain, ALU.add,
                                                   ALU.mult).then_inc(ex_taken, 1)
                if g in POST_G:
                    dve.wait_ge(postg_loaded, 16 * (POST_G[g] + 1))
                for h, bank in ((0, bb), (1, ba)):
                    dve.wait_ge(ex_done, e + 2 + h)
                    to = gate[:, GATE_SLOT[g], h * HALF:(h + 1) * HALF]
                    if g in POST_G:
                        ins = nc.vector.tensor_tensor(to, ps[:, bank, :], postg[:, h * HALF:(h + 1) * HALF], ALU.mult)
                    else:
                        ins = nc.vector.tensor_copy(to, ps[:, bank, :])
                    ins.then_inc(ex_taken, 1)

            def take(u):
                if u >= N_UNITS:
                    return
                if u not in DIRECT:
                    lo_part(u, split_no(u))
                taken.append(("w", u))
                if u in EXTRACT_AFTER:
                    g = EXTRACT_AFTER[u]
                    extract(g, *EX_BANKS[g])
                for v in ADA_AFTER.get(u, ()):
                    ada_part(v)

            def rstd(r, scale, src=None):
                c0, c1 = R_AT[r], R_AT[r + 1]
                nc.vector.tensor_scalar(ms[:, c0:c1], ss[:, c0:c1] if src is None else src, scale, EPS, ALU.mult,
                                        ALU.add).then_inc(ms_ready, 1)
                dve.wait_ge(rt_ready, r + 1)
                link(nc.vector.reciprocal(rs[:, c0:c1], rt[:, c0:c1]))

            def rs_of(r, k):
                return rs[:, R_AT[r] + k:R_AT[r] + k + 1]

            def normalise(r, src, dst):
                dve.wait_ge(sq_done, SQ_BASE[r + 1])
                rstd(r, 1.0 / D)
                for t in range(NT):
                    nc.vector.tensor_scalar(dst[:, t, :], src[:, t, :], rs_of(r, t), None,
                                            ALU.mult).then_inc(xn_ready, 1)

            def low_of_turned(n, lo=None, hi=None):
                lo, hi = lo or hl, hi or hh
                for b in range(4):
                    dve.wait_ge(t_hi, 4 * n + b + 1)
                    nc.vector.tensor_tensor(lo[:, 2 * b:2 * b + 2, :],
                                            hraw[:, b % 2, :].rearrange("p (k t) -> p k t", k=2),
                                            hi[:, 2 * b:2 * b + 2, :].bitcast(F32), ALU.subtract).then_inc(t_lo, 1)

            def residual(last_unit, slot, r=None, done=1):
                if r is None:
                    dve.wait_ge(w_used, split_no(last_unit) + 1)
                else:
                    dve.wait_ge(sq_done, SQ_BASE[r + 1])
                    c = R_AT[r]
                    link(nc.vector.tensor_tensor(ss[:, c:c + 2], ss[:, c:c + 3:2], ss[:, c + 1:c + 4:2], ALU.add))
                    rstd(r, 1.0 / D)
                for q in range(4):
                    t, cb = q // 2, q % 2
                    to = x[:, t, cb * HALF:(cb + 1) * HALF]
                    g = gate[:, slot, cb * HALF:(cb + 1) * HALF]
                    part = tmp[:, (q % 2) * HALF:(q % 2 + 1) * HALF]
                    if r is None:
                        link(nc.vector.tensor_tensor(part, ps[:, q, :], g, ALU.mult))
                    else:
                        link(nc.vector.scalar_tensor_tensor(part, ps[:, q, :], rs_of(r, t), g, ALU.mult, ALU.mult))
                    ins = nc.vector.tensor_tensor(to, to, part, ALU.add)
                    if q < 3:
                        link(ins)
                    else:
                        ins.then_inc(x_ready, 1)
                        dve.wait_ge(x_ready, done)

            nc.vector.memset(nmax[:, :], 0.0).then_inc(hid_dve, CREDIT)
            dve.wait_ge(cols_turned, 3)
            for t, rows in enumerate(VEC_ROWS):
                ins = nc.vector.tensor_copy(col[:, t * P:t * P + rows], ps[:, 7, t * P:t * P + rows])
            ins.then_inc(cols_ready, 1)
            dve.wait_ge(cols_ready, 1)
            nc.vector.memset(mod[:, N_RET, 0, 0:4], 1.0)
            nc.vector.tensor_copy(mod[:, N_RET, 0, 4:8], columns("g_ret", 0, 4))
            nc.vector.memset(mod[:, N_RET, 1, :], 0.0)
            nc.vector.memset(mod[:, N_FOX, 0, :], 1.0)
            link(nc.vector.memset(mod[:, N_FOX, 1, :], 0.0))
            dve.wait_ge(lg_exp, 1)
            nc.vector.tensor_scalar(lg[:, 0, :], lg[:, 1, :], -1.0, None, ALU.mult)
            nc.vector.tensor_scalar(lg[:, 2, :], lg[:, 1, :], -float(TOK), None, ALU.mult).then_inc(lg_ready, 1)
            normalise(R_X, x, xn)
            normalise(R_CTX, cx, xn_c)
            dve.wait_ge(mod1_used, 8)
            for q in range(4):
                ins = nc.vector.tensor_copy(m1[0:2, q * HALF:(q + 1) * HALF], ps[0:2, q, :])
            ins.then_inc(m1_ready, 1)
            dve.wait_ge(m1_turned, 1)
            m1t = ps[:, 6, 0:32].rearrange("p (k j) -> p k j", j=2)
            for j, n in ((0, N_X), (1, N_CTX)):
                nc.vector.tensor_copy(mod[:, n, 1, :], m1t[:, 0:8, j])
                ins = nc.vector.scalar_tensor_tensor(mod[:, n, 0, :], m1t[:, 8:16, j], 1.0,
                                                     columns("g_norm1", 0, KD), ALU.add, ALU.mult)
            ins.then_inc(mod1_ready, 1)
            taken.extend(("a", v) for v in range(8))
            take(0)
            take(1)
            low_of_turned(N_X)
            low_of_turned(N_CTX, cl, ch)
            for u in range(2, 13):
                take(u)
            take(13)
            take(14)

            dve.wait_ge(sq_done, SQ_BASE[R_C + 1])
            rstd(R_C, 1.0 / 256)
            for j in range(6):
                nc.vector.tensor_scalar(cn[:, j, :], cqkv[:, j, :], rs_of(R_C, j), None,
                                        ALU.mult).then_inc(cn_ready, 1)

            def rope_m(xv, t, h, first, buf):
                c, s = cos_m[:, t], sin_m[:, t]
                if h > 1:
                    c, s = bcast(c, 1, h), bcast(s, 1, h)
                x1, x2 = xv[..., 0:8], xv[..., 8:16]
                w = [buf[:, j] for j in range(4)]
                nc.vector.tensor_tensor(w[0], x1, c, ALU.mult)
                nc.vector.tensor_tensor(w[1], x2, s, ALU.mult)
                nc.vector.tensor_tensor(w[2], x1, s, ALU.mult)
                link(nc.vector.tensor_tensor(w[3], x2, c, ALU.mult))
                nc.vector.tensor_tensor(x1, w[0], w[1], ALU.subtract)
                return nc.vector.tensor_tensor(x2, w[2], w[3], ALU.add)

            rope_buf = rtmp.rearrange("p (j h a c) -> p j h a c", j=4, h=MLA_H, a=2)
            dve.wait_ge(evac, 17)
            for t in range(NT):
                xv = kpe[:, t, :].rearrange("p (a c) -> p a c", a=2)
                ins = rope_m(xv, t, 1, False, rope_buf[:, :, 0])
                if t == 0:
                    link(ins)
            ins.then_inc(kpe_roped, 1)
            dve.wait_ge(kpe_roped, 1)
            for t in range(NT):
                dve.wait_ge(q_evac, 2 * t + 2)
                xv = qk_st[:, t, :, NOPE:QK].rearrange("p h (a c) -> p h a c", a=2)
                ins = rope_m(xv, t, MLA_H, False, rope_buf)
                ins.then_inc(q_roped, 1)
                dve.wait_ge(q_roped, t + 1)
            for t in range(4):
                for half in range(2):
                    dve.wait_ge(kv_proj, 2 * t + half + 1)
                    src = ps[:, 4 + 2 * (t % 2) + half, :].rearrange("p (h c) -> p h c", h=4)
                    dve.wait_ge(k_evac, 2 * t + half + 1)
                    nc.vector.tensor_copy(v_m[:, t, 4 * half:4 * half + 4, :], src[:, :, NOPE:]).then_inc(v_evac, 1)
                nc.vector.tensor_copy(qk_st[:, t % 2, :, NOPE:QK], bcast(kpe[:, t, :], 1, MLA_H)).then_inc(k_full, 1)

            def head_max(it):
                dve.wait_ge(score, it + 1)
                nc.vector.tensor_reduce(nmax[:, it:it + 1], ps[:, 4 + it % 2, :], AX.X, ALU.max,
                                        negate=True).then_inc(max_ready, 1)

            head_max(0)
            for it in range(2 * MLA_H):
                if it + 1 < 2 * MLA_H:
                    head_max(it + 1)
                dve.wait_ge(p_turned, it + 1)
                if it >= 2:
                    dve.wait_ge(pv_done, it - 1)
                nc.vector.tensor_copy(prob_t[:, it % 2, :], ps[:, 6 + it % 2, :]).then_inc(pt_ready, 1)
            dve.wait_ge(p_ready, 2 * MLA_H)
            link(nc.vector.reciprocal(prec[:, 0:16], psumr[:, 0:16]))
            dve.wait_ge(pv_done, 2 * MLA_H)
            for t in range(NT):
                nc.vector.tensor_tensor(o[:, t, 0:HALF].rearrange("p (h c) -> p h c", h=MLA_H),
                                        ps[:, t, :].rearrange("p (h c) -> p h c", h=MLA_H),
                                        bcast(prec[:, t:16:2], 2, MLA_V), ALU.mult)
            d2 = diff[:, :, :]
            dve.wait_ge(diff_loaded, 16)
            for h in range(RH):
                link(nc.vector.tensor_scalar(mask[:, h, 0:2, :], d2, lg[:, 1, 4 + h:5 + h], None, ALU.mult))
                nc.vector.scalar_tensor_tensor(mask[:, h, 0:2, :], d2, lg[:, 0, h:h + 1], mask[:, h, 0:2, :],
                                               ALU.mult, ALU.min).then_inc(arg_ready, 1)
            for h in range(RH):
                dve.wait_ge(mask_ready, h + 1)
                for half in range(2):
                    dve.wait_ge(att_done, 2 * h + half + 1)
                    if h >= 2:
                        dve.wait_ge(y_done, h - 1)
                    bank = 4 + 2 * (h % 2) + half
                    nc.vector.tensor_tensor(pr[:, h % 2, 2 * half:2 * half + 2, :],
                                            ps[:, bank, :].rearrange("p (k t) -> p k t", k=2),
                                            mask[:, h, 2 * half:2 * half + 2, :], ALU.mult).then_inc(pr_ready, 1)
            dve.wait_ge(y_done, RH)
            for t in range(NT):
                for h in range(RH):
                    ins = nc.vector.bn_stats(bns[:, t * RH + h, :], ps[:, t, h * RDK:(h + 1) * RDK])
            link(ins)
            for j in range(NT * RH):
                ins = nc.vector.bn_aggr(bna[:, j, :], bns[:, j, :])
            link(ins)
            rstd(R_RET, 1.0, bna[:, :, 1])
            for t in range(NT):
                for h in range(RH):
                    j = t * RH + h
                    ins = nc.vector.tensor_scalar(o[:, t, HALF + h * RDK:HALF + (h + 1) * RDK],
                                                  ps[:, t, h * RDK:(h + 1) * RDK], bna[:, j, 0:1], rs_of(R_RET, j),
                                                  ALU.subtract, ALU.mult)
                link(ins)
                nc.vector.tensor_tensor(o[:, t, HALF:], o[:, t, HALF:], rg[:, t, :], ALU.mult).then_inc(xn_ready, 1)
            extract(2, *EX_BANKS[2])
            low_of_turned(N_RET)
            take(15)
            take(16)
            take(17)
            take(18)
            residual(W_OUT + 3, 0, done=1)
            normalise(R_FF0, x, xn)
            low_of_turned(N_FF0)

            def conv(pp, c, i=None):
                more = 0 if i is None else 4 * i
                dve.wait_ge(conv_base, 2 * (pp + 1) + 2 * more)
                bank = 4 + pp % 4

                def tap(which, half):
                    k = COL[("conv_w", 0 if which == 0 else 88 * P)] + half * NFF + pp
                    w = col[:, bass.ds(k + more, 1)] if i is not None else col[:, k:k + 1]
                    if which == 0:
                        to, src = hu[:, c, half, 1:TOK], ps[:, bank, half * TOK:half * TOK + TOK - 1]
                    else:
                        to, src = hu[:, c, half, 0:TOK - 1], ps[:, bank, half * TOK + 1:half * TOK + TOK]
                    return nc.vector.scalar_tensor_tensor(to, src, w, to, ALU.mult, ALU.add)

                for n, (which, half) in enumerate(((0, 0), (0, 1), (2, 0), (2, 1))):
                    if n == 2:
                        dve.wait_ge(conv_mid, 4 * pp + 1 + 4 * more)
                    if n == 3:
                        dve.wait_ge(conv_mid, 4 * pp + 2 + 4 * more)
                    tap(which, half).then_inc(conv_mid, 1)

            def gated(f, pp, c, i=None):
                more = 0 if i is None else 4 * i
                dve.wait_ge(silu_done, NFF * f + pp + 1 + more)
                dve.wait_ge(gl_done, NFF * f + pp - 1 + CREDIT + more)
                nc.vector.tensor_tensor(hid[:, c, :], sl[:, c, :], ps[:, 4 + pp % 4, TOK:], ALU.mult)\
                    .then_inc(hid_dve, 1)

            def ffn(f):
                u0, s0 = UP[f], split_no(UP[f])
                pair = (lambda pp, c, i=None: conv(pp, c, i)) if f == 0 else \
                    (lambda pp, c, i=None: gated(f, pp, c, i))
                base = 2
                with dve.Fori(0, 4) as i:
                    for j in range(4):
                        lo_part(u0 + j + base, s0 + j + base, i)
                        pair(j, j % 2, i)
                for i in range(4):
                    taken.extend(("w", u0 + base + 4 * i + j) for j in range(4))
                for pp in range(16, NFF):
                    take(u0 + base + pp)
                    pair(pp, pp % 2)
                for j in range(NBLK):
                    take(DOWN[f] + j + base)

            ffn(0)
            residual(DOWN[0] + 10, 1, done=2)
            dve.wait_ge(sq_done, SQ_BASE[R_FIN + 1])
            rstd(R_FIN, 1.0 / D)
            dve.wait_ge(postg_loaded, 16)
            for t in range(NT):
                ins = nc.vector.scalar_tensor_tensor(x[:, t, :], x[:, t, :], rs_of(R_FIN, t), postg[:, :], ALU.mult,
                                                     ALU.mult)
            ins.then_inc(x_ready, 1)
            dve.wait_ge(x_ready, 3)
            normalise(R_MIX1, x, xn)
            low_of_turned(N_MIX1)
            for b in range(4):
                for t in range(NT):
                    dve.wait_ge(w_used, split_no(GM_V + 2 * b + 1) + 1)
                    if t == 0:
                        dve.wait_ge(bc_loaded[b], 16)
                    nc.vector.tensor_tensor(vg[:, t, b * HALF:(b + 1) * HALF], ps[:, 4 + 2 * (b % 2) + t, :],
                                            bc[:, b, :], ALU.add).then_inc(v_added, 1)
                take(GM_V + 2 * b + 2)
                take(GM_V + 2 * b + 3)
            for t in range(NT):
                for b in range(4):
                    dve.wait_ge(v_gelu, 2 * b + t + 1)
                    ins = nc.vector.bn_stats(bns[:, t * 4 + b, :], vg[:, t, b * HALF:(b + 1) * HALF])
            link(ins)
            for t in range(NT):
                ins = nc.vector.bn_aggr(bna[:, t, :], bns[:, 4 * t:4 * t + 4, :].rearrange("p a b -> p (a b)"))
            link(ins)
            rstd(R_LN, 1.0, bna[:, 0:2, 1])
            for t in range(NT):
                ins = nc.vector.tensor_scalar(vg[:, t, :], vg[:, t, :], bna[:, t, 0:1], rs_of(R_LN, t), ALU.subtract,
                                              ALU.mult)
            link(ins)
            for b in range(4):
                part = vg[:, :, b * HALF:(b + 1) * HALF]
                for j, op in ((4 + 2 * b, ALU.mult), (5 + 2 * b, ALU.add)):
                    dve.wait_ge(bc_loaded[j % 4], 16 * (j // 4 + 1))
                    nc.vector.tensor_tensor(part, part, bcast(bc[:, j % 4, :], 1, NT), op).then_inc(affine, 1)
                    dve.wait_ge(affine, j - 3)
            for q in range(4):
                dve.wait_ge(ws_turned, q + 1)
                nc.vector.tensor_tensor(wst[:, 4 * q:4 * q + 4, :], ps[:, q, :].rearrange("p (g t) -> p g t", g=4),
                                        bcast(tri, 1, 4), ALU.mult).then_inc(wst_ready, 1)
            for b in range(5):
                first = (60, 62, 66, 70, 74)[b]
                take(first)
                take(first + 1)
                if b < 4:
                    nb = 12 + b
                    dve.wait_ge(bc_loaded[nb % 4], 16 * (nb // 4 + 1))
                    dve.wait_ge(sp_done, b + 1)
                    if b >= 1:
                        dve.wait_ge(yh_ready, b)
                    for q in range(2):
                        bias = bcast(bc[:, nb % 4, :].rearrange("p (g t) -> p g t", g=4)[:, 2 * q:2 * q + 2, :], 2, NT)
                        ins = nc.vector.tensor_tensor(
                            yr[:, 2 * q:2 * q + 2, :].rearrange("p g (n t) -> p g n t", n=NT),
                            ps[:, 6 + q, :].rearrange("p (g n t) -> p g n t", g=2, n=NT), bias, ALU.add)
                    link(ins)
                    dve.wait_ge(ub_ready, 4 * b + 4)
                    nc.vector.tensor_tensor(yr[:, :, :], yr[:, :, :], ub[:, :, :], ALU.mult).then_inc(yr_ready, 1)
                    dve.wait_ge(yh_ready, b + 1)
                    nc.vector.tensor_tensor(yl[:, b % 2], yr[:, :, :], yh[:, b % 2].bitcast(F32), ALU.subtract)\
                        .then_inc(yl_ready, 1)
                if 1 <= b < 4:
                    take(first + 2)
                    take(first + 3)
            residual(None, 0, R_PM1, done=4)
            normalise(R_FF1, x, xn)
            low_of_turned(N_FF1)
            ffn(1)
            residual(None, 1, R_PF1, done=5)
            normalise(R_KV, x, xn)
            low_of_turned(N_KV)
            for u in range(KV + 2, KV + 9):
                take(u)
            take(QG)

            def head_rstd(src, sq, r, ready):
                for t in range(NT):
                    dve.wait_ge(evac, ready[t])
                    link(nc.vector.tensor_tensor(sq[:, :], src[:, t, :], src[:, t, :], ALU.mult))
                    c = R_AT[r] + t * FH
                    link(nc.vector.reduce_sum(ss[:, c:c + FH], sq[:, :].rearrange("p (h c) -> p h c", h=FH), AX.X))
                rstd(r, 1.0 / FD)

            head_rstd(k_st, ksq, R_KH, (20, 21))
            for t in range(NT):
                c = R_AT[R_KH] + t * FH
                ins = nc.vector.tensor_tensor(ka[:, t, :, 0:FD], k_st[:, t, :].rearrange("p (h c) -> p h c", h=FH),
                                              bcast(rs[:, c:c + FH], 2, FD), ALU.mult)
            link(ins)
            dve.wait_ge(w_used, split_no(KV + 8) + 1)
            z, az, e1, mn, ln, ls = (fz[:, j] for j in range(6))
            dve.wait_ge(in_small, 16 * 4)
            link(nc.vector.tensor_tensor(z, ps[:, 4, 0:32].rearrange("p (t h) -> p t h", t=NT), bcast(bf[:, :], 1, NT),
                                         ALU.add))
            nc.vector.tensor_scalar(mn, z, 0.0, None, ALU.min)
            nc.vector.scalar_tensor_tensor(az, z, -1.0, z, ALU.mult, ALU.max).then_inc(f_pre, 1)
            dve.wait_ge(f_act, 1)
            nc.vector.tensor_scalar(e1, e1, 1.0, None, ALU.add).then_inc(f_pre, 1)
            dve.wait_ge(f_act, 2)
            nc.vector.tensor_tensor(ls, mn, ln, ALU.subtract).then_inc(ls_ready, 1)
            dve.wait_ge(cum_done, 1)
            link(nc.vector.tensor_copy(dcum[:, :, :], ps[:, 5, 0:32].rearrange("p (t h) -> p t h", t=NT)))
            nc.vector.memset(ka[:, :, :, FD:FD + 1], 1.0)
            nc.vector.tensor_scalar(ka[:, :, :, FD + 1], dcum[:, :, :], -1.0, None, ALU.mult).then_inc(ka_ready, 1)
            take(QG + 1)
            low_of_turned(N_MIX2)
            for u in range(QG + 2, QG + 8):
                take(u)
            for q in range(0, 8, 2):
                dve.wait_ge(f_turned, q + 2)
                nc.vector.tensor_copy(kt_f[:, 2 * q + 2:2 * q + 4, :],
                                      ps[0:FA, 4 + (q + 1) % 4, :].rearrange("p (h t) -> p h t", h=2))\
                    .then_inc(ft_evac, 1)
            take(WO)
            take(WO + 1)
            link(nc.vector.tensor_tensor(gq[:, 0, :], gq[:, 0, :], gq[:, 1, :], ALU.mult))
            link(nc.vector.tensor_scalar(gq[:, 0, :], gq[:, 0, :], FD ** -0.5, None, ALU.mult))
            head_rstd(q_st, qsq, R_QH, (28, 29))
            for t in range(NT):
                c = R_AT[R_QH] + t * FH
                to = qa[:, t, :, 0:FD]
                link(nc.vector.tensor_tensor(to, q_st[:, t, :].rearrange("p (h c) -> p h c", h=FH),
                                             bcast(rs[:, c:c + FH], 2, FD), ALU.mult))
                nc.vector.tensor_tensor(to, to, bcast(gq[:, 0, :], 1, FH), ALU.mult)
            nc.vector.memset(qa[:, :, :, FD + 1:FD + 2], 1.0)
            nc.vector.tensor_copy(qa[:, :, :, FD], dcum[:, :, :]).then_inc(qa_ready, 1)
            for q in range(0, 8, 2):
                dve.wait_ge(f_turned, 8 + q + 2)
                nc.vector.tensor_copy(qt_f[:, 2 * q + 2:2 * q + 4, :],
                                      ps[0:FA, 4 + (q + 1) % 4, :].rearrange("p (h t) -> p h t", h=2))\
                    .then_inc(ft_evac, 1)

            extract(9, *EX_BANKS[9])

            def fox_max(h):
                dve.wait_ge(fs_done, h + 1)
                nc.vector.tensor_reduce(nmax[:, 2 * h:2 * h + 1], ps[:, 4 + h % 2, 0:P], AX.X, ALU.max, negate=True)
                nc.vector.tensor_reduce(nmax[:, 2 * h + 1:2 * h + 2], ps[:, 4 + h % 2, P:3 * P], AX.X, ALU.max,
                                        negate=True).then_inc(fm_ready, 1)

            fox_max(0)
            for h in range(FH):
                if h + 1 < FH:
                    fox_max(h + 1)
                dve.wait_ge(fp_turned, h + 1)
                if h >= 2:
                    dve.wait_ge(fpv_done, h - 1)
                nc.vector.tensor_copy(prob_ft[:, h % 2, :], ps[:, 6 + h % 2, 0:384]).then_inc(fpt_ready, 1)
            dve.wait_ge(fp_ready, 2 * FH)
            link(nc.vector.reciprocal(prec[:, :], psumr[:, :]))
            dve.wait_ge(fpv_done, FH)
            dve.wait_ge(evac, 33)
            for t in range(NT):
                for half in range(2):
                    sums = prec[:, 16 * half + t:16 * half + 16:2]
                    to = o_f[:, t, half * HALF:(half + 1) * HALF]
                    ins = nc.vector.tensor_tensor(to.rearrange("p (h c) -> p h c", h=8),
                                                  ps[:, 2 * t + half, :].rearrange("p (h c) -> p h c", h=8),
                                                  bcast(sums, 2, FD), ALU.mult)
                link(ins)
                nc.vector.tensor_tensor(o_f[:, t, :], o_f[:, t, :], sg[:, t, :], ALU.mult).then_inc(xn_ready, 1)
            low_of_turned(N_FOX)
            for u in range(WO + 2, WO + 6):
                take(u)
            residual(None, 0, R_PM2, done=6)
            normalise(R_FF2, x, xn)
            low_of_turned(N_FF2)
            ffn(2)
            residual(None, 1, R_PF2, done=7)

        @block.scalar
        def _(act):
            def hi_part(u, i=None):
                if u >= N_UNITS or u in DIRECT:
                    return
                s, n = split_no(u), width(u)
                more = 0 if i is None else 4 * i
                act.wait_ge(raw_loaded[u % RAW], 32 * (u // RAW + 1) + 8 * more)
                if s >= 2:
                    act.wait_ge(w_used, s - 1 + more)
                nc.scalar.activation(wh[:, s % 2, 0:n], raw[:, u % RAW, 0:n], ACT.Copy).then_inc(hi_done, 1)

            def squares(r, pieces):
                for j, src in enumerate(pieces):
                    c = R_AT[r] + j
                    if SQ_BASE[r] + j >= 1:
                        act.wait_ge(sq_done, SQ_BASE[r] + j)
                    n = src.shape[1]
                    nc.scalar.activation(sqj[:, 0:n], src, ACT.Square, accum_out=ss[:, c:c + 1]).then_inc(sq_done, 1)

            def root(r):
                c0, c1 = R_AT[r], R_AT[r + 1]
                act.wait_ge(ms_ready, r + 1)
                nc.scalar.activation(rt[:, c0:c1], ms[:, c0:c1], ACT.Sqrt).then_inc(rt_ready, 1)

            def turn_evac(n, b0, hi=None):
                hi = hi or hh
                for b in range(4):
                    j = 4 * n + b
                    act.wait_ge(turned, j + 1)
                    if j >= 2:
                        act.wait_ge(t_lo, j - 1)
                    for kk in range(2):
                        k = 2 * b + kk
                        nc.scalar.activation(hraw[:, b % 2, kk * TOK:(kk + 1) * TOK],
                                             ps[:, b0 + b, kk * TOK:(kk + 1) * TOK], ACT.Identity,
                                             scale=mod[:, n, 0, k:k + 1], bias=mod[:, n, 1, k:k + 1])\
                            .then_inc(t_raw, 1)
                    act.wait_ge(t_raw, 2 * j + 2)
                    nc.scalar.activation(hi[:, 2 * b:2 * b + 2, :],
                                         hraw[:, b % 2, :].rearrange("p (k t) -> p k t", k=2), ACT.Copy)\
                        .then_inc(t_hi, 1)

            sqj = junk

            act.wait_ge(cols_ready, 1)
            at = COL[("c", 0)]
            nc.scalar.activation(cs[:, :], col[:, at:at + 24], ACT.Silu).then_inc(cs_ready, 1)
            act.wait_ge(in_small, 16 * 4)
            nc.scalar.activation(lg[:, 1, :], lg[:, 3, :], ACT.Exp).then_inc(lg_exp, 1)
            act.wait_ge(in_x, 16)
            squares(R_X, [x[:, t, :] for t in range(NT)])
            act.wait_ge(in_ctx, 16)
            squares(R_CTX, [cx[:, t, :] for t in range(NT)])
            root(R_X)
            root(R_CTX)
            hi_part(0)
            hi_part(1)
            act.wait_ge(mod1_ready, 1)
            turn_evac(N_X, 4)
            turn_evac(N_CTX, 0, ch)

            def take_evac(out_, src, fn=ACT.Copy):
                nc.scalar.activation(out_, src, fn).then_inc(evac, 1)

            hi_part(2)
            hi_part(3)
            act.wait_ge(w_used, 2)
            for t in range(4):
                if t < NT:
                    take_evac(cqkv[:, t:t + 3:2, :], ps[:, t, :].rearrange("p (a c) -> p a c", a=2))
                else:
                    take_evac(cqkv[:, 2 + t, :], ps[:, t, 0:256])
            hi_part(4)
            hi_part(5)
            act.wait_ge(w_used, 4)
            for t in range(4):
                take_evac(rk[:, t, :], ps[:, 4 + t, :])
            hi_part(6)
            hi_part(7)
            act.wait_ge(w_used, 6)
            for t in range(4):
                take_evac(rv[:, t, :], ps[:, t, :])
            hi_part(8)
            hi_part(9)
            act.wait_ge(w_used, 8)
            for t in range(NT):
                take_evac(rq[:, t, :], ps[:, 4 + t, :])
            hi_part(10)
            act.wait_ge(w_used, 10)
            for t in range(NT):
                take_evac(rg[:, t, :], ps[:, 6 + t, :], ACT.Silu)
            act.wait_ge(w_used, 11)
            take_evac(kpe[:, :, :], ps[:, 0, 0:4 * ROPE].rearrange("p (t c) -> p t c", t=4))
            hi_part(13)
            hi_part(14)
            act.wait_ge(evac, 17)
            squares(R_C, [cqkv[:, j, :] for j in range(6)])
            root(R_C)
            for kc in range(2):
                act.wait_ge(c_turned, 1)
                nc.scalar.activation(cqt[:, kc, :], ps[:, 1, kc * TOK:(kc + 1) * TOK], ACT.Copy,
                                     scale=column("g_q", 0, kc)).then_inc(ct_ready, 1)
            for kc in range(2):
                act.wait_ge(c_turned, 2 + kc)
                nc.scalar.activation(ckt[:, kc, :], ps[:, 2 + kc, :], ACT.Copy,
                                     scale=column("g_kv", 0, kc)).then_inc(ct_ready, 1)
            for t in range(NT):
                for part, (h0, h1) in enumerate(((0, 5), (5, 8))):
                    act.wait_ge(q_proj, 2 * t + part + 1)
                    nc.scalar.activation(qk_st[:, t, h0:h1, :],
                                         ps[:, 4 + 2 * t + part, 0:(h1 - h0) * QK].rearrange("p (h c) -> p h c",
                                                                                              h=h1 - h0),
                                         ACT.Copy).then_inc(q_evac, 1)
            for q in range(4):
                act.wait_ge(q_turned, 2)
                nc.scalar.activation(qt_m[:, 2 * q:2 * q + 2, :],
                                     ps[0:QK, q, :].rearrange("p (h t) -> p h t", h=2), ACT.Copy,
                                     scale=MLA_SCALE).then_inc(qt_ready, 1)

            def turn_keys(t):
                for half in range(2):
                    act.wait_ge(k_turned, 2 * t + half + 1)
                    nc.scalar.activation(kt_m[:, 4 * half:4 * half + 4, t * P:(t + 1) * P],
                                         ps[0:QK, 2 * (t % 2) + half, :].rearrange("p (h c) -> p h c", h=4),
                                         ACT.Copy).then_inc(kt_ready, 1)

            for t in range(4):
                for half in range(2):
                    act.wait_ge(kv_proj, 2 * t + half + 1)
                    if half == 0:
                        act.wait_ge(q_turned, 2)
                        if t >= 2:
                            act.wait_ge(k_turned, 2 * (t - 2) + 2)
                    src = ps[:, 4 + 2 * (t % 2) + half, :].rearrange("p (h c) -> p h c", h=4)
                    nc.scalar.activation(qk_st[:, t % 2, 4 * half:4 * half + 4, 0:NOPE], src[:, :, 0:NOPE],
                                         ACT.Copy).then_inc(k_evac, 1)
                if t >= 1:
                    turn_keys(t - 1)
            turn_keys(3)
            for it in range(2 * MLA_H):
                act.wait_ge(max_ready, it + 1)
                if it >= 2:
                    act.wait_ge(p_turned, it - 1)
                nc.scalar.activation(prob[:, it % 2, :], ps[:, 4 + it % 2, :], ACT.Exp, bias=nmax[:, it:it + 1],
                                     accum_out=psumr[:, it:it + 1]).then_inc(p_ready, 1)
            for q in range(6):
                act.wait_ge(r_turned, q + 1)
                if q < 2:
                    dst = rqt[:, 2 * q:2 * q + 2, :]
                    src = ps[:, 4 + q, :].rearrange("p (h t) -> p h t", h=2)
                    nc.scalar.activation(dst, src, ACT.Copy).then_inc(rt_evac, 1)
                else:
                    bank = (6, 7, 2, 3)[q - 2]
                    nc.scalar.activation(rkt[:, q - 2, :], ps[:, bank, :], ACT.Copy, scale=RDK ** -0.5)\
                        .then_inc(rt_evac, 1)
            for h in range(RH):
                act.wait_ge(arg_ready, h + 1)
                if h >= 1:
                    act.wait_ge(mask_ready, h)
                nc.scalar.activation(mask[:, h, 0:2, :], mask[:, h, 0:2, :], ACT.Exp)
                nc.scalar.activation(mask[:, h, 2:4, :], diff[:, :, :], ACT.Exp, scale=lg[:, 0, h:h + 1],
                                     bias=lg[:, 2, h:h + 1])
                nc.scalar.activation(mt[:, :, :], diff[:, :, :], ACT.Exp, scale=lg[:, 1, 4 + h:5 + h],
                                     bias=lg[:, 2, 4 + h:5 + h]).then_inc(mask_exp, 1)
            root(R_RET)
            turn_evac(N_RET, 4)
            hi_part(15)
            hi_part(16)
            hi_part(17)
            hi_part(18)
            act.wait_ge(x_ready, 1)
            squares(R_FF0, [x[:, t, :] for t in range(NT)])
            root(R_FF0)
            turn_evac(N_FF0, 4)

            def ffn(f):
                u0, base = UP[f], 2

                def at_(name, first, k, i):
                    c = COL[(name, first)] + k
                    return col[:, bass.ds(c + 4 * i, 1)] if i is not None else col[:, c:c + 1]

                def up_wait(pp, i):
                    if pp % 2 == 0:
                        act.wait_ge(up_done, NBLK * f + pp // 2 + 1 + (0 if i is None else 2 * i))
                    else:
                        act.wait_ge(w_used, split_no(u0 + pp) + 1 + (0 if i is None else 4 * i))

                def first_step(pp, i=None):
                    more = 0 if i is None else 4 * i
                    c, bank = pp % 2, 4 + pp % 4
                    if f == 0:
                        up_wait(pp, i)
                        act.wait_ge(hid_pool, pp - 1 + CREDIT + more)
                        for half in range(2):
                            nc.scalar.activation(hu[:, c, half, :], ps[:, bank, half * TOK:(half + 1) * TOK],
                                                 ACT.Identity, scale=at_("conv_w", 0, 44 + half * NFF + pp, i),
                                                 bias=at_("conv_b", 0, half * NFF + pp, i)).then_inc(conv_base, 1)
                    else:
                        up_wait(pp, i)
                        act.wait_ge(hid_dve, NFF * (f - 1) + pp - 1 + CREDIT + more)
                        nc.scalar.activation(sl[:, c, :], ps[:, bank, 0:TOK], ACT.Silu).then_inc(silu_done, 1)

                def silu_step(pp, i=None):
                    more = 0 if i is None else 4 * i
                    if f == 0:
                        act.wait_ge(conv_mid, 4 * pp + 4 + 4 * more)
                        nc.scalar.activation(sl[:, pp % 2, :], hu[:, pp % 2, 1, :], ACT.Silu).then_inc(silu_done, 1)

                def high_step(pp, i=None):
                    more = 0 if i is None else 4 * i
                    if f == 0:
                        act.wait_ge(hid_pool, pp + 1 + CREDIT + more)
                    else:
                        act.wait_ge(hid_dve, NFF * (f - 1) + pp + 1 + CREDIT + more)
                    dst = gh[:, bass.ds(pp + more, 1), :] if i is not None else gh[:, pp:pp + 1, :]
                    nc.scalar.activation(dst, hid[:, pp % 2:pp % 2 + 1, :], ACT.Copy).then_inc(gh_done, 1)

                with act.Fori(0, 4) as i:
                    for b in range(2):
                        hi_part(u0 + base + 2 * b, i)
                        first_step(2 * b, i)
                        hi_part(u0 + base + 2 * b + 1, i)
                        first_step(2 * b + 1, i)
                        silu_step(2 * b, i)
                        high_step(2 * b, i)
                        silu_step(2 * b + 1, i)
                        high_step(2 * b + 1, i)
                for pp in range(16, NFF, 2):
                    hi_part(u0 + base + pp)
                    first_step(pp)
                    hi_part(u0 + base + pp + 1)
                    first_step(pp + 1)
                    silu_step(pp)
                    high_step(pp)
                    silu_step(pp + 1)
                    high_step(pp + 1)
                for j in range(NBLK):
                    hi_part(DOWN[f] + j + base)

            ffn(0)
            act.wait_ge(x_ready, 2)
            squares(R_FIN, [x[:, t, :] for t in range(NT)])
            root(R_FIN)
            act.wait_ge(x_ready, 3)
            squares(R_MIX1, [x[:, t, :] for t in range(NT)])
            root(R_MIX1)
            turn_evac(N_MIX1, 4)
            for b in range(4):
                hi_part(GM_V + 2 * b + 2)
                hi_part(GM_V + 2 * b + 3)
                for t in range(NT):
                    act.wait_ge(v_added, 2 * b + t + 1)
                    part = vg[:, t, b * HALF:(b + 1) * HALF]
                    nc.scalar.activation(part, part, ACT.Gelu_apprx_tanh).then_inc(v_gelu, 1)
            root(R_LN)
            for b in range(5):
                first = (60, 62, 66, 70, 74)[b]
                hi_part(first)
                hi_part(first + 1)
                if b < 4:
                    for c in range(4):
                        act.wait_ge(w_used, split_no((59, 61, 65, 69)[b]) + 1)
                        if b >= 1:
                            act.wait_ge(yr_ready, b)
                        nc.scalar.activation(ub[:, c, :], ps[:, 4 + c // 2, (c % 2) * TOK:(c % 2 + 1) * TOK],
                                             ACT.Gelu_apprx_tanh, bias=column("a_b_in_2", 0, 4 * b + c))\
                            .then_inc(ub_ready, 1)
                    act.wait_ge(yr_ready, b + 1)
                    if b >= 2:
                        act.wait_ge(w_used, split_no((63, 67)[b - 2]) + 1)
                    nc.scalar.activation(yh[:, b % 2], yr[:, :, :], ACT.Copy).then_inc(yh_ready, 1)
                if 1 <= b < 4:
                    hi_part(first + 2)
                    hi_part(first + 3)

            def post_squares(r, last_unit):
                act.wait_ge(w_used, split_no(last_unit) + 1)
                squares(r, [ps[:, q, :] for q in range(4)])
                root(r)

            post_squares(R_PM1, 73)
            act.wait_ge(x_ready, 4)
            squares(R_FF1, [x[:, t, :] for t in range(NT)])
            root(R_FF1)
            turn_evac(N_FF1, 4)
            ffn(1)
            post_squares(R_PF1, DOWN[1] + 10)
            act.wait_ge(x_ready, 5)
            squares(R_KV, [x[:, t, :] for t in range(NT)])
            root(R_KV)
            turn_evac(N_KV, 4)
            for b in range(4):
                hi_part(KV + 2 * b + 2)
                hi_part(KV + 2 * b + 3)
                act.wait_ge(w_used, split_no(KV + 2 * b + 1) + 1)
                for t in range(NT):
                    dst = k_st if b < 2 else v_f
                    take_evac(dst[:, t, (b % 2) * HALF:(b % 2 + 1) * HALF], ps[:, 2 * (b % 2) + t, :])
            root(R_KH)
            z, az, e1, mn, ln, ls = (fz[:, j] for j in range(6))
            act.wait_ge(f_pre, 1)
            nc.scalar.activation(e1, az, ACT.Exp, scale=-1.0).then_inc(f_act, 1)
            act.wait_ge(f_pre, 2)
            nc.scalar.activation(ln, e1, ACT.Ln).then_inc(f_act, 1)
            hi_part(QG + 1)
            act.wait_ge(w_used, split_no(KV + 8) + 1)
            turn_evac(N_MIX2, 4)
            for b in range(4):
                if b < 3:
                    hi_part(QG + 2 * b + 2)
                    hi_part(QG + 2 * b + 3)
                act.wait_ge(w_used, split_no(QG + 2 * b + 1) + 1)
                for t in range(NT):
                    dst = q_st if b < 2 else sg
                    take_evac(dst[:, t, (b % 2) * HALF:(b % 2 + 1) * HALF], ps[:, 2 * (b % 2) + t, :],
                              ACT.Copy if b < 2 else ACT.Sigmoid)
            for q in range(0, 8, 2):
                act.wait_ge(f_turned, q + 1)
                nc.scalar.activation(kt_f[:, 2 * q:2 * q + 2, :],
                                     ps[0:FA, 4 + q % 4, :].rearrange("p (h t) -> p h t", h=2), ACT.Copy)\
                    .then_inc(act_step, 1)
            hi_part(WO)
            hi_part(WO + 1)
            root(R_QH)
            for q in range(0, 8, 2):
                act.wait_ge(f_turned, 8 + q + 1)
                nc.scalar.activation(qt_f[:, 2 * q:2 * q + 2, :],
                                     ps[0:FA, 4 + q % 4, :].rearrange("p (h t) -> p h t", h=2), ACT.Copy)\
                    .then_inc(act_step, 1)
            for h in range(FH):
                act.wait_ge(fm_ready, h + 1)
                if h >= 2:
                    act.wait_ge(fp_turned, h - 1)
                for t in range(NT):
                    lo_, hi_ = (0, P) if t == 0 else (P, 3 * P)
                    nc.scalar.activation(prob_f[:, h % 2, lo_:hi_], ps[:, 4 + h % 2, lo_:hi_], ACT.Exp,
                                         bias=nmax[:, 2 * h + t:2 * h + t + 1],
                                         accum_out=psumr[:, 2 * h + t:2 * h + t + 1]).then_inc(fp_ready, 1)
            turn_evac(N_FOX, 4)
            for u in range(WO + 2, WO + 6):
                hi_part(u)
            post_squares(R_PM2, WO + 3)
            act.wait_ge(x_ready, 6)
            squares(R_FF2, [x[:, t, :] for t in range(NT)])
            root(R_FF2)
            turn_evac(N_FF2, 4)
            ffn(2)
            post_squares(R_PF2, DOWN[2] + 10)

        @block.tensor
        def _(pe):
            def three(to, lh, ll, rh, rl, start, stop):
                nc.tensor.matmul(to, lh, rh, start=start, stop=False, skip_group_check=True)
                nc.tensor.matmul(to, lh, rl, start=False, stop=False, skip_group_check=True)
                return nc.tensor.matmul(to, ll, rh, start=False, stop=stop, skip_group_check=True)

            def unit(u, cols, i=None):
                s = split_no(u)
                pe.wait_ge(lo_done, s + 1 + (0 if i is None else 4 * i))
                n = width(u)
                return (wh[:, s % 2, 0:n].rearrange("p (k c) -> p k c", c=cols),
                        wl[:, s % 2, 0:n].rearrange("p (k c) -> p k c", c=cols))

            def turn(n, src, b0):
                pe.wait_ge(xn_ready, XN_NEED[n])
                for b in range(4):
                    for q in range(4):
                        k, t = 2 * b + q // 2, q % 2
                        ins = nc.tensor.transpose(ps[:, b0 + b, q * P:(q + 1) * P], src[:, t, k * P:(k + 1) * P],
                                                  ident)
                    ins.then_inc(turned, 1)

            def rows_product(u, hparts, tiles, banks, cols, k0, nk, first, last, c0=0):
                w_hi, w_lo = unit(u, cols)
                for kk in range(nk):
                    k = k0 + kk
                    for j, (hi, lo, t) in enumerate(tiles):
                        a0 = c0[j] if isinstance(c0, (list, tuple)) else 0
                        ins = three(banks[j], hi[:, k, t * P:(t + 1) * P], lo[:, k, t * P:(t + 1) * P],
                                    w_hi[:, kk, a0:], w_lo[:, kk, a0:], first and kk == 0, last and kk == nk - 1)
                ins.then_inc(w_used, 1)

            def acc_product(u, hi, lo, k0, first, last):
                w_hi, w_lo = unit(u, D)
                for kk in range(2):
                    for t in range(NT):
                        for cb in range(2):
                            cc = slice(cb * HALF, (cb + 1) * HALF)
                            tt = slice(t * P, (t + 1) * P)
                            ins = three(ps[:, 2 * t + cb, :], hi[:, k0 + kk, tt], lo[:, k0 + kk, tt],
                                        w_hi[:, kk, cc], w_lo[:, kk, cc], first and kk == 0, last and kk == 1)
                ins.then_inc(w_used, 1)

            def extract(g):
                ba, bb = EX_BANKS[g]
                kind, _ = GROUPS[g]
                e = EX_BASE[g]
                pe.wait_ge(acc_step, 8 * g)
                pe.wait_ge(brow_loaded, 16 * (g + 1))
                c0, c1 = {"shift_scale": (0, 16), "gate_shift": (8, 16), "scale_gate": (0, 8)}[kind]
                for j, c in enumerate(range(c0, c1)):
                    nc.tensor.matmul(ps[:, ba, j:j + 1], acc[:, c * P:(c + 1) * P], ones[:, 0:1], start=True,
                                     stop=False)
                    ins = nc.tensor.matmul(ps[:, ba, j:j + 1], brow[0:4, (c % 4) * P:(c % 4 + 1) * P],
                                           ident[0:4, c // 4:c // 4 + 1], start=False, stop=True)
                ins.then_inc(ex_done, 1)
                if kind == "shift_scale":
                    return
                q0 = 0 if kind == "gate_shift" else 2
                for h, bank in ((0, bb), (1, ba)):
                    if h == 1:
                        pe.wait_ge(ex_taken, e + 1)
                    q = q0 + h
                    nc.tensor.matmul(ps[:, bank, :], ones, acc[:, q * HALF:(q + 1) * HALF], start=True, stop=False)
                    nc.tensor.matmul(ps[:, bank, :], pick[0:4, q, :], brow[0:4, :], start=False, stop=True)\
                        .then_inc(ex_done, 1)

            pe.wait_ge(in_const, 16)
            pe.wait_ge(in_rows, 16 * sum(len(r) for r in VEC_TILES))
            for t, n in enumerate(VEC_ROWS):
                nc.tensor.transpose(ps[:, 7, t * P:t * P + n], vrow[0:n, t, :], ident[0:n, 0:n]).then_inc(cols_turned, 1)
            pe.wait_ge(cs_ready, 1)
            pe.wait_ge(brow_loaded, 16)
            for k in range(KD):
                pe.wait_ge(au_loaded[k % 2], 16 * (k // 2 + 1))
                for q in range(4):
                    if k == 0:
                        nc.tensor.matmul(ps[0:2, q, :], pick[0:4, q, 0:2], brow[0:4, :], start=True, stop=False)
                    ins = nc.tensor.matmul(ps[0:2, q, :], cs[:, k:k + 9:8], au[:, k % 2, q * HALF:(q + 1) * HALF],
                                           start=False, stop=(k == KD - 1))
                ins.then_inc(mod1_used, 1)
            pe.wait_ge(m1_ready, 1)
            for c in range(16):
                ins = nc.tensor.transpose(ps[:, 6, 2 * c:2 * c + 2], m1[0:2, c * P:(c + 1) * P], ident[0:2, 0:2])
            ins.then_inc(m1_turned, 1)
            pe.wait_ge(mod1_ready, 1)
            turn(N_X, xn, 4)
            turn(N_CTX, xn_c, 0)
            lat = [(hh, hl, t) for t in range(NT)]
            con_ = [(ch, cl, t) for t in range(NT)]
            pe.wait_ge(t_lo, 8)
            for h in range(2):
                rows_product(0 + h, None, lat + con_, [ps[:, 0, :], ps[:, 1, :], ps[:, 2, 0:256], ps[:, 3, 0:256]],
                             512, 4 * h, 4, h == 0, h == 1, c0=[0, 0, 256, 256])
            for h in range(2):
                rows_product(2 + h, None, lat + con_, [ps[:, 4 + t, :] for t in range(4)], 512, 4 * h, 4, h == 0,
                             h == 1)
            pe.wait_ge(evac, 4)
            for h in range(2):
                rows_product(4 + h, None, lat + con_, [ps[:, t, :] for t in range(4)], 512, 4 * h, 4, h == 0, h == 1)
            pe.wait_ge(evac, 8)
            extract(1)
            for h in range(2):
                rows_product(6 + h, None, lat, [ps[:, 4 + t, :] for t in range(2)], 512, 4 * h, 4, h == 0, h == 1)
            pe.wait_ge(ex_taken, 3)
            for h in range(2):
                rows_product(8 + h, None, lat, [ps[:, 6 + t, :] for t in range(2)], 512, 4 * h, 4, h == 0, h == 1)
            pe.wait_ge(evac, 12)
            w_hi, w_lo = unit(10, ROPE)
            for j, (hi, lo, t) in enumerate(lat + con_):
                for k in range(KD):
                    ins = three(ps[:, 0, j * ROPE:(j + 1) * ROPE], hi[:, k, t * P:(t + 1) * P],
                                lo[:, k, t * P:(t + 1) * P], w_hi[:, k, :], w_lo[:, k, :], k == 0, k == KD - 1)
            ins.then_inc(w_used, 1)
            pe.wait_ge(cn_ready, 6)
            for bank, tiles in ((1, (0, 1)), (2, (2, 3, 4, 5)), (3, (2, 3, 4, 5))):
                for q in range(4):
                    if bank == 1:
                        j, kc = tiles[q % 2], q // 2
                    else:
                        j, kc = tiles[q], bank - 2
                    ins = nc.tensor.transpose(ps[:, bank, q * P:(q + 1) * P], cn[:, j, kc * P:(kc + 1) * P], ident)
                ins.then_inc(c_turned, 1)
            pe.wait_ge(evac, 16)
            uq = raw[:, W_UQ % RAW, 0:2 * MLA_H * QK].rearrange("p (k c) -> p k c", k=2)
            pe.wait_ge(raw_loaded[W_UQ % RAW], 32 * (W_UQ // RAW + 1))
            pe.wait_ge(ct_ready, 2)
            for t in range(NT):
                for part, (c0, c1) in enumerate(((0, 5 * QK), (5 * QK, 8 * QK))):
                    for kc in range(2):
                        ins = nc.tensor.matmul(ps[:, 4 + 2 * t + part, 0:c1 - c0], cqt[:, kc, t * P:(t + 1) * P],
                                               uq[:, kc, c0:c1], start=(kc == 0), stop=(kc == 1))
                    ins.then_inc(q_proj, 1)
            for t in range(NT):
                pe.wait_ge(q_roped, t + 1)
                if t == 0:
                    pe.wait_ge(ct_ready, 4)
                    pe.wait_ge(evac, 17)
                for h in range(MLA_H):
                    at = (h % 2) * TOK + t * P
                    ins = nc.tensor.transpose(ps[0:QK, h // 2, at:at + P], qk_st[:, t, h, :], ident)
                ins.then_inc(q_turned, 1)
            ukv = raw[:, W_UKV % RAW, :].rearrange("p (k c) -> p k c", k=2)
            pe.wait_ge(raw_loaded[W_UKV % RAW], 32 * (W_UKV // RAW + 1))

            def turn_keys(t):
                pe.wait_ge(k_full, t + 1)
                pe.wait_ge(k_evac, 2 * t + 2)
                if t < 2:
                    pe.wait_ge(qt_ready, 4)
                else:
                    pe.wait_ge(kt_ready, 2 * (t - 2) + 2)
                for h in range(MLA_H):
                    ins = nc.tensor.transpose(ps[0:QK, 2 * (t % 2) + h // 4, (h % 4) * P:(h % 4 + 1) * P],
                                              qk_st[:, t % 2, h, :], ident)
                    if h % 4 == 3:
                        ins.then_inc(k_turned, 1)

            for t in range(4):
                for half in range(2):
                    if t >= 2:
                        pe.wait_ge(v_evac, 2 * (t - 2) + half + 1)
                    else:
                        pe.wait_ge(q_evac, 2 * t + half + 1)
                    for kc in range(2):
                        ins = nc.tensor.matmul(ps[:, 4 + 2 * (t % 2) + half, :], ckt[:, kc, t * P:(t + 1) * P],
                                               ukv[:, kc, half * HALF:(half + 1) * HALF], start=(kc == 0),
                                               stop=(kc == 1))
                    ins.then_inc(kv_proj, 1)
                if t >= 1:
                    turn_keys(t - 1)
            turn_keys(3)
            pe.wait_ge(v_evac, 8)
            pe.wait_ge(kt_ready, 8)

            def scores(it):
                h, t = it // 2, it % 2
                if it >= 2:
                    pe.wait_ge(p_ready, it - 1)
                nc.tensor.matmul(ps[:, 4 + it % 2, :], qt_m[:, h, t * P:(t + 1) * P], kt_m[:, h, :], start=True,
                                 stop=True).then_inc(score, 1)

            def turn_probs(it):
                pe.wait_ge(p_ready, it + 1)
                if it >= 2:
                    pe.wait_ge(pt_ready, it - 1)
                for q in range(4):
                    ins = nc.tensor.transpose(ps[:, 6 + it % 2, q * P:(q + 1) * P],
                                              prob[:, it % 2, q * P:(q + 1) * P], ident)
                ins.then_inc(p_turned, 1)

            def values(it):
                h, t = it // 2, it % 2
                pe.wait_ge(pt_ready, it + 1)
                for q in range(4):
                    ins = nc.tensor.matmul(ps[:, t, h * MLA_V:(h + 1) * MLA_V], prob_t[:, it % 2, q * P:(q + 1) * P],
                                           v_m[:, q, h, :], start=(q == 0), stop=(q == 3))
                ins.then_inc(pv_done, 1)

            scores(0)
            for it in range(2 * MLA_H):
                if it + 1 < 2 * MLA_H:
                    scores(it + 1)
                turn_probs(it)
                if it >= 1:
                    values(it - 1)
            values(2 * MLA_H - 1)
            pe.wait_ge(ret_roped, 4)
            pe.wait_ge(p_ready, 2 * MLA_H)
            for q in range(2):
                for j in range(4):
                    h, t = 2 * q + j // 2, j % 2
                    ins = nc.tensor.transpose(ps[:, 4 + q, j * P:(j + 1) * P], rq[:, t, h * RDK:(h + 1) * RDK], ident)
                ins.then_inc(r_turned, 1)
            pe.wait_ge(pt_ready, 2 * MLA_H)
            for h, bank in enumerate((6, 7, 2, 3)):
                for t in range(4):
                    ins = nc.tensor.transpose(ps[:, bank, t * P:(t + 1) * P], rk[:, t, h * RDK:(h + 1) * RDK], ident)
                ins.then_inc(r_turned, 1)
            pe.wait_ge(rt_evac, 6)

            def decayed(h):
                for half in range(2):
                    if h >= 2:
                        pe.wait_ge(pr_ready, 2 * (h - 2) + half + 1)
                    for j in range(2):
                        kt = 2 * half + j
                        ins = nc.tensor.matmul(ps[:, 4 + 2 * (h % 2) + half, j * TOK:(j + 1) * TOK],
                                               rkt[:, h, kt * P:(kt + 1) * P], rqt[:, h, :], start=True, stop=True)
                    ins.then_inc(att_done, 1)

            def retained(h):
                pe.wait_ge(pr_ready, 2 * h + 2)
                for t in range(NT):
                    for kt in range(4):
                        ins = nc.tensor.matmul(ps[:, t, h * RDK:(h + 1) * RDK], pr[:, h % 2, kt, t * P:(t + 1) * P],
                                               rv[:, kt, h * RDK:(h + 1) * RDK], start=(kt == 0), stop=(kt == 3))
                ins.then_inc(y_done, 1)

            decayed(0)
            for h in range(RH):
                if h + 1 < RH:
                    decayed(h + 1)
                retained(h)
            extract(2)
            turn(N_RET, o, 4)
            pe.wait_ge(t_lo, 4 * (N_RET + 1))
            pe.wait_ge(ex_taken, EX_BASE[3])
            for j in range(4):
                acc_product(W_OUT + j, hh, hl, 2 * j, j == 0, j == 3)

            def up_unit(f, u, b_in, h, i=None):
                more = 0 if i is None else 4 * i
                w_hi, w_lo = unit(u, 512, i)
                for c in range(2):
                    pp = 2 * b_in + c
                    if h == 0:
                        if f == 0:
                            pe.wait_ge(hid_pool, pp - 3 + CREDIT + more)
                        else:
                            pe.wait_ge(hid_dve, NFF * (f - 1) + pp - 3 + CREDIT + more)
                    for s in range(2):
                        to = ps[:, 4 + pp % 4, s * TOK:(s + 1) * TOK]
                        for kk in range(4):
                            k = 4 * h + kk
                            cc = slice(s * 256 + c * P, s * 256 + (c + 1) * P)
                            wh_, wl_ = w_hi[:, kk, cc], w_lo[:, kk, cc]
                            ins = three(to, wh_, wl_, hh[:, k, :], hl[:, k, :], h == 0 and s == 0 and kk == 0,
                                        h == 1 and kk == 3)
                    if h == 1 and c == 0:
                        ins.then_inc(up_done, 1)
                    elif h == 1:
                        ins.then_inc(w_used, 1)
                if h == 0:
                    ins.then_inc(w_used, 1)

            def ffn(f):
                u0 = UP[f]
                pe.wait_ge(t_lo, 4 * ((N_FF0, N_FF1, N_FF2)[f] + 1))
                with pe.Fori(0, 4) as i:
                    for b in range(2):
                        for h in range(2):
                            up_unit(f, u0 + 2 * b + h, b, h, i)
                for b in range(8, NBLK):
                    for h in range(2):
                        up_unit(f, u0 + 2 * b + h, b, h)
                for j in range(NBLK):
                    pe.wait_ge(gl_done, NFF * f + 2 * j + 2 + CREDIT)
                    acc_product(DOWN[f] + j, gh, gl, 2 * j, j == 0, j == NBLK - 1)
                    if f == 1 and j == 0:
                        pe.wait_ge(hid_dve, NFF + CREDIT)
                        extract(6)

            turn(N_FF0, xn, 4)
            ffn(0)
            extract(3)
            turn(N_MIX1, xn, 4)
            pe.wait_ge(t_lo, 4 * (N_MIX1 + 1))
            for b in range(4):
                if b >= 2:
                    pe.wait_ge(v_added, 2 * (b - 2) + 2)
                for h in range(2):
                    rows_product(GM_V + 2 * b + h, None, lat, [ps[:, 4 + 2 * (b % 2) + t, :] for t in range(2)], 512,
                                 4 * h, 4, h == 0, h == 1)
            pe.wait_ge(ws_loaded, 16)
            for q in range(4):
                for j in range(4):
                    ins = nc.tensor.transpose(ps[:, q, j * P:(j + 1) * P], wsr[:, 4 * q + j, :], ident)
                ins.then_inc(ws_turned, 1)
            pe.wait_ge(v_added, 8)
            extract(4)
            pe.wait_ge(wst_ready, 4)
            for b in range(5):
                if b < 4:
                    u0 = (58, 60, 64, 68)[b]
                    if b >= 1:
                        pe.wait_ge(ub_ready, 4 * b)
                    else:
                        pe.wait_ge(v_added, 8)
                    for h in range(2):
                        w_hi, w_lo = unit(u0 + h, 512)
                        for c in range(4):
                            for kk in range(4):
                                k = 4 * h + kk
                                ins = three(ps[:, 4 + c // 2, (c % 2) * TOK:(c % 2 + 1) * TOK],
                                            w_hi[:, kk, c * P:(c + 1) * P], w_lo[:, kk, c * P:(c + 1) * P],
                                            hh[:, k, :], hl[:, k, :], h == 0 and c % 2 == 0 and kk == 0,
                                            h == 1 and kk == 3)
                        ins.then_inc(w_used, 1)
                    if b == 0:
                        pe.wait_ge(affine, 8)
                        pe.wait_ge(ex_taken, EX_BASE[5])
                    else:
                        pe.wait_ge(yr_ready, b)
                    for g in range(4):
                        for n in range(NT):
                            gg = 4 * b + g
                            ins = nc.tensor.matmul(ps[:, 6 + g // 2, (g % 2) * TOK + n * P:(g % 2) * TOK + (n + 1) * P],
                                                   vg[:, n, gg * P:(gg + 1) * P], wst[:, gg, :], start=True,
                                                   stop=True)
                    ins.then_inc(sp_done, 1)
                if b > 0:
                    pe.wait_ge(yl_ready, b)
                    w0 = (62, 66, 70, 72)[b - 1]
                    for j in range(2):
                        w_hi, w_lo = unit(w0 + j, D)
                        for kk in range(2):
                            for t in range(NT):
                                for cb in range(2):
                                    cc, tt = slice(cb * HALF, (cb + 1) * HALF), slice(t * P, (t + 1) * P)
                                    kq = 2 * j + kk
                                    ins = three(ps[:, 2 * t + cb, :], yh[:, (b - 1) % 2, kq, tt],
                                                yl[:, (b - 1) % 2, kq, tt], w_hi[:, kk, cc], w_lo[:, kk, cc],
                                                b == 1 and kq == 0, b == 4 and kq == 3)
                        ins.then_inc(w_used, 1)
            extract(5)
            turn(N_FF1, xn, 4)
            ffn(1)
            extract(7)
            turn(N_KV, xn, 4)
            pe.wait_ge(t_lo, 4 * (N_KV + 1))
            for b in range(4):
                if b >= 2:
                    pe.wait_ge(evac, 17 + 2 * (b - 1))
                for h in range(2):
                    rows_product(KV + 2 * b + h, None, lat, [ps[:, 2 * (b % 2) + t, :] for t in range(2)], 512,
                                 4 * h, 4, h == 0, h == 1)
            w_hi, w_lo = unit(KV + 8, FH)
            for t in range(NT):
                for k in range(KD):
                    ins = three(ps[:, 4, t * FH:(t + 1) * FH], hh[:, k, t * P:(t + 1) * P],
                                hl[:, k, t * P:(t + 1) * P], w_hi[:, k, :], w_lo[:, k, :], k == 0, k == KD - 1)
            ins.then_inc(w_used, 1)
            extract(8)
            pe.wait_ge(ls_ready, 1)
            ls = fz[:, 5]
            nc.tensor.matmul(ps[:, 5, 0:FH], tri, ls[:, 0, :], start=True, stop=True)
            nc.tensor.matmul(ps[:, 5, FH:2 * FH], tri, ls[:, 1, :], start=True, stop=False)
            nc.tensor.matmul(ps[:, 5, FH:2 * FH], ones, ls[:, 0, :], start=False, stop=True).then_inc(cum_done, 1)
            pe.wait_ge(ka_ready, 1)
            pe.wait_ge(ex_taken, EX_BASE[9])
            turn(N_MIX2, xn, 4)
            pe.wait_ge(t_lo, 4 * (N_MIX2 + 1))
            pe.wait_ge(evac, 25)
            for b in range(4):
                if b >= 2:
                    pe.wait_ge(evac, 25 + 2 * (b - 1))
                for h in range(2):
                    rows_product(QG + 2 * b + h, None, lat, [ps[:, 2 * (b % 2) + t, :] for t in range(2)], 512,
                                 4 * h, 4, h == 0, h == 1)

            def turn_heads(src, base):
                for q in range(8):
                    if base + q >= 4:
                        p_ = base + q - 4
                        pe.wait_ge(ft_evac if p_ % 2 else act_step, p_ // 2 + 1)
                    for j in range(4):
                        h, t = 2 * q + j // 2, j % 2
                        ins = nc.tensor.transpose(ps[0:FA, 4 + q % 4, j * P:(j + 1) * P], src[:, t, h, :], ident)
                    ins.then_inc(f_turned, 1)

            turn_heads(ka, 0)
            pe.wait_ge(qa_ready, 1)
            turn_heads(qa, 8)
            pe.wait_ge(ft_evac, 8)
            pe.wait_ge(act_step, 8)
            extract(9)
            pe.wait_ge(evac, 33)

            def fox_scores(h):
                if h >= 2:
                    pe.wait_ge(fp_ready, 2 * (h - 1))
                bank = 4 + h % 2
                nc.tensor.matmul(ps[:, bank, 0:P], qt_f[:, h, 0:P], kt_f[:, h, 0:P], start=True, stop=False,
                                 skip_group_check=True)
                nc.tensor.matmul(ps[:, bank, 0:P], ident, neg, start=False, stop=True, skip_group_check=True)
                nc.tensor.matmul(ps[:, bank, P:3 * P], qt_f[:, h, P:2 * P], kt_f[:, h, :], start=False, stop=False,
                                 skip_group_check=True)
                nc.tensor.matmul(ps[:, bank, 2 * P:3 * P], ident, neg, start=False, stop=True,
                                 skip_group_check=True).then_inc(fs_done, 1)

            def fox_turn(h):
                pe.wait_ge(fp_ready, 2 * h + 2)
                if h >= 2:
                    pe.wait_ge(fpt_ready, h - 1)
                for q in range(3):
                    ins = nc.tensor.transpose(ps[:, 6 + h % 2, q * P:(q + 1) * P],
                                              prob_f[:, h % 2, q * P:(q + 1) * P], ident)
                ins.then_inc(fp_turned, 1)

            def fox_values(h):
                pe.wait_ge(fpt_ready, h + 1)
                cc = slice((h % 8) * FD, (h % 8 + 1) * FD)
                vv = slice(h * FD, (h + 1) * FD)
                nc.tensor.matmul(ps[:, h // 8, cc], prob_ft[:, h % 2, 0:P], v_f[:, 0, vv], start=True, stop=True)
                nc.tensor.matmul(ps[:, 2 + h // 8, cc], prob_ft[:, h % 2, P:2 * P], v_f[:, 0, vv], start=True,
                                 stop=False)
                nc.tensor.matmul(ps[:, 2 + h // 8, cc], prob_ft[:, h % 2, 2 * P:3 * P], v_f[:, 1, vv], start=False,
                                 stop=True).then_inc(fpv_done, 1)

            pe.wait_ge(ex_taken, EX_BASE[10])
            fox_scores(0)
            for h in range(FH):
                if h + 1 < FH:
                    fox_scores(h + 1)
                fox_turn(h)
                if h >= 1:
                    fox_values(h - 1)
            fox_values(FH - 1)
            turn(N_FOX, o_f, 4)
            pe.wait_ge(t_lo, 4 * (N_FOX + 1))
            for j in range(4):
                acc_product(WO + j, hh, hl, 2 * j, j == 0, j == 3)
            turn(N_FF2, xn, 4)
            ffn(2)

        @block.gpsimd
        def _(pool):
            steps = [0]

            def link(ins):
                steps[0] += 1
                ins.then_inc(pool_step, 1)
                pool.wait_ge(pool_step, steps[0])

            def flat(v):
                return v.rearrange("a b -> (a b)") if len(v.shape) == 2 else v

            def load_brow(g):
                if g == 1:
                    pool.wait_ge(mod1_used, 1)
                elif g > 1:
                    pool.wait_ge(ex_done, EX_BASE[g])
                pool.dma_start(brow[:, :], ada[g][1]).then_inc(brow_loaded, 16)

            post_rows = [a["g_final"], a["post_mix_g_2"][0], a["post_ffn_g_2"][0], a["post_mix_g_2"][1],
                         a["post_ffn_g_2"][1]]

            def load_postg(k):
                pool.dma_start(postg[:, :], post_rows[k].partition_broadcast(P)).then_inc(postg_loaded, 16)

            a_bias, ln_g, ln_b = a["a_b_in_2"][0], a["a_ln_g_2"][0], a["a_ln_b_2"][0]
            b_s = a["a_b_s_2"][0].rearrange("g t -> (g t)")
            bc_rows = [a_bias[GW + b * HALF:GW + (b + 1) * HALF] for b in range(4)]
            for b in range(4):
                bc_rows += [ln_g[b * HALF:(b + 1) * HALF], ln_b[b * HALF:(b + 1) * HALF]]
            bc_rows += [b_s[b * HALF:(b + 1) * HALF] for b in range(4)]

            def load_bc(j):
                if 4 <= j < 8:
                    pool.wait_ge(v_added, 2 * (j - 4) + 2)
                elif j >= 8:
                    pool.wait_ge(affine, j - 7)
                pool.dma_start(bc[:, j % 4, :], bc_rows[j].partition_broadcast(P)).then_inc(bc_loaded[j % 4], 16)

            nc.gpsimd.memset(credit[:, 0:1], 0.0).then_inc(hid_pool, CREDIT)
            nc.gpsimd.memset(credit[:, 1:2], 0.0).then_inc(gl_done, CREDIT)
            load_brow(0)
            pool.dma_start(lg[:, 3, :], a["ret_decay"][0].rearrange("d h -> (d h)").partition_broadcast(P))\
                .then_inc(in_small, 16)
            pool.dma_start(bf[:, :], a["kv_b_f_2"].partition_broadcast(P)).then_inc(in_small, 16)
            pool.dma_start(gq[:, 0, :], a["b_q_norm_g_2"][0].partition_broadcast(P)).then_inc(in_small, 16)
            pool.dma_start(gq[:, 1, :], a["k_norm_g_2"].partition_broadcast(P)).then_inc(in_small, 16)
            load_postg(0)
            load_brow(1)
            load_brow(2)
            pool.wait_ge(evac, 14)
            pool.wait_ge(sq_done, SQ_BASE[R_C + 1])
            rb = rtmp_pool.rearrange("p (h a c) -> p h a c", h=RH, a=2)
            for src in (rq, rk):
                for t in range(NT):
                    xv = src[:, t, :].rearrange("p (h a c) -> p h a c", h=RH, a=2)
                    s_ = bcast(sin_r[:, t, :], 1, RH)
                    c_ = bcast(bcast(cos_r[:, t, :], 1, 2), 1, RH)
                    nc.gpsimd.tensor_tensor(rb[:, :, 0, :], xv[:, :, 1, :], s_, ALU.mult)
                    link(nc.gpsimd.tensor_tensor(rb[:, :, 1, :], xv[:, :, 0, :], s_, ALU.mult))
                    link(nc.gpsimd.tensor_tensor(xv, xv, c_, ALU.mult))
                    nc.gpsimd.tensor_tensor(xv[:, :, 0, :], xv[:, :, 0, :], rb[:, :, 0, :], ALU.subtract)
                    ins = nc.gpsimd.tensor_tensor(xv[:, :, 1, :], xv[:, :, 1, :], rb[:, :, 1, :], ALU.add)
                    ins.then_inc(ret_roped, 1)
                    pool.wait_ge(ret_roped, (0 if src is rq else 2) + t + 1)
            pool.wait_ge(pv_done, 2 * MLA_H)
            at = CONST_AT["diff"]
            pool.dma_start(diff[:, :, :], a["shape_consts"][:, at:at + NT * TOK].rearrange("p (t c) -> p t c", t=NT))\
                .then_inc(diff_loaded, 16)
            for h in range(RH):
                pool.wait_ge(mask_exp, h + 1)
                nc.gpsimd.tensor_tensor(mask[:, h, 2:4, :], mask[:, h, 2:4, :], mt[:, :, :], ALU.add)\
                    .then_inc(mask_ready, 1)
            load_brow(3)

            def pair(f, pp, i=None):
                more = 0 if i is None else 4 * i
                n, c = NFF * f + pp, pp % 2
                if f == 0:
                    pool.wait_ge(silu_done, n + 1 + more)
                    pool.wait_ge(gl_done, n - 1 + CREDIT + more)
                    nc.gpsimd.tensor_tensor(hid[:, c, :], sl[:, c, :], hu[:, c, 0, :], ALU.mult).then_inc(hid_pool, 1)
                pool.wait_ge(gh_done, n + 1 + more)
                at_ = bass.ds(pp + more, 1) if i is not None else slice(pp, pp + 1)
                nc.gpsimd.tensor_tensor(gl[:, at_, :], hid[:, c:c + 1, :], gh[:, at_, :].bitcast(F32), ALU.subtract)\
                    .then_inc(gl_done, 1)

            def ffn(f):
                with pool.Fori(0, 4) as i:
                    for j in range(4):
                        pair(f, j, i)
                for pp in range(16, NFF):
                    pair(f, pp)

            ffn(0)
            pool.wait_ge(w_used, split_no(DOWN[0] + 10) + 1)
            for j in range(4):
                load_bc(j)
            pool.dma_start(wsr[:, :, :], a["a_w_s_2"][0].rearrange("g t s -> t g s")).then_inc(ws_loaded, 16)
            load_brow(4)
            pool.wait_ge(x_ready, 3)
            load_postg(1)
            for j in range(4, 8):
                load_bc(j)
            load_brow(5)
            pool.wait_ge(ex_taken, EX_BASE[4] + 3)
            load_postg(2)
            for j in range(8, 16):
                load_bc(j)
            load_brow(6)
            pool.wait_ge(ex_taken, EX_BASE[5] + 3)
            load_postg(3)
            ffn(1)
            load_brow(7)
            load_brow(8)
            load_brow(9)
            pool.wait_ge(ex_taken, EX_BASE[8] + 3)
            load_postg(4)
            ffn(2)

        @block.sync
        def _(sp):
            def send(u):
                if u >= N_UNITS:
                    return
                src = units[u]
                if u >= RAW:
                    q = u - RAW
                    if q == W_UQ:
                        sp.wait_ge(q_proj, 4)
                    elif q == W_UKV:
                        sp.wait_ge(kv_proj, 8)
                    else:
                        sp.wait_ge(lo_done, split_no(q) + 1)
                dst = raw[:, u % RAW, 0:width(u)]
                if isinstance(src, tuple):
                    _, f, b, h = src
                    send_up(f, u % RAW, b, h)
                else:
                    chunks = src.shape[1]
                    dst = dst.rearrange("p (k c) -> p k c", k=chunks)
                    for k0 in (0, chunks // 2):
                        sp.dma_start(dst[:, k0:k0 + chunks // 2], src[:, k0:k0 + chunks // 2])\
                            .then_inc(raw_loaded[u % RAW], 16)

            def send_up(f, slot, b, h):
                dst = raw[:, slot, :].rearrange("p (k s c) -> p k s c", k=4, s=2)
                src = pair_blocks(up_w[f], b, h)
                for s in range(2):
                    sp.dma_start(dst[:, :, s], src[:, :, s]).then_inc(raw_loaded[slot], 16)

            def send_ada(v):
                if v >= 80:
                    return
                if v >= 2:
                    if v - 2 < 8:
                        sp.wait_ge(mod1_used, v - 1)
                    else:
                        sp.wait_ge(acc_step, v - 9)
                k = v % 8
                sp.dma_start(au[:, v % 2, :], ada[v // 8][0][k * P:(k + 1) * P, :]).then_inc(au_loaded[v % 2], 16)

            sp.dma_start(con[:, :], a["shape_consts"][:, 0:CONST_AT["diff"]]).then_inc(in_const, 16)
            for t, rows in enumerate(VEC_TILES):
                r = 0
                for name, first, n in rows:
                    v = a[name]
                    if len(v.shape) == 2:
                        v = v.rearrange("a b -> (a b)")
                    elif len(v.shape) == 3:
                        v = v.rearrange("a b c -> (a b c)")
                    sp.dma_start(vrow[r:r + n, t, :], v[first:first + n * P].rearrange("(r c) -> r c", c=P))\
                        .then_inc(in_rows, 16)
                    r += n
            send_ada(0)
            send_ada(1)
            sp.dma_start(x[:, :, :], a["x"][0].rearrange("(t p) d -> p t d", p=P)).then_inc(in_x, 16)
            sp.dma_start(cx[:, :, :], a["ctx"][0].rearrange("(t p) d -> p t d", p=P)).then_inc(in_ctx, 16)
            first_w = 0
            k = 0
            loops = {UP[f] + 2: f for f in range(3)}
            while k < len(taken):
                kind, n = taken[k]
                if kind == "w" and first_w < RAW:
                    pass
                if k == 8:
                    for u in range(RAW):
                        send(u)
                    first_w = RAW
                if kind == "w" and n in loops:
                    f = loops[n]
                    assert taken[k:k + 16] == [("w", n + j) for j in range(16)]
                    u0 = n + RAW
                    with sp.Fori(0, 4) as i:
                        for j in range(4):
                            sp.wait_ge(lo_done, split_no(n + j) + 1 + 4 * i)
                            send_up(f, (u0 + j) % RAW, 3 + j // 2 + 2 * i, j % 2)
                    k += 16
                    continue
                if kind == "w":
                    send(n + RAW)
                else:
                    send_ada(n + 2)
                k += 1
            sp.wait_ge(x_ready, 7)
            sp.dma_start(out[0].rearrange("(t p) d -> p t d", p=P), x[:, :, :]).then_inc(out_sent, 16)
            sp.wait_ge(out_sent, 16)


_INS = ["x", "c", "ctx", "c_ctx", "w_ada", "b_ada", "g_norm1", "w_in", "g_q", "w_uq", "g_kv", "w_ukv", "ret_decay",
        "g_ret", "w_out", "g_norm2", "w_up", "conv_w", "conv_b", "w_down", "g_final", "c_2", "ada_w_2", "ada_b_2",
        "pre_mix_g_2", "post_mix_g_2", "pre_ffn_g_2", "post_ffn_g_2", "ffn_w_gu_2", "ffn_w_down_2", "a_w_in_2",
        "a_b_in_2", "a_ln_g_2", "a_ln_b_2", "a_w_s_2", "a_b_s_2", "a_w_out_2", "kv_ada_w_2", "kv_ada_b_2",
        "kv_norm_g_2", "kv_w_2", "kv_b_f_2", "k_norm_g_2", "b_w_qg_2", "b_q_norm_g_2", "b_w_o_2"]


def kernel(**inputs):
    import concourse.bacc as bacc
    from concourse.bass_utils import run_bass_kernel_spmd as run

    nc = bacc.Bacc("TRN2", target_bir_lowering=False, num_devices=1)
    arrays, args = {}, {}
    for name in _INS:
        v = np.ascontiguousarray(inputs[name])
        arrays[f"in_{name}_dram"] = v
        args[name] = nc.dram_tensor(f"in_{name}_dram", v.shape, mybir.dt.from_np(v.dtype), kind="ExternalInput").ap()
    table = shape_constants()
    arrays["in_shape_consts_dram"] = table
    args["shape_consts"] = nc.dram_tensor("in_shape_consts_dram", table.shape, F32, kind="ExternalInput").ap()
    out = nc.dram_tensor("out_0_dram", (1, TOK, D), F32, kind="ExternalOutput").ap()
    build(nc, args, out)
    r = run(nc, [arrays], core_ids=[0])
    return r.results[0]["out_0_dram"]
```

```python
from contextlib import ExitStack

import numpy as np

import concourse.bass as bass
from concourse import mybir

ALU = mybir.AluOpType
ACT = mybir.ActivationFunctionType
AX = mybir.AxisListType
F32 = mybir.dt.float32
F32R = mybir.dt.float32r

P = 128
TOK = 256
NT = TOK // P
D = 1024
KD = D // P
EPS = 1e-6
GRID_W = 64

MLA_H, NOPE, ROPE, MLA_V = 8, 64, 32, 64
QK = NOPE + ROPE
MLA_SCALE = QK ** -0.5
RH, RDK = 4, 128
FF = 2816
NFF = FF // P
NBLK = NFF // 2
GW = 2048
NG = 16
FH, FD = 16, 64
FA = FD + 2
NEG = -1.0e30

UNIT = 2048
RAW = 4
HALF = 512

CONST_PARTS = [("ident", 128), ("ones", 128), ("tri", 128), ("neg", 128), ("pick", 512), ("cos_r", 128),
               ("sin_r", 128), ("cos_m", 32), ("sin_m", 32), ("diff", 512)]
CONST_AT = {}
CONST_W = 0
for _name, _w in CONST_PARTS:
    CONST_AT[_name] = CONST_W
    CONST_W += _w


def shape_constants():
    p = np.arange(P)
    tok = np.arange(TOK)
    c = np.zeros((P, CONST_W), np.float32)

    def put(name, value):
        c[:, CONST_AT[name]:CONST_AT[name] + value.shape[1]] = value

    put("ident", np.eye(P, dtype=np.float32))
    put("ones", np.ones((P, P), np.float32))
    put("tri", (p[:, None] <= p[None, :]).astype(np.float32))
    put("neg", np.where(p[None, :] <= p[:, None], 0.0, NEG).astype(np.float32))
    put("pick", np.repeat((p[:, None] == np.arange(4)[None, :]).astype(np.float32), P, axis=1))
    inv = (np.float32(10000.0) ** (-np.arange(0, RDK, 2, dtype=np.float32) / np.float32(RDK))).astype(np.float32)
    ang = (tok.astype(np.float32)[:, None] * inv[None, :]).astype(np.float32)
    for name, f in (("cos_r", np.cos), ("sin_r", np.sin)):
        put(name, f(ang).astype(np.float32).reshape(NT, P, RDK // 2).transpose(1, 0, 2).reshape(P, -1))
    half = ROPE // 2
    inv = (np.float32(10000.0) ** (-np.arange(0, half, 2, dtype=np.float32) / np.float32(half))).astype(np.float32)
    pos = np.stack([tok // GRID_W, tok % GRID_W], 1).astype(np.float32)
    ang = (pos[:, :, None] * inv[None, None, :]).astype(np.float32)
    for name, f in (("cos_m", np.cos), ("sin_m", np.sin)):
        put(name, f(ang).astype(np.float32).reshape(NT, P, half).transpose(1, 0, 2).reshape(P, -1))
    key = (np.arange(NT)[:, None] * P + p[None, :])
    put("diff", (tok[None, None, :] - key[:, :, None]).astype(np.float32).transpose(1, 0, 2).reshape(P, -1))
    return c


VEC_TILES = [
    [("c", 0, 8), ("c_ctx", 0, 8), ("c_2", 0, 8), ("g_norm1", 0, 8), ("g_q", 0, 2), ("g_kv", 0, 2),
     ("g_ret", 0, 4), ("g_norm2", 0, 8), ("conv_b", 0, 44), ("pre_mix_g_2", 0, 16), ("pre_ffn_g_2", 0, 16)],
    [("conv_w", 0, 88), ("a_b_in_2", 0, 16), ("kv_norm_g_2", 0, 8)],
    [("conv_w", 88 * P, 44)],
]
COL = {}
for _t, _rows in enumerate(VEC_TILES):
    _r = 0
    for _n, _e, _k in _rows:
        COL[(_n, _e)] = _t * P + _r
        _r += _k
VEC_ROWS = [sum(k for _, _, k in rows) for rows in VEC_TILES]

W_IN, W_UQ, W_UKV = 0, 11, 12
CKV = 544
EVACS = 22
W_OUT = 13
UP = [17, 74, 128]
DOWN = [39, 96, 150]
GM_V, GM_U = 50, 58
GM_ORDER = [("u", 0), ("u", 1), ("u", 2), ("o", 0), ("u", 3), ("o", 1), ("o", 2), ("o", 3)]
U_UNIT = [GM_U + 2 * GM_ORDER.index(("u", b)) for b in range(4)]
O_UNIT = [GM_U + 2 * GM_ORDER.index(("o", b)) for b in range(4)]
KV, QG, WO = 107, 116, 124
N_UNITS = 161
DIRECT = (W_UQ, W_UKV)


def split_no(u):
    return u if u < W_UQ else u - len(DIRECT)


N_X, N_CTX, N_RET, N_FF0, N_MIX1, N_FF1, N_KV, N_MIX2, N_FOX, N_FF2 = range(10)
GROUPS = [
    ("first",),
    ("gate_shift", N_FF0), ("scale_gate", N_FF0),
    ("shift_scale", N_MIX1), ("gate_shift", N_FF1), ("scale_gate", N_FF1),
    ("shift_scale", N_KV),
    ("shift_scale", N_MIX2), ("gate_shift", N_FF2), ("scale_gate", N_FF2),
]
GATE_SLOT = {1: 0, 2: 1, 4: 0, 5: 1, 8: 0, 9: 1}
POST_G = {4: 1, 5: 2, 8: 3, 9: 4}
EX_STEPS = [0] + [1 if g[0] == "shift_scale" else 3 for g in GROUPS[1:]]
EX_BASE = [sum(EX_STEPS[:g]) for g in range(len(GROUPS) + 1)]
ADA_AFTER = {}


def _spread(group, at):
    for k, u in enumerate(at):
        ADA_AFTER.setdefault(u, []).append(8 * group + k)


_spread(1, range(2, 10))
_spread(3, range(41, 49))
_spread(4, [51, 52, 53, 54, 55, 56, 57, 57])
_spread(5, range(64, 72))
ADA_AFTER.update({14: [16], 15: [21], 16: [22], 17: [23], 126: [77], 127: [78], 128: [79]})
_spread(6, range(92, 100))
_spread(7, [102, 103, 104, 105, 106, 109, 109, 110])
_spread(8, range(113, 121))
EXTRACT_AFTER = {58: 4, 101: 6, 111: 7}
EX_BANKS = {1: (5, 6, 7), 2: (7, 5, 6), 3: (7, 5, 6), 4: (4, 5, 4), 5: (7, 5, 6), 6: (7, 5, 6), 7: (1, 1, 1),
            8: (6, 7, 6), 9: (7, 5, 6)}
TURN_NO = [n - (n >= N_MIX2) for n in range(10)]
CREDIT = 4

R_X, R_CTX, R_C, R_RET, R_FF0, R_FIN, R_MIX1, R_LN, R_PM1, R_FF1, R_PF1, R_KV, R_KH, R_QH, R_PM2, R_FF2, R_PF2 = range(17)
R_W = [2, 2, 6, 8, 2, 2, 2, 2, 2, 2, 2, 2, 32, 32, 2, 2, 2]
R_AT = [sum(R_W[:r]) for r in range(len(R_W) + 1)]
SQ_N = [2, 2, 6, 0, 2, 2, 2, 0, 4, 2, 4, 2, 0, 0, 4, 2, 4]
SQ_BASE = [sum(SQ_N[:r]) for r in range(len(SQ_N) + 1)]
XN_NEED = [2, 4, 6, 8, 10, 12, 14, 14, 16, 18]


def build(nc, a, out):
    ctx = ExitStack()
    with ctx:
        def sb(name, shape, dt=F32):
            return ctx.enter_context(nc.sbuf_tensor(name, shape, dt))

        def sem(name):
            return ctx.enter_context(nc.semaphore(name))

        con = sb("con", [P, CONST_AT["diff"]])
        col = sb("col", [P, 3 * P])
        raw = sb("raw", [P, RAW, UNIT])
        wh = sb("wh", [P, 2, UNIT], F32R)
        wl = sb("wl", [P, 2, UNIT], F32R)
        au = sb("au", [P, 2, UNIT])
        acc = sb("acc", [P, UNIT])
        x = sb("x", [P, NT, D])
        gate = sb("gate", [P, 2, D])
        postg = sb("postg", [P, D])
        hraw = sb("hraw", [P, 2, HALF])
        junk = hraw[:, :, :].rearrange("p a c -> p (a c)")
        cs = sb("cs", [P, 24])
        mod = sb("mod", [P, 10, 2, KD])
        ss = sb("ss", [P, 128])
        ms = sb("ms", [P, 128])
        rt = sb("rt", [P, 128])
        rs = sb("rs", [P, 128])
        lg = sb("lg", [P, 4, 8])
        bns = sb("bns", [P, 8, 6])
        bna = sb("bna", [P, 8, 2])
        nmax = sb("nmax", [P, 32])
        psumr = sb("psumr", [P, 32])
        prec = sb("prec", [P, 32])
        credit = sb("credit", [P, 16])
        f_rows = sb("f_rows", [FH, TOK])
        bf = sb("bf", [P, FH])
        gq = sb("gq", [P, 2, FD])
        fz = sb("fz", [P, 6, NT, FH])
        dcum = sb("dcum", [P, NT, FH])
        vrow = junk[:, 0:3 * P].rearrange("p (t c) -> p t c", t=3)

        KB = 1024
        h_at = nc.sbuf_base + (-nc.sbuf_base) % 32
        h_area = sb("h_area", [P, 16 * KB // 4])
        r_at = nc.sbuf_base + (-nc.sbuf_base) % 32
        r_area = sb("r_area", [P, 64 * KB // 4])

        def in_h(name, kb, shape, dt=F32):
            return nc.alloc_sbuf_tensor_at(name, shape, dt, offset=h_at + int(kb * KB))

        def in_r(name, kb, shape, dt=F32):
            return nc.alloc_sbuf_tensor_at(name, shape, dt, offset=r_at + int(kb * KB))

        hh = in_h("hh", 0, [P, KD, TOK], F32R)
        hl = in_h("hl", 8, [P, KD, TOK], F32R)
        xn = in_r("xn", 52, [P, NT, D])
        m1 = in_r("m1", 32, [2, UNIT])
        mod1_w = [au[:, 0, :], au[:, 1, :]]
        for k, (place, kb) in enumerate(((in_h, 0), (in_h, 8), (in_r, 0), (in_r, 8), (in_r, 32), (in_r, 40))):
            mod1_w.append(place(f"mod1_w{k}", kb, [P, UNIT])[:, :])
        ch = in_r("ch", 0, [P, KD, TOK], F32R)
        cl = in_r("cl", 8, [P, KD, TOK], F32R)
        cx = in_r("cx", 16, [P, NT, D])
        xn_c = in_r("xn_c", 24, [P, NT, D])
        cqkv = in_r("cqkv", 32, [P, 6, 256])
        kpe = in_r("kpe", 38, [P, 4, ROPE])
        rk = in_r("rk", 40, [P, 4, HALF])
        rv = in_r("rv", 48, [P, 4, HALF])
        rq = in_r("rq", 56, [P, NT, HALF])
        rg = in_r("rg", 60, [P, NT, HALF])
        rtmp = hraw[:, 0, :]
        rtmp_pool = hraw[:, 1, :]
        kt_m = in_r("kt_m", 0, [QK, MLA_H, 2 * TOK])
        qt_m = in_r("qt_m", 16, [QK, MLA_H, TOK])
        v_m = in_r("v_m", 24, [P, 4, MLA_H, MLA_V])
        o = in_r("o", 32, [P, NT, D])
        cqt = in_h("cqt", 6, [P, 2, TOK])
        ckt = in_h("ckt", 8, [P, 2, 2 * TOK])
        qk_st = in_h("qk_st", 0, [P, 2, MLA_H, QK])
        prob = in_h("prob", 8, [P, 2, HALF])
        prob_t = in_h("prob_t", 12, [P, 2, HALF])
        rqt = in_r("rqt", 0, [P, RH, TOK])
        rkt = in_r("rkt", 4, [P, RH, 2 * TOK])
        mask = in_r("mask", 12, [P, RH, 4, TOK])
        mt = in_r("mt", 28, [P, 2, TOK])
        diff = in_r("diff", 30, [P, NT, TOK])
        pr = in_h("pr", 0, [P, 2, 4, TOK])
        gh = in_r("gh", 0, [P, NFF, TOK], F32R)
        gl = in_r("gl", 22, [P, NFF, TOK], F32R)
        hu = in_r("hu", 44, [P, 2, 2, TOK])
        sl = in_r("sl", 48, [P, 2, TOK])
        hid = in_r("hid", 50, [P, 2, TOK])
        vg = in_r("vg", 0, [P, NT, GW])
        wsr = in_r("wsr", 16, [P, NG, P])
        yh = in_r("yh", 16, [P, 2, 4, TOK], F32R)
        yl = in_r("yl", 24, [P, 2, 4, TOK], F32R)
        wst = in_r("wst", 32, [P, NG, P])
        bc = in_r("bc", 40, [P, 4, HALF])
        ub = [in_r("ub0", 48, [P, 4, TOK]), in_r("ub1", 60, [P, 4, TOK])]
        yr = in_r("yr", 52, [P, 4, TOK])
        kt_f = in_r("kt_f", 0, [FA, FH, TOK])
        qt_f = in_r("qt_f", 16, [FA, FH, TOK])
        v_f = in_r("v_f", 32, [P, NT, D])
        k_st = in_r("k_st", 40, [P, NT, D])
        hh2 = in_r("hh2", 16, [P, KD, TOK], F32R)
        hl2 = in_r("hl2", 24, [P, KD, TOK], F32R)
        ka = in_h("ka", 0, [P, NT, FH, FA])
        ksq = in_r("ksq", 0, [P, NT, D])
        q_st = in_r("q_st", 48, [P, NT, D])
        qa = in_h("qa", 0, [P, NT, FH, FA])
        qsq = in_r("qsq", 40, [P, NT, D])
        prob_f = in_h("prob_f", 0, [P, 2, 384])
        prob_ft = in_h("prob_ft", 3, [P, 2, 384])
        sg = in_r("sg", 56, [P, NT, D])
        o_f = in_r("o_f", 40, [P, NT, D])

        ps = ctx.enter_context(nc.psum_tensor("ps", [P, 8, HALF], F32))

        def const(name):
            at = CONST_AT[name]
            return con[:, at:at + dict(CONST_PARTS)[name]]

        ident, ones = const("ident"), const("ones")
        tri, neg = const("tri"), const("neg")
        pick = const("pick").rearrange("p (r c) -> p r c", r=4)
        cos_r = const("cos_r").rearrange("p (t c) -> p t c", t=NT)
        sin_r = const("sin_r").rearrange("p (t c) -> p t c", t=NT)
        cos_m = const("cos_m").rearrange("p (t a c) -> p t a c", t=NT, a=2)
        sin_m = const("sin_m").rearrange("p (t a c) -> p t a c", t=NT, a=2)

        def column(name, first=0, k=0):
            at = COL[(name, first)] + k
            return col[:, at:at + 1]

        def columns(name, k, n, first=0):
            at = COL[(name, first)] + k
            return col[:, at:at + n]

        def bcast(ap, at, n):
            ap = ap.unsqueeze(at)
            shape = list(ap.shape)
            shape[at] = n
            return ap.broadcast_to(tuple(shape))

        in_const = sem("in_const")
        in_rows = sem("in_rows")
        in_x = sem("in_x")
        in_ctx = sem("in_ctx")
        in_small = sem("in_small")
        raw_loaded = [sem(f"raw_loaded{i}") for i in range(RAW)]
        au_loaded = [sem(f"au_loaded{i}") for i in range(2)]
        acc_zeroed = sem("acc_zeroed")
        acc_biased = sem("acc_biased")
        mod1_loaded = [sem(f"mod1_loaded{i}") for i in range(6)]
        postg_loaded = sem("postg_loaded")
        bc_loaded = [sem(f"bc_loaded{i}") for i in range(4)]
        ws_loaded = sem("ws_loaded")
        hi_done = sem("hi_done")
        lo_done = sem("lo_done")
        w_used = sem("w_used")
        acc_step = sem("acc_step")
        ex_done = sem("ex_done")
        ex_taken = sem("ex_taken")
        cols_turned = sem("cols_turned")
        cols_ready = sem("cols_ready")
        cs_ready = sem("cs_ready")
        mod1_used = sem("mod1_used")
        mod1_ready = sem("mod1_ready")
        m1_ready = sem("m1_ready")
        m1_act = sem("m1_act")
        m1_turned = sem("m1_turned")
        lg_exp = sem("lg_exp")
        lg_ready = sem("lg_ready")
        sq_done = sem("sq_done")
        ms_ready = sem("ms_ready")
        rt_ready = sem("rt_ready")
        xn_ready = sem("xn_ready")
        x_ready = sem("x_ready")
        turned = sem("turned")
        t_raw = sem("t_raw")
        t_hi = sem("t_hi")
        t_lo = sem("t_lo")
        evac = sem("evac")
        dve_step = sem("dve_step")
        act_step = sem("act_step")
        pool_step = sem("pool_step")
        cn_ready = sem("cn_ready")
        c_turned = sem("c_turned")
        ct_ready = sem("ct_ready")
        q_proj = sem("q_proj")
        q_evac = sem("q_evac")
        q_roped = sem("q_roped")
        q_turned = sem("q_turned")
        qt_ready = sem("qt_ready")
        kv_proj = sem("kv_proj")
        k_evac = sem("k_evac")
        v_evac = sem("v_evac")
        kpe_roped = sem("kpe_roped")
        k_full = sem("k_full")
        diff_loaded = sem("diff_loaded")
        k_turned = sem("k_turned")
        kt_ready = sem("kt_ready")
        score = sem("score")
        max_ready = sem("max_ready")
        p_ready = sem("p_ready")
        p_turned = sem("p_turned")
        pt_ready = sem("pt_ready")
        pv_done = sem("pv_done")
        ret_roped = sem("ret_roped")
        r_turned = sem("r_turned")
        rt_evac = sem("rt_evac")
        arg_ready = sem("arg_ready")
        mask_exp = sem("mask_exp")
        mask_ready = sem("mask_ready")
        att_done = sem("att_done")
        pr_ready = sem("pr_ready")
        y_done = sem("y_done")
        up_done = sem("up_done")
        conv_base = sem("conv_base")
        conv_mid = sem("conv_mid")
        silu_done = sem("silu_done")
        hid_pool = sem("hid_pool")
        hid_dve = sem("hid_dve")
        gh_done = sem("gh_done")
        gl_done = sem("gl_done")
        v_added = sem("v_added")
        v_gelu = sem("v_gelu")
        affine = sem("affine")
        ws_turned = sem("ws_turned")
        wst_ready = sem("wst_ready")
        ub_ready = sem("ub_ready")
        sp_done = sem("sp_done")
        yr_ready = sem("yr_ready")
        yh_ready = sem("yh_ready")
        yl_ready = sem("yl_ready")
        f_act = sem("f_act")
        f_copied = sem("f_copied")
        head_sq = sem("head_sq")
        k_scaled = sem("k_scaled")
        f_cols = sem("f_cols")
        f_pre = sem("f_pre")
        ls_ready = sem("ls_ready")
        cum_done = sem("cum_done")
        ka_ready = sem("ka_ready")
        qa_ready = sem("qa_ready")
        f_turned = sem("f_turned")
        ft_evac = sem("ft_evac")
        fs_done = sem("fs_done")
        fm_ready = sem("fm_ready")
        fp_ready = sem("fp_ready")
        fp_turned = sem("fp_turned")
        fpt_ready = sem("fpt_ready")
        fpv_done = sem("fpv_done")
        fo_ready = sem("fo_ready")
        out_sent = sem("out_sent")

        def k_major(w, k0, k1, c0, c1):
            return w[k0 * P:k1 * P, c0:c1].rearrange("(k p) n -> p k n", p=P)

        def pair_blocks(w, b, h):
            v = w.rearrange("(k p) (s n) -> p k s n", p=P, s=2)
            return v[:, 4 * h:4 * h + 4, :, bass.ds(b * 256, 256)]

        w_in = a["w_in"][0]
        units = []
        units += [k_major(w_in, k0, min(k0 + 3, KD), 0, CKV) for k0 in range(0, KD, 3)]
        for c0 in (CKV + 512, CKV + 1024, CKV, CKV + 1536):
            units += [k_major(w_in, 4 * h, 4 * h + 4, c0, c0 + 512) for h in range(2)]
        units.append(k_major(a["w_uq"][0], 0, 2, 0, MLA_H * QK))
        units.append(k_major(a["w_ukv"][0], 0, 2, 0, 1024))
        units += [k_major(a["w_out"][0], 2 * j, 2 * j + 2, 0, D) for j in range(4)]
        up_w = [a["w_up"][0], a["ffn_w_gu_2"][0], a["ffn_w_gu_2"][1]]
        down_w = [a["w_down"][0], a["ffn_w_down_2"][0], a["ffn_w_down_2"][1]]

        def ffn_units(f):
            got = [("up", f, b, h) for b in range(NBLK) for h in range(2)]
            return got + [k_major(down_w[f], 2 * j, 2 * j + 2, 0, D) for j in range(NBLK)]

        units += ffn_units(0)
        a_in, a_out = a["a_w_in_2"][0], a["a_w_out_2"][0]
        for b in range(4):
            units += [k_major(a_in, 4 * h, 4 * h + 4, GW + b * 512, GW + b * 512 + 512) for h in range(2)]
        for kind, b in GM_ORDER:
            if kind == "u":
                units += [k_major(a_in, 4 * h, 4 * h + 4, b * 512, b * 512 + 512) for h in range(2)]
            else:
                units += [k_major(a_out, 4 * b + 2 * h, 4 * b + 2 * h + 2, 0, D) for h in range(2)]
        units += ffn_units(1)
        for b in range(4):
            units += [k_major(a["kv_w_2"], 4 * h, 4 * h + 4, b * 512, b * 512 + 512) for h in range(2)]
        units.append(k_major(a["kv_w_2"], 0, KD, 2048, 2048 + FH))
        for b in range(4):
            units += [k_major(a["b_w_qg_2"][0], 4 * h, 4 * h + 4, b * 512, b * 512 + 512) for h in range(2)]
        units += [k_major(a["b_w_o_2"][0], 2 * j, 2 * j + 2, 0, D) for j in range(4)]
        units += ffn_units(2)
        assert len(units) == N_UNITS

        def width(u):
            if isinstance(units[u], tuple):
                return UNIT
            return units[u].shape[1] * units[u].shape[2]

        ada = []
        for g in range(10):
            if g < 3:
                w, bias, c0 = a["w_ada"][0], a["b_ada"][0], g * 2048
            elif g < 6:
                w, bias, c0 = a["ada_w_2"][0], a["ada_b_2"][0], (g - 3) * 2048
            elif g == 6:
                w, bias, c0 = a["kv_ada_w_2"], a["kv_ada_b_2"], 0
            else:
                w, bias, c0 = a["ada_w_2"][1], a["ada_b_2"][1], (g - 7) * 2048
            ada.append((w[:, c0:c0 + 2048], bias[c0:c0 + 2048].rearrange("(r c) -> r c", r=1)))

        taken = []

        block = ctx.enter_context(nc.Block())

        @block.vector
        def _(dve):
            steps = [0]

            def link(ins):
                steps[0] += 1
                ins.then_inc(dve_step, 1)
                dve.wait_ge(dve_step, steps[0])

            def lo_part(u, s, i=None):
                more = 0 if i is None else 4 * i
                dve.wait_ge(hi_done, s + 1 + more)
                n = width(u)
                nc.vector.tensor_tensor(wl[:, s % 2, 0:n], raw[:, u % RAW, 0:n], wh[:, s % 2, 0:n].bitcast(F32),
                                        ALU.subtract).then_inc(lo_done, 1)

            def ada_part(v):
                g, k = v // 8, v % 8
                dve.wait_ge(au_loaded[v % 2], 16 * (v // 2 - 2))
                at = (16 if g > 2 else 0) + k
                if k == 0:
                    dve.wait_ge(acc_biased, 16 * (g + 1))
                else:
                    dve.wait_ge(acc_step, v - 8)
                nc.vector.scalar_tensor_tensor(acc[:, :], au[:, v % 2, :], cs[:, at:at + 1], acc[:, :],
                                               ALU.mult, ALU.add).then_inc(acc_step, 1)
                taken.append(("a", v))

            def extract(g):
                kind, n = GROUPS[g]
                ba, b0, b1 = EX_BANKS[g]
                e = EX_BASE[g]
                dve.wait_ge(ex_done, e + 1)
                gains = {N_FF0: ("g_norm2", 0), N_MIX1: ("pre_mix_g_2", 0), N_FF1: ("pre_ffn_g_2", 0),
                         N_KV: ("kv_norm_g_2", 0), N_MIX2: ("pre_mix_g_2", 8), N_FF2: ("pre_ffn_g_2", 8)}[n]
                gain = columns(gains[0], gains[1], KD)
                if kind == "shift_scale":
                    nc.vector.tensor_copy(mod[:, n, 1, :], ps[:, ba, 0:8])
                    nc.vector.scalar_tensor_tensor(mod[:, n, 0, :], ps[:, ba, 8:16], 1.0, gain, ALU.add,
                                                   ALU.mult).then_inc(ex_taken, 1)
                    return
                if kind == "gate_shift":
                    nc.vector.tensor_copy(mod[:, n, 1, :], ps[:, ba, 0:8]).then_inc(ex_taken, 1)
                else:
                    nc.vector.scalar_tensor_tensor(mod[:, n, 0, :], ps[:, ba, 0:8], 1.0, gain, ALU.add,
                                                   ALU.mult).then_inc(ex_taken, 1)
                if g in POST_G:
                    dve.wait_ge(postg_loaded, 16 * (POST_G[g] + 1))
                for h, bank in ((0, b0), (1, b1)):
                    dve.wait_ge(ex_done, e + 2 + h)
                    to = gate[:, GATE_SLOT[g], h * HALF:(h + 1) * HALF]
                    if g in POST_G:
                        ins = nc.vector.tensor_tensor(to, ps[:, bank, :], postg[:, h * HALF:(h + 1) * HALF], ALU.mult)
                    else:
                        ins = nc.vector.tensor_copy(to, ps[:, bank, :])
                    ins.then_inc(ex_taken, 1)

            def take(u):
                if u >= N_UNITS:
                    return
                if u not in DIRECT:
                    lo_part(u, split_no(u))
                taken.append(("w", u))
                if u in EXTRACT_AFTER:
                    extract(EXTRACT_AFTER[u])
                for v in ADA_AFTER.get(u, ()):
                    ada_part(v)

            def rstd(r, scale, src=None):
                c0, c1 = R_AT[r], R_AT[r + 1]
                nc.vector.tensor_scalar(ms[:, c0:c1], ss[:, c0:c1] if src is None else src, scale, EPS, ALU.mult,
                                        ALU.add).then_inc(ms_ready, 1)
                dve.wait_ge(rt_ready, r + 1)
                link(nc.vector.reciprocal(rs[:, c0:c1], rt[:, c0:c1]))

            def rs_of(r, k):
                return rs[:, R_AT[r] + k:R_AT[r] + k + 1]

            def normalise(r, src, dst):
                dve.wait_ge(sq_done, SQ_BASE[r + 1])
                rstd(r, 1.0 / D)
                for t in range(NT):
                    nc.vector.tensor_scalar(dst[:, t, :], src[:, t, :], rs_of(r, t), None,
                                            ALU.mult).then_inc(xn_ready, 1)

            def low_of_turned(n, lo=None, hi=None):
                lo, hi = lo or hl, hi or hh
                for b in range(4):
                    dve.wait_ge(t_hi, 4 * n + b + 1)
                    nc.vector.tensor_tensor(lo[:, 2 * b:2 * b + 2, :],
                                            hraw[:, b % 2, :].rearrange("p (k t) -> p k t", k=2),
                                            hi[:, 2 * b:2 * b + 2, :].bitcast(F32), ALU.subtract).then_inc(t_lo, 1)

            def residual(last_unit, slot, r=None, done=1):
                if r is None:
                    dve.wait_ge(w_used, split_no(last_unit) + 1)
                else:
                    dve.wait_ge(sq_done, SQ_BASE[r + 1])
                    c = R_AT[r]
                    link(nc.vector.tensor_tensor(ss[:, c:c + 2], ss[:, c:c + 3:2], ss[:, c + 1:c + 4:2], ALU.add))
                    rstd(r, 1.0 / D)
                for t in range(NT):
                    acc_t = ps[:, 2 * t:2 * t + 2, :].rearrange("p a c -> p (a c)")
                    if r is None:
                        link(nc.vector.tensor_tensor(xn[:, t, :], acc_t, gate[:, slot, :], ALU.mult))
                    else:
                        link(nc.vector.scalar_tensor_tensor(xn[:, t, :], acc_t, rs_of(r, t), gate[:, slot, :], ALU.mult,
                                                            ALU.mult))
                    nc.vector.tensor_tensor(x[:, t, :], x[:, t, :], xn[:, t, :], ALU.add).then_inc(x_ready, 1)
                dve.wait_ge(x_ready, 2 * done)

            nc.vector.memset(nmax[:, :], 0.0).then_inc(hid_dve, CREDIT)
            dve.wait_ge(cols_turned, 3)
            for t, rows in enumerate(VEC_ROWS):
                ins = nc.vector.tensor_copy(col[:, t * P:t * P + rows], ps[:, 7, t * P:t * P + rows])
            ins.then_inc(cols_ready, 1)
            dve.wait_ge(cols_ready, 1)
            nc.vector.memset(mod[:, N_RET, 0, 0:4], 1.0)
            nc.vector.tensor_copy(mod[:, N_RET, 0, 4:8], columns("g_ret", 0, 4))
            nc.vector.memset(mod[:, N_RET, 1, :], 0.0)
            nc.vector.memset(mod[:, N_FOX, 0, :], 1.0)
            link(nc.vector.memset(mod[:, N_FOX, 1, :], 0.0))
            dve.wait_ge(lg_exp, 1)
            nc.vector.tensor_scalar(lg[:, 0, :], lg[:, 1, :], -1.0, None, ALU.mult)
            nc.vector.tensor_scalar(lg[:, 2, :], lg[:, 1, :], -float(TOK), None, ALU.mult).then_inc(lg_ready, 1)
            normalise(R_X, x, xn)
            normalise(R_CTX, cx, xn_c)
            dve.wait_ge(mod1_used, 8)
            for q in range(2):
                nc.vector.tensor_copy(m1[0:2, q * HALF:(q + 1) * HALF], ps[0:2, q, :]).then_inc(m1_ready, 1)
            dve.wait_ge(m1_turned, 1)
            m1t = ps[:, 6, 0:32].rearrange("p (k j) -> p k j", j=2)
            for j, n in ((0, N_X), (1, N_CTX)):
                nc.vector.tensor_copy(mod[:, n, 1, :], m1t[:, 0:8, j])
                ins = nc.vector.scalar_tensor_tensor(mod[:, n, 0, :], m1t[:, 8:16, j], 1.0,
                                                     columns("g_norm1", 0, KD), ALU.add, ALU.mult)
            ins.then_inc(mod1_ready, 1)
            take(0)
            take(1)
            low_of_turned(N_X)
            low_of_turned(N_CTX, cl, ch)
            for u in range(2, 5):
                take(u)
            dve.wait_ge(sq_done, SQ_BASE[R_C + 1])
            rstd(R_C, 1.0 / 256)
            for j in range(6):
                nc.vector.tensor_scalar(cqkv[:, j, :], cqkv[:, j, :], rs_of(R_C, j), None,
                                        ALU.mult).then_inc(cn_ready, 1)

            def rope_m(xv, t, h, first, buf):
                c, s = cos_m[:, t], sin_m[:, t]
                if h > 1:
                    c, s = bcast(c, 1, h), bcast(s, 1, h)
                x1, x2 = xv[..., 0:8], xv[..., 8:16]
                w = [buf[:, j] for j in range(4)]
                nc.vector.tensor_tensor(w[0], x1, c, ALU.mult)
                nc.vector.tensor_tensor(w[1], x2, s, ALU.mult)
                nc.vector.tensor_tensor(w[2], x1, s, ALU.mult)
                link(nc.vector.tensor_tensor(w[3], x2, c, ALU.mult))
                nc.vector.tensor_tensor(x1, w[0], w[1], ALU.subtract)
                return nc.vector.tensor_tensor(x2, w[2], w[3], ALU.add)

            rope_buf = rtmp.rearrange("p (j h a c) -> p j h a c", j=4, h=MLA_H, a=2)
            for t in range(NT):
                xv = kpe[:, t, :].rearrange("p (a c) -> p a c", a=2)
                ins = rope_m(xv, t, 1, False, rope_buf[:, :, 0])
                if t == 0:
                    link(ins)
            ins.then_inc(kpe_roped, 1)
            dve.wait_ge(kpe_roped, 1)
            for u in range(5, 14):
                take(u)
            extract(1)
            for t in range(NT):
                dve.wait_ge(q_evac, 2 * t + 2)
                xv = qk_st[:, t, :, NOPE:QK].rearrange("p h (a c) -> p h a c", a=2)
                ins = rope_m(xv, t, MLA_H, False, rope_buf)
                ins.then_inc(q_roped, 1)
                dve.wait_ge(q_roped, t + 1)
            take(14)
            for t in range(4):
                for half in range(2):
                    dve.wait_ge(kv_proj, 2 * t + half + 1)
                    src = ps[:, 4 + 2 * (t % 2) + half, :].rearrange("p (h c) -> p h c", h=4)
                    dve.wait_ge(k_evac, 2 * t + half + 1)
                    nc.vector.tensor_copy(v_m[:, t, 4 * half:4 * half + 4, :], src[:, :, NOPE:]).then_inc(v_evac, 1)
                nc.vector.tensor_copy(qk_st[:, t % 2, :, NOPE:QK], bcast(kpe[:, t, :], 1, MLA_H)).then_inc(k_full, 1)

            def head_max(it):
                dve.wait_ge(score, it + 1)
                nc.vector.tensor_reduce(nmax[:, it:it + 1], ps[:, 4 + it % 2, :], AX.X, ALU.max,
                                        negate=True).then_inc(max_ready, 1)

            head_max(0)
            for it in range(2 * MLA_H):
                if it + 1 < 2 * MLA_H:
                    head_max(it + 1)
                dve.wait_ge(p_turned, it + 1)
                if it >= 2:
                    dve.wait_ge(pv_done, it - 1)
                nc.vector.tensor_copy(prob_t[:, it % 2, :], ps[:, 6 + it % 2, :]).then_inc(pt_ready, 1)
                if it % 4 == 3:
                    ada_part(17 + it // 4)
            dve.wait_ge(p_ready, 2 * MLA_H)
            link(nc.vector.reciprocal(prec[:, 0:16], psumr[:, 0:16]))
            dve.wait_ge(pv_done, 2 * MLA_H)
            for t in range(NT):
                nc.vector.tensor_tensor(o[:, t, 0:HALF].rearrange("p (h c) -> p h c", h=MLA_H),
                                        ps[:, t, :].rearrange("p (h c) -> p h c", h=MLA_H),
                                        bcast(prec[:, t:16:2], 2, MLA_V), ALU.mult)
            d2 = diff[:, :, :]
            dve.wait_ge(diff_loaded, 16)
            for h in range(RH):
                link(nc.vector.tensor_scalar(mask[:, h, 0:2, :], d2, lg[:, 1, 4 + h:5 + h], None, ALU.mult))
                nc.vector.scalar_tensor_tensor(mask[:, h, 0:2, :], d2, lg[:, 0, h:h + 1], mask[:, h, 0:2, :],
                                               ALU.mult, ALU.min).then_inc(arg_ready, 1)
            for h in range(RH):
                dve.wait_ge(mask_ready, h + 1)
                for half in range(2):
                    dve.wait_ge(att_done, 2 * h + half + 1)
                    if h >= 2:
                        dve.wait_ge(y_done, h - 1)
                    bank = 4 + 2 * (h % 2) + half
                    nc.vector.tensor_tensor(pr[:, h % 2, 2 * half:2 * half + 2, :],
                                            ps[:, bank, :].rearrange("p (k t) -> p k t", k=2),
                                            mask[:, h, 2 * half:2 * half + 2, :], ALU.mult).then_inc(pr_ready, 1)
            dve.wait_ge(y_done, RH)
            for t in range(NT):
                for h in range(RH):
                    ins = nc.vector.bn_stats(bns[:, t * RH + h, :], ps[:, t, h * RDK:(h + 1) * RDK])
            link(ins)
            for j in range(NT * RH):
                ins = nc.vector.bn_aggr(bna[:, j, :], bns[:, j, :])
            link(ins)
            rstd(R_RET, 1.0, bna[:, :, 1])
            for t in range(NT):
                for h in range(RH):
                    j = t * RH + h
                    ins = nc.vector.tensor_scalar(o[:, t, HALF + h * RDK:HALF + (h + 1) * RDK],
                                                  ps[:, t, h * RDK:(h + 1) * RDK], bna[:, j, 0:1], rs_of(R_RET, j),
                                                  ALU.subtract, ALU.mult)
                link(ins)
                nc.vector.tensor_tensor(o[:, t, HALF:], o[:, t, HALF:], rg[:, t, :], ALU.mult).then_inc(xn_ready, 1)
            low_of_turned(N_RET)
            take(15)
            take(16)
            take(17)
            residual(W_OUT + 3, 0, done=1)
            extract(2)
            normalise(R_FF0, x, xn)
            take(18)
            low_of_turned(N_FF0)

            def conv(pp, c, i=None):
                more = 0 if i is None else 4 * i
                dve.wait_ge(conv_base, 2 * (pp + 1) + 2 * more)
                bank = 4 + pp % 4

                def tap(which, half):
                    k = COL[("conv_w", 0 if which == 0 else 88 * P)] + half * NFF + pp
                    w = col[:, bass.ds(k + more, 1)] if i is not None else col[:, k:k + 1]
                    if which == 0:
                        to, src = hu[:, c, half, 1:TOK], ps[:, bank, half * TOK:half * TOK + TOK - 1]
                    else:
                        to, src = hu[:, c, half, 0:TOK - 1], ps[:, bank, half * TOK + 1:half * TOK + TOK]
                    return nc.vector.scalar_tensor_tensor(to, src, w, to, ALU.mult, ALU.add)

                for n, (which, half) in enumerate(((0, 0), (0, 1), (2, 0), (2, 1))):
                    if n == 2:
                        dve.wait_ge(conv_mid, 4 * pp + 1 + 4 * more)
                    if n == 3:
                        dve.wait_ge(conv_mid, 4 * pp + 2 + 4 * more)
                    tap(which, half).then_inc(conv_mid, 1)

            def gated(f, pp, c, i=None):
                more = 0 if i is None else 4 * i
                dve.wait_ge(silu_done, NFF * f + pp + 1 + more)
                dve.wait_ge(gl_done, NFF * f + pp - 1 + CREDIT + more)
                nc.vector.tensor_tensor(hid[:, c, :], sl[:, c, :], ps[:, 4 + pp % 4, TOK:], ALU.mult)\
                    .then_inc(hid_dve, 1)

            def ffn(f):
                u0, s0 = UP[f], split_no(UP[f])
                pair = (lambda pp, c, i=None: conv(pp, c, i)) if f == 0 else \
                    (lambda pp, c, i=None: gated(f, pp, c, i))
                base = 2
                with dve.Fori(0, 4) as i:
                    for j in range(4):
                        lo_part(u0 + j + base, s0 + j + base, i)
                        pair(j, j % 2, i)
                for i in range(4):
                    taken.extend(("w", u0 + base + 4 * i + j) for j in range(4))
                for pp in range(16, NFF):
                    take(u0 + base + pp)
                    pair(pp, pp % 2)
                for j in range(NBLK - 1):
                    take(DOWN[f] + j + base)

            ffn(0)
            residual(DOWN[0] + 10, 1, done=2)
            dve.wait_ge(sq_done, SQ_BASE[R_FIN + 1])
            rstd(R_FIN, 1.0 / D)
            dve.wait_ge(postg_loaded, 16)
            for t in range(NT):
                nc.vector.scalar_tensor_tensor(x[:, t, :], x[:, t, :], rs_of(R_FIN, t), postg[:, :], ALU.mult,
                                               ALU.mult).then_inc(x_ready, 1)
            dve.wait_ge(x_ready, 6)
            extract(3)
            normalise(R_MIX1, x, xn)
            take(DOWN[0] + 12)
            low_of_turned(N_MIX1)
            for b in range(4):
                take(GM_V + 2 * b + 2)
                for t in range(NT):
                    dve.wait_ge(w_used, split_no(GM_V + 2 * b + 1) + 1)
                    if t == 0:
                        dve.wait_ge(bc_loaded[b], 16)
                    nc.vector.tensor_tensor(vg[:, t, b * HALF:(b + 1) * HALF], ps[:, 4 + 2 * (b % 2) + t, :],
                                            bc[:, b, :], ALU.add).then_inc(v_added, 1)
                take(GM_V + 2 * b + 3)
            for t in range(NT):
                for b in range(4):
                    dve.wait_ge(v_gelu, 2 * b + t + 1)
                    ins = nc.vector.bn_stats(bns[:, t * 4 + b, :], vg[:, t, b * HALF:(b + 1) * HALF])
            link(ins)
            for t in range(NT):
                ins = nc.vector.bn_aggr(bna[:, t, :], bns[:, 4 * t:4 * t + 4, :].rearrange("p a b -> p (a b)"))
            link(ins)
            rstd(R_LN, 1.0, bna[:, 0:2, 1])
            for t in range(NT):
                ins = nc.vector.tensor_scalar(vg[:, t, :], vg[:, t, :], bna[:, t, 0:1], rs_of(R_LN, t), ALU.subtract,
                                              ALU.mult)
            link(ins)
            take(U_UNIT[1])
            for b in range(4):
                part = vg[:, :, b * HALF:(b + 1) * HALF]
                for j, op in ((4 + 2 * b, ALU.mult), (5 + 2 * b, ALU.add)):
                    dve.wait_ge(bc_loaded[j % 4], 16 * (j // 4 + 1))
                    nc.vector.tensor_tensor(part, part, bcast(bc[:, j % 4, :], 1, NT), op).then_inc(affine, 1)
                    dve.wait_ge(affine, j - 3)
                if b == 0:
                    take(U_UNIT[1] + 1)
            for q in range(4):
                dve.wait_ge(ws_turned, q + 1)
                nc.vector.tensor_tensor(wst[:, 4 * q:4 * q + 4, :], ps[:, q, :].rearrange("p (g t) -> p g t", g=4),
                                        bcast(tri, 1, 4), ALU.mult).then_inc(wst_ready, 1)
            for b, (before, after) in enumerate((((62, 63), ()), ((64, 65), (66, 67)), ((68, 69), (70, 71)),
                                                 ((), (72, 73)))):
                for u in before:
                    take(u)
                nb = 12 + b
                dve.wait_ge(bc_loaded[nb % 4], 16 * (nb // 4 + 1))
                dve.wait_ge(sp_done, b + 1)
                if b >= 1:
                    dve.wait_ge(yl_ready, b)
                for q in range(2):
                    bias = bcast(bc[:, nb % 4, :].rearrange("p (g t) -> p g t", g=4)[:, 2 * q:2 * q + 2, :], 2, NT)
                    ins = nc.vector.tensor_tensor(
                        yr[:, 2 * q:2 * q + 2, :].rearrange("p g (n t) -> p g n t", n=NT),
                        ps[:, 6 + q, :].rearrange("p (g n t) -> p g n t", g=2, n=NT), bias, ALU.add)
                link(ins)
                dve.wait_ge(ub_ready, 4 * b + 4)
                nc.vector.tensor_tensor(yr[:, :, :], yr[:, :, :], ub[b % 2][:, :, :], ALU.mult).then_inc(yr_ready, 1)
                dve.wait_ge(yh_ready, b + 1)
                nc.vector.tensor_tensor(yl[:, b % 2], yr[:, :, :], yh[:, b % 2].bitcast(F32), ALU.subtract)\
                    .then_inc(yl_ready, 1)
                for u in after:
                    take(u)
            take(74)
            residual(None, 0, R_PM1, done=4)
            extract(5)
            normalise(R_FF1, x, xn)
            take(75)
            low_of_turned(N_FF1)
            ffn(1)
            residual(None, 1, R_PF1, done=5)
            normalise(R_KV, x, xn)
            take(DOWN[1] + 12)
            low_of_turned(N_KV)
            for u in range(KV + 2, KV + 8):
                take(u)
            low_of_turned(N_MIX2, hl2, hh2)

            def head_sums(sq, r, done):
                for t in range(NT):
                    dve.wait_ge(head_sq, done + t + 1)
                    c = R_AT[r] + t * FH
                    link(nc.vector.reduce_sum(ss[:, c:c + FH], sq[:, t, :].rearrange("p (h c) -> p h c", h=FH), AX.X))
                c0, c1 = R_AT[r], R_AT[r + 1]
                nc.vector.tensor_scalar(ms[:, c0:c1], ss[:, c0:c1], 1.0 / FD, EPS, ALU.mult,
                                        ALU.add).then_inc(ms_ready, 1)

            def head_rstd(r):
                dve.wait_ge(rt_ready, r + 1)
                link(nc.vector.reciprocal(rs[:, R_AT[r]:R_AT[r + 1]], rt[:, R_AT[r]:R_AT[r + 1]]))

            take(KV + 8)
            head_sums(ksq, R_KH, 0)
            take(QG)
            head_rstd(R_KH)
            dve.wait_ge(w_used, split_no(KV + 8) + 1)
            for t in range(NT):
                c = R_AT[R_KH] + t * FH
                nc.vector.tensor_tensor(ka[:, t, :, 0:FD], k_st[:, t, :].rearrange("p (h c) -> p h c", h=FH),
                                        bcast(rs[:, c:c + FH], 2, FD), ALU.mult).then_inc(k_scaled, 1)
            nc.vector.memset(ka[:, :, :, FD:FD + 1], 1.0)
            for u in range(QG + 1, QG + 4):
                take(u)
            z, az, e1, mn, ln, ls = (fz[:, j] for j in range(6))
            dve.wait_ge(in_small, 16 * 4)
            dve.wait_ge(f_cols, 1)
            link(nc.vector.tensor_tensor(z, ps[:, 4, TOK:TOK + 32].rearrange("p (t h) -> p t h", t=NT),
                                         bcast(bf[:, :], 1, NT), ALU.add))
            nc.vector.tensor_scalar(mn, z, 0.0, None, ALU.min)
            nc.vector.scalar_tensor_tensor(az, z, -1.0, z, ALU.mult, ALU.max).then_inc(f_pre, 1)
            dve.wait_ge(f_act, 1)
            nc.vector.tensor_scalar(e1, e1, 1.0, None, ALU.add).then_inc(f_pre, 1)
            link(nc.vector.tensor_tensor(gq[:, 0, :], gq[:, 0, :], gq[:, 1, :], ALU.mult))
            link(nc.vector.tensor_scalar(gq[:, 0, :], gq[:, 0, :], FD ** -0.5, None, ALU.mult))
            dve.wait_ge(f_act, 2)
            nc.vector.tensor_tensor(ls, mn, ln, ALU.subtract).then_inc(ls_ready, 1)
            take(QG + 4)
            take(QG + 5)
            dve.wait_ge(cum_done, 1)
            link(nc.vector.tensor_copy(dcum[:, :, :], ps[:, 5, 0:32].rearrange("p (t h) -> p t h", t=NT)))
            nc.vector.tensor_scalar(ka[:, :, :, FD + 1], dcum[:, :, :], -1.0, None, ALU.mult).then_inc(ka_ready, 1)
            head_sums(qsq, R_QH, 2)
            take(QG + 6)
            extract(8)

            def turned_heads(to, base):
                for q in range(0, 8, 2):
                    dve.wait_ge(f_turned, base + q + 2)
                    nc.vector.tensor_copy(to[:, 2 * q + 2:2 * q + 4, :],
                                          ps[0:FA, 4 + (q + 1) % 4, :].rearrange("p (h t) -> p h t", h=2))\
                        .then_inc(ft_evac, 1)

            turned_heads(kt_f, 0)
            take(QG + 7)
            head_rstd(R_QH)
            for t in range(NT):
                c = R_AT[R_QH] + t * FH
                to = qa[:, t, :, 0:FD]
                link(nc.vector.tensor_tensor(to, q_st[:, t, :].rearrange("p (h c) -> p h c", h=FH),
                                             bcast(rs[:, c:c + FH], 2, FD), ALU.mult))
                nc.vector.tensor_tensor(to, to, bcast(gq[:, 0, :], 1, FH), ALU.mult)
            nc.vector.memset(qa[:, :, :, FD + 1:FD + 2], 1.0)
            nc.vector.tensor_copy(qa[:, :, :, FD], dcum[:, :, :]).then_inc(qa_ready, 1)
            take(WO)
            turned_heads(qt_f, 8)
            take(WO + 1)

            def fox_max(h):
                dve.wait_ge(fs_done, h + 1)
                nc.vector.tensor_reduce(nmax[:, 2 * h:2 * h + 1], ps[:, 4 + h % 2, 0:P], AX.X, ALU.max, negate=True)
                nc.vector.tensor_reduce(nmax[:, 2 * h + 1:2 * h + 2], ps[:, 4 + h % 2, P:3 * P], AX.X, ALU.max,
                                        negate=True).then_inc(fm_ready, 1)

            fox_max(0)
            for h in range(FH):
                if h + 1 < FH:
                    fox_max(h + 1)
                dve.wait_ge(fp_turned, h + 1)
                if h >= 2:
                    dve.wait_ge(fpv_done, h - 1)
                nc.vector.tensor_copy(prob_ft[:, h % 2, :], ps[:, 6 + h % 2, 0:384]).then_inc(fpt_ready, 1)
                if h % 3 == 1 and h < 15:
                    ada_part(72 + h // 3)
            dve.wait_ge(fp_ready, 2 * FH)
            link(nc.vector.reciprocal(prec[:, :], psumr[:, :]))
            dve.wait_ge(fpv_done, FH)
            dve.wait_ge(evac, EVACS + 16)
            for t in range(NT):
                for half in range(2):
                    sums = prec[:, 16 * half + t:16 * half + 16:2]
                    to = o_f[:, t, half * HALF:(half + 1) * HALF]
                    ins = nc.vector.tensor_tensor(to.rearrange("p (h c) -> p h c", h=8),
                                                  ps[:, 2 * t + half, :].rearrange("p (h c) -> p h c", h=8),
                                                  bcast(sums, 2, FD), ALU.mult)
                link(ins)
                nc.vector.tensor_tensor(o_f[:, t, :], o_f[:, t, :], sg[:, t, :], ALU.mult).then_inc(xn_ready, 1)
            low_of_turned(N_FOX)
            for u in range(WO + 2, WO + 5):
                take(u)
            residual(None, 0, R_PM2, done=6)
            extract(9)
            normalise(R_FF2, x, xn)
            take(WO + 5)
            low_of_turned(N_FF2)
            ffn(2)
            residual(None, 1, R_PF2, done=7)

        @block.scalar
        def _(act):
            def hi_part(u, i=None):
                if u >= N_UNITS or u in DIRECT:
                    return
                s, n = split_no(u), width(u)
                more = 0 if i is None else 4 * i
                act.wait_ge(raw_loaded[u % RAW], 32 * (u // RAW + 1) + 8 * more)
                if s >= 2:
                    act.wait_ge(w_used, s - 1 + more)
                nc.scalar.activation(wh[:, s % 2, 0:n], raw[:, u % RAW, 0:n], ACT.Copy).then_inc(hi_done, 1)

            def squares(r, pieces, sqj=junk, x_stage=None):
                for j, src in enumerate(pieces):
                    if x_stage is not None:
                        act.wait_ge(x_ready, 2 * x_stage - 1 + j)
                    c = R_AT[r] + j
                    if SQ_BASE[r] + j >= 1:
                        act.wait_ge(sq_done, SQ_BASE[r] + j)
                    n = src.shape[1]
                    nc.scalar.activation(sqj[:, 0:n], src, ACT.Square, accum_out=ss[:, c:c + 1]).then_inc(sq_done, 1)

            def root(r):
                c0, c1 = R_AT[r], R_AT[r + 1]
                act.wait_ge(ms_ready, r + 1)
                nc.scalar.activation(rt[:, c0:c1], ms[:, c0:c1], ACT.Sqrt).then_inc(rt_ready, 1)

            used = [2]

            def root_table():
                nc.scalar.activation(credit[:, used[0]:used[0] + 1], ones[:, 0:1], ACT.Sqrt)
                used[0] += 1

            def turn_evac(n, b0, hi=None, between=None):
                hi = hi or hh
                for b in range(4):
                    if b == 2 and between is not None:
                        hi_part(between)
                    j = 4 * n + b
                    act.wait_ge(turned, 4 * TURN_NO[n] + b + 1)
                    if j >= 2:
                        act.wait_ge(t_lo, j - 1)
                    for kk in range(2):
                        k = 2 * b + kk
                        nc.scalar.activation(hraw[:, b % 2, kk * TOK:(kk + 1) * TOK],
                                             ps[:, b0 + b, kk * TOK:(kk + 1) * TOK], ACT.Identity,
                                             scale=mod[:, n, 0, k:k + 1], bias=mod[:, n, 1, k:k + 1])\
                            .then_inc(t_raw, 1)
                    act.wait_ge(t_raw, 2 * j + 2)
                    nc.scalar.activation(hi[:, 2 * b:2 * b + 2, :],
                                         hraw[:, b % 2, :].rearrange("p (k t) -> p k t", k=2), ACT.Copy)\
                        .then_inc(t_hi, 1)


            for k in range(KD):
                if k == 2:
                    act.wait_ge(in_const, 16)
                    nc.scalar.activation(credit[:, 15:16], ones[:, 0:1], ACT.Silu)
                    act.wait_ge(in_rows, 16 * sum(len(r) for r in VEC_TILES))
                act.dma_start(mod1_w[k], ada[0][0][k * P:(k + 1) * P, :])\
                    .then_inc(au_loaded[k] if k < 2 else mod1_loaded[k - 2], 16)
            act.wait_ge(cols_ready, 1)
            at = COL[("c", 0)]
            nc.scalar.activation(cs[:, :], col[:, at:at + 24], ACT.Silu).then_inc(cs_ready, 1)
            act.wait_ge(in_small, 16 * 4)
            nc.scalar.activation(lg[:, 1, :], lg[:, 3, :], ACT.Exp).then_inc(lg_exp, 1)
            act.wait_ge(in_x, 16)
            squares(R_X, [x[:, t, :] for t in range(NT)], xn[:, 0, :])
            act.wait_ge(in_ctx, 16)
            squares(R_CTX, [cx[:, t, :] for t in range(NT)], xn_c[:, 0, :])
            root(R_X)
            root(R_CTX)
            hi_part(0)
            hi_part(1)
            act.wait_ge(mod1_used, 8)
            for q in range(2, 4):
                nc.scalar.activation(m1[0:2, q * HALF:(q + 1) * HALF], ps[0:2, q, :], ACT.Copy).then_inc(m1_act, 1)
            act.wait_ge(mod1_ready, 1)
            turn_evac(N_X, 4)
            turn_evac(N_CTX, 0, ch)

            def take_evac(out_, src, fn=ACT.Copy):
                nc.scalar.activation(out_, src, fn).then_inc(evac, 1)

            hi_part(2)
            hi_part(3)
            act.wait_ge(w_used, 3)
            for t in range(4):
                if t < NT:
                    take_evac(cqkv[:, t, :], ps[:, 2 * t, 0:256])
                bank = 2 * t + 1 if t < NT else 2 + t
                take_evac(cqkv[:, 2 + t, :], ps[:, bank, 0:256])
                take_evac(kpe[:, t, :], ps[:, bank, 256:256 + ROPE])
            hi_part(4)
            act.wait_ge(evac, 10)
            squares(R_C, [cqkv[:, j, :] for j in range(6)])
            root(R_C)
            hi_part(5)
            hi_part(6)
            act.wait_ge(w_used, 5)
            for t in range(4):
                take_evac(rk[:, t, :], ps[:, (6, 7, 0, 1)[t], :])
            hi_part(7)
            hi_part(8)
            act.wait_ge(w_used, 7)
            for t in range(4):
                take_evac(rv[:, t, :], ps[:, 2 + t, :])
            hi_part(9)
            hi_part(10)
            act.wait_ge(w_used, 9)
            for t in range(NT):
                take_evac(rq[:, t, :], ps[:, 6 + t, :])
            hi_part(13)
            act.wait_ge(w_used, 11)
            for t in range(NT):
                take_evac(rg[:, t, :], ps[:, t, :], ACT.Silu)
            for kc in range(2):
                act.wait_ge(c_turned, 1)
                nc.scalar.activation(cqt[:, kc, :], ps[:, 2, kc * TOK:(kc + 1) * TOK], ACT.Copy,
                                     scale=column("g_q", 0, kc)).then_inc(ct_ready, 1)
            for kc in range(2):
                act.wait_ge(c_turned, 2 + kc)
                nc.scalar.activation(ckt[:, kc, :], ps[:, (3, 1)[kc], :], ACT.Copy,
                                     scale=column("g_kv", 0, kc)).then_inc(ct_ready, 1)
            for t in range(NT):
                for part, (h0, h1) in enumerate(((0, 5), (5, 8))):
                    act.wait_ge(q_proj, 2 * t + part + 1)
                    nc.scalar.activation(qk_st[:, t, h0:h1, :],
                                         ps[:, 4 + 2 * t + part, 0:(h1 - h0) * QK].rearrange("p (h c) -> p h c",
                                                                                              h=h1 - h0),
                                         ACT.Copy).then_inc(q_evac, 1)
            for q in range(4):
                act.wait_ge(q_turned, 2)
                nc.scalar.activation(qt_m[:, 2 * q:2 * q + 2, :],
                                     ps[0:QK, q, :].rearrange("p (h t) -> p h t", h=2), ACT.Copy,
                                     scale=MLA_SCALE).then_inc(qt_ready, 1)

            def turn_keys(t):
                for half in range(2):
                    act.wait_ge(k_turned, 2 * t + half + 1)
                    nc.scalar.activation(kt_m[:, 4 * half:4 * half + 4, t * P:(t + 1) * P],
                                         ps[0:QK, 2 * (t % 2) + half, :].rearrange("p (h c) -> p h c", h=4),
                                         ACT.Copy).then_inc(kt_ready, 1)

            hi_part(14)
            for t in range(4):
                for half in range(2):
                    act.wait_ge(kv_proj, 2 * t + half + 1)
                    if half == 0:
                        act.wait_ge(q_turned, 2)
                        if t >= 2:
                            act.wait_ge(k_turned, 2 * (t - 2) + 2)
                    src = ps[:, 4 + 2 * (t % 2) + half, :].rearrange("p (h c) -> p h c", h=4)
                    nc.scalar.activation(qk_st[:, t % 2, 4 * half:4 * half + 4, 0:NOPE], src[:, :, 0:NOPE],
                                         ACT.Copy).then_inc(k_evac, 1)
                if t >= 1:
                    turn_keys(t - 1)
            turn_keys(3)
            for it in range(2 * MLA_H):
                act.wait_ge(max_ready, it + 1)
                if it >= 2:
                    act.wait_ge(p_turned, it - 1)
                nc.scalar.activation(prob[:, it % 2, :], ps[:, 4 + it % 2, :], ACT.Exp, bias=nmax[:, it:it + 1],
                                     accum_out=psumr[:, it:it + 1]).then_inc(p_ready, 1)
            for q in range(6):
                act.wait_ge(r_turned, q + 1)
                if q < 2:
                    dst = rqt[:, 2 * q:2 * q + 2, :]
                    src = ps[:, 4 + q, :].rearrange("p (h t) -> p h t", h=2)
                    nc.scalar.activation(dst, src, ACT.Copy).then_inc(rt_evac, 1)
                else:
                    bank = (6, 7, 2, 3)[q - 2]
                    nc.scalar.activation(rkt[:, q - 2, :], ps[:, bank, :], ACT.Copy, scale=RDK ** -0.5)\
                        .then_inc(rt_evac, 1)
            for h in range(RH):
                act.wait_ge(arg_ready, h + 1)
                if h >= 1:
                    act.wait_ge(mask_ready, h)
                nc.scalar.activation(mask[:, h, 0:2, :], mask[:, h, 0:2, :], ACT.Exp)
                nc.scalar.activation(mask[:, h, 2:4, :], diff[:, :, :], ACT.Exp, scale=lg[:, 0, h:h + 1],
                                     bias=lg[:, 2, h:h + 1])
                nc.scalar.activation(mt[:, :, :], diff[:, :, :], ACT.Exp, scale=lg[:, 1, 4 + h:5 + h],
                                     bias=lg[:, 2, 4 + h:5 + h]).then_inc(mask_exp, 1)
            root_table()
            root(R_RET)
            turn_evac(N_RET, 4)
            hi_part(15)
            hi_part(16)
            hi_part(17)
            hi_part(18)
            root_table()
            squares(R_FF0, [x[:, t, :] for t in range(NT)], xn[:, 0, :], 1)
            root(R_FF0)
            turn_evac(N_FF0, 4)

            def ffn(f):
                u0, base = UP[f], 2

                def at_(name, first, k, i):
                    c = COL[(name, first)] + k
                    return col[:, bass.ds(c + 4 * i, 1)] if i is not None else col[:, c:c + 1]

                def up_wait(pp, i):
                    if pp % 2 == 0:
                        act.wait_ge(up_done, NBLK * f + pp // 2 + 1 + (0 if i is None else 2 * i))
                    else:
                        act.wait_ge(w_used, split_no(u0 + pp) + 1 + (0 if i is None else 4 * i))

                def first_step(pp, i=None):
                    more = 0 if i is None else 4 * i
                    c, bank = pp % 2, 4 + pp % 4
                    if f == 0:
                        up_wait(pp, i)
                        act.wait_ge(hid_pool, pp - 1 + CREDIT + more)
                        for half in range(2):
                            nc.scalar.activation(hu[:, c, half, :], ps[:, bank, half * TOK:(half + 1) * TOK],
                                                 ACT.Identity, scale=at_("conv_w", 0, 44 + half * NFF + pp, i),
                                                 bias=at_("conv_b", 0, half * NFF + pp, i)).then_inc(conv_base, 1)
                    else:
                        up_wait(pp, i)
                        act.wait_ge(hid_dve, NFF * (f - 1) + pp - 1 + CREDIT + more)
                        nc.scalar.activation(sl[:, c, :], ps[:, bank, 0:TOK], ACT.Silu).then_inc(silu_done, 1)

                def silu_step(pp, i=None):
                    more = 0 if i is None else 4 * i
                    if f == 0:
                        act.wait_ge(conv_mid, 4 * pp + 4 + 4 * more)
                        nc.scalar.activation(sl[:, pp % 2, :], hu[:, pp % 2, 1, :], ACT.Silu).then_inc(silu_done, 1)

                def high_step(pp, i=None):
                    more = 0 if i is None else 4 * i
                    if f == 0:
                        act.wait_ge(hid_pool, pp + 1 + CREDIT + more)
                    else:
                        act.wait_ge(hid_dve, NFF * (f - 1) + pp + 1 + CREDIT + more)
                    dst = gh[:, bass.ds(pp + more, 1), :] if i is not None else gh[:, pp:pp + 1, :]
                    nc.scalar.activation(dst, hid[:, pp % 2:pp % 2 + 1, :], ACT.Copy).then_inc(gh_done, 1)

                def pair(pp, i=None):
                    hi_part(u0 + base + pp, i)
                    silu_step(pp - 1, i)
                    first_step(pp, i)
                    high_step(pp - 1, i)

                hi_part(u0 + base)
                first_step(0)
                pair(1)
                with act.Fori(0, 4) as i:
                    for pp in range(2, 6):
                        pair(pp, i)
                for pp in range(18, NFF):
                    pair(pp)
                hi_part(DOWN[f] + base)
                silu_step(NFF - 1)
                high_step(NFF - 1)
                for j in range(1, NBLK - 1):
                    hi_part(DOWN[f] + j + base)

            ffn(0)
            hi_part(DOWN[0] + 12)
            root_table()
            squares(R_FIN, [x[:, t, :] for t in range(NT)], xn[:, 0, :], 2)
            root(R_FIN)
            squares(R_MIX1, [x[:, t, :] for t in range(NT)], xn[:, 0, :], 3)
            root(R_MIX1)
            turn_evac(N_MIX1, 4)
            for b in range(4):
                hi_part(GM_V + 2 * b + 2)
                hi_part(GM_V + 2 * b + 3)
                for t in range(NT):
                    act.wait_ge(v_added, 2 * b + t + 1)
                    part = vg[:, t, b * HALF:(b + 1) * HALF]
                    nc.scalar.activation(part, part, ACT.Gelu_apprx_tanh).then_inc(v_gelu, 1)
            root(R_LN)

            def partners(b):
                act.wait_ge(w_used, split_no(U_UNIT[b] + 1) + 1)
                if b >= 2:
                    act.wait_ge(yr_ready, b - 1)
                for c in range(4):
                    nc.scalar.activation(ub[b % 2][:, c, :], ps[:, 4 + c // 2, (c % 2) * TOK:(c % 2 + 1) * TOK],
                                         ACT.Gelu_apprx_tanh, bias=column("a_b_in_2", 0, 4 * b + c))\
                        .then_inc(ub_ready, 1)

            hi_part(60)
            partners(0)
            hi_part(61)
            for b, (before, after) in enumerate((((62, 63), ()), ((64, 65), (66, 67)), ((68, 69), (70, 71)),
                                                 ((), (72, 73)))):
                for u in before:
                    hi_part(u)
                if b < 3:
                    partners(b + 1)
                act.wait_ge(yr_ready, b + 1)
                if b >= 2:
                    act.wait_ge(w_used, split_no(O_UNIT[b - 2] + 1) + 1)
                nc.scalar.activation(yh[:, b % 2], yr[:, :, :], ACT.Copy).then_inc(yh_ready, 1)
                for u in after:
                    hi_part(u)
            hi_part(74)

            def post_squares(r, last_unit):
                root_table()
                act.wait_ge(w_used, split_no(last_unit) + 1)
                squares(r, [ps[:, q, :] for q in range(4)], xn[:, 0, :])
                root(r)

            post_squares(R_PM1, 73)
            hi_part(75)
            squares(R_FF1, [x[:, t, :] for t in range(NT)], xn[:, 0, :], 4)
            root(R_FF1)
            turn_evac(N_FF1, 4)
            ffn(1)
            post_squares(R_PF1, DOWN[1] + 10)
            hi_part(DOWN[1] + 12)
            squares(R_KV, [x[:, t, :] for t in range(NT)], xn[:, 0, :], 5)
            root(R_KV)
            turn_evac(N_KV, 4)
            for b in range(4):
                if b < 3:
                    hi_part(KV + 2 * b + 2)
                hi_part(KV + 2 * b + 3)
                if b == 3:
                    root(R_KH)
                act.wait_ge(w_used, split_no(KV + 2 * b + 1) + 1)
                for t in range(NT):
                    dst = k_st if b < 2 else v_f
                    take_evac(dst[:, t, (b % 2) * HALF:(b % 2 + 1) * HALF], ps[:, 2 * (b % 2) + t, :])
                if b == 2:
                    turn_evac(N_MIX2, 4, hh2, KV + 8)
            hi_part(QG + 1)
            act.wait_ge(w_used, split_no(KV + 8) + 1)
            nc.scalar.activation(f_rows[:, :], ps[0:FH, 4, 0:TOK], ACT.Copy).then_inc(f_copied, 1)

            def turned_heads(to, base):
                for q in range(0, 8, 2):
                    act.wait_ge(f_turned, base + q + 1)
                    nc.scalar.activation(to[:, 2 * q:2 * q + 2, :],
                                         ps[0:FA, 4 + q % 4, :].rearrange("p (h t) -> p h t", h=2), ACT.Copy)\
                        .then_inc(act_step, 1)

            z, az, e1, mn, ln, ls = (fz[:, j] for j in range(6))
            for b in range(4):
                if b < 3:
                    hi_part(QG + 2 * b + 2)
                    hi_part(QG + 2 * b + 3)
                else:
                    hi_part(WO)
                act.wait_ge(w_used, split_no(QG + 2 * b + 1) + 1)
                for t in range(NT):
                    dst = q_st if b < 2 else sg
                    take_evac(dst[:, t, (b % 2) * HALF:(b % 2 + 1) * HALF], ps[:, 2 * (b % 2) + t, :],
                              ACT.Copy if b < 2 else ACT.Sigmoid)
                if b == 0:
                    act.wait_ge(f_pre, 1)
                    nc.scalar.activation(e1, az, ACT.Exp, scale=-1.0).then_inc(f_act, 1)
                    act.wait_ge(f_pre, 2)
                    nc.scalar.activation(ln, e1, ACT.Ln).then_inc(f_act, 1)
                if b == 2:
                    root(R_QH)
                    turned_heads(kt_f, 0)
            hi_part(WO + 1)
            turned_heads(qt_f, 8)
            for h in range(FH):
                act.wait_ge(fm_ready, h + 1)
                if h >= 2:
                    act.wait_ge(fp_turned, h - 1)
                for t in range(NT):
                    lo_, hi_ = (0, P) if t == 0 else (P, 3 * P)
                    nc.scalar.activation(prob_f[:, h % 2, lo_:hi_], ps[:, 4 + h % 2, lo_:hi_], ACT.Exp,
                                         bias=nmax[:, 2 * h + t:2 * h + t + 1],
                                         accum_out=psumr[:, 2 * h + t:2 * h + t + 1]).then_inc(fp_ready, 1)
            turn_evac(N_FOX, 4)
            for u in range(WO + 2, WO + 5):
                hi_part(u)
            post_squares(R_PM2, WO + 3)
            hi_part(WO + 5)
            squares(R_FF2, [x[:, t, :] for t in range(NT)], xn[:, 0, :], 6)
            root(R_FF2)
            turn_evac(N_FF2, 4)
            ffn(2)
            post_squares(R_PF2, DOWN[2] + 10)

        @block.tensor
        def _(pe):
            def three(to, lh, ll, rh, rl, start, stop):
                nc.tensor.matmul(to, lh, rh, start=start, stop=False, skip_group_check=True)
                nc.tensor.matmul(to, lh, rl, start=False, stop=False, skip_group_check=True)
                return nc.tensor.matmul(to, ll, rh, start=False, stop=stop, skip_group_check=True)

            def unit(u, cols, i=None):
                s = split_no(u)
                pe.wait_ge(lo_done, s + 1 + (0 if i is None else 4 * i))
                n = width(u)
                return (wh[:, s % 2, 0:n].rearrange("p (k c) -> p k c", c=cols),
                        wl[:, s % 2, 0:n].rearrange("p (k c) -> p k c", c=cols))

            def turn(n, src, b0, after=None):
                if after is not None:
                    pe.wait_ge(ex_taken, EX_BASE[after + 1])
                pe.wait_ge(xn_ready, XN_NEED[n])
                for b in range(4):
                    for q in range(4):
                        k, t = 2 * b + q // 2, q % 2
                        ins = nc.tensor.transpose(ps[:, b0 + b, q * P:(q + 1) * P], src[:, t, k * P:(k + 1) * P],
                                                  ident)
                    ins.then_inc(turned, 1)

            def rows_product(u, tiles, banks, cols, k0, nk, first, last):
                w_hi, w_lo = unit(u, cols)
                for kk in range(nk):
                    k = k0 + kk
                    for j, (hi, lo, t) in enumerate(tiles):
                        ins = three(banks[j], hi[:, k, t * P:(t + 1) * P], lo[:, k, t * P:(t + 1) * P],
                                    w_hi[:, kk, :], w_lo[:, kk, :], first and kk == 0, last and kk == nk - 1)
                ins.then_inc(w_used, 1)

            def acc_product(u, hi, lo, k0, first, last):
                w_hi, w_lo = unit(u, D)
                for kk in range(2):
                    for t in range(NT):
                        for cb in range(2):
                            cc = slice(cb * HALF, (cb + 1) * HALF)
                            tt = slice(t * P, (t + 1) * P)
                            ins = three(ps[:, 2 * t + cb, :], hi[:, k0 + kk, tt], lo[:, k0 + kk, tt],
                                        w_hi[:, kk, cc], w_lo[:, kk, cc], first and kk == 0, last and kk == 1)
                ins.then_inc(w_used, 1)

            def extract(g):
                ba, b0, b1 = EX_BANKS[g]
                kind, _ = GROUPS[g]
                e = EX_BASE[g]
                pe.wait_ge(acc_step, 8 * g)
                c0, c1 = {"shift_scale": (0, 16), "gate_shift": (8, 16), "scale_gate": (0, 8)}[kind]
                for j, c in enumerate(range(c0, c1)):
                    ins = nc.tensor.matmul(ps[:, ba, j:j + 1], acc[:, c * P:(c + 1) * P], ones[:, 0:1], start=True,
                                           stop=True)
                ins.then_inc(ex_done, 1)
                if kind == "shift_scale":
                    return
                q0 = 0 if kind == "gate_shift" else 2
                for h, bank in ((0, b0), (1, b1)):
                    if bank == ba:
                        pe.wait_ge(ex_taken, e + 1)
                    q = q0 + h
                    nc.tensor.matmul(ps[:, bank, :], ones, acc[:, q * HALF:(q + 1) * HALF], start=True, stop=True)\
                        .then_inc(ex_done, 1)

            pe.wait_ge(in_const, 16)
            pe.wait_ge(acc_biased, 16)
            for q in range(4):
                nc.tensor.matmul(ps[0:2, q, :], ones[:, 0:2], acc[:, q * HALF:(q + 1) * HALF], start=True, stop=False)
            pe.wait_ge(in_rows, 16 * sum(len(r) for r in VEC_TILES))
            for t, n in enumerate(VEC_ROWS):
                nc.tensor.transpose(ps[:, 7, t * P:t * P + n], vrow[0:n, t, :], ident[0:n, 0:n]).then_inc(cols_turned, 1)
            pe.wait_ge(cs_ready, 1)
            for k in range(KD):
                pe.wait_ge(au_loaded[k] if k < 2 else mod1_loaded[k - 2], 16)
                for q in range(4):
                    ins = nc.tensor.matmul(ps[0:2, q, :], cs[:, k:k + 9:8], mod1_w[k][:, q * HALF:(q + 1) * HALF],
                                           start=False, stop=(k == KD - 1))
                ins.then_inc(mod1_used, 1)
            pe.wait_ge(m1_ready, 2)
            pe.wait_ge(m1_act, 2)
            for c in range(16):
                ins = nc.tensor.transpose(ps[:, 6, 2 * c:2 * c + 2], m1[0:2, c * P:(c + 1) * P], ident[0:2, 0:2])
            ins.then_inc(m1_turned, 1)
            pe.wait_ge(mod1_ready, 1)
            turn(N_X, xn, 4)
            turn(N_CTX, xn_c, 0)
            lat = [(hh, hl, t) for t in range(NT)]
            con_ = [(ch, cl, t) for t in range(NT)]
            pe.wait_ge(t_lo, 8)
            for u, k0 in enumerate(range(0, KD, 3)):
                w_hi, w_lo = unit(u, CKV)
                for kk in range(min(3, KD - k0)):
                    k = k0 + kk
                    first, last = k == 0, k == KD - 1
                    for j, (hi, lo, t) in enumerate(lat + con_):
                        tt = slice(t * P, (t + 1) * P)
                        if j < NT:
                            three(ps[:, 2 * j, 0:256], hi[:, k, tt], lo[:, k, tt], w_hi[:, kk, 0:256],
                                  w_lo[:, kk, 0:256], first, last)
                        to = ps[:, 2 * j + 1 if j < NT else 2 + j, 0:CKV - 256]
                        ins = three(to, hi[:, k, tt], lo[:, k, tt], w_hi[:, kk, 256:], w_lo[:, kk, 256:], first, last)
                ins.then_inc(w_used, 1)
            for u, tiles, banks, freed in ((3, lat + con_, (6, 7, 0, 1), 3), (5, lat + con_, (2, 3, 4, 5), 10),
                                           (7, lat, (6, 7), 12), (9, lat, (0, 1), 14)):
                pe.wait_ge(evac, freed)
                for h in range(2):
                    rows_product(u + h, tiles, [ps[:, b, :] for b in banks], 512, 4 * h, 4, h == 0, h == 1)
            pe.wait_ge(cn_ready, 6)
            pe.wait_ge(evac, 18)
            for n, (bank, tiles) in enumerate(((2, (0, 1)), (3, (2, 3, 4, 5)), (1, (2, 3, 4, 5)))):
                if n == 2:
                    pe.wait_ge(evac, EVACS)
                for q in range(4):
                    if n == 0:
                        j, kc = tiles[q % 2], q // 2
                    else:
                        j, kc = tiles[q], n - 1
                    ins = nc.tensor.transpose(ps[:, bank, q * P:(q + 1) * P], cqkv[:, j, kc * P:(kc + 1) * P], ident)
                ins.then_inc(c_turned, 1)
            extract(1)
            uq = raw[:, W_UQ % RAW, 0:2 * MLA_H * QK].rearrange("p (k c) -> p k c", k=2)
            pe.wait_ge(raw_loaded[W_UQ % RAW], 32 * (W_UQ // RAW + 1))
            pe.wait_ge(ct_ready, 2)
            for t in range(NT):
                for part, (c0, c1) in enumerate(((0, 5 * QK), (5 * QK, 8 * QK))):
                    if 2 * t + part in (1, 2):
                        pe.wait_ge(ex_taken, 1 if part else 3)
                    for kc in range(2):
                        ins = nc.tensor.matmul(ps[:, 4 + 2 * t + part, 0:c1 - c0], cqt[:, kc, t * P:(t + 1) * P],
                                               uq[:, kc, c0:c1], start=(kc == 0), stop=(kc == 1))
                    ins.then_inc(q_proj, 1)
            for t in range(NT):
                pe.wait_ge(q_roped, t + 1)
                if t == 0:
                    pe.wait_ge(ct_ready, 4)
                for h in range(MLA_H):
                    at = (h % 2) * TOK + t * P
                    ins = nc.tensor.transpose(ps[0:QK, h // 2, at:at + P], qk_st[:, t, h, :], ident)
                ins.then_inc(q_turned, 1)
            ukv = raw[:, W_UKV % RAW, :].rearrange("p (k c) -> p k c", k=2)
            pe.wait_ge(raw_loaded[W_UKV % RAW], 32 * (W_UKV // RAW + 1))

            def turn_keys(t):
                pe.wait_ge(k_full, t + 1)
                pe.wait_ge(k_evac, 2 * t + 2)
                if t < 2:
                    pe.wait_ge(qt_ready, 4)
                else:
                    pe.wait_ge(kt_ready, 2 * (t - 2) + 2)
                for h in range(MLA_H):
                    ins = nc.tensor.transpose(ps[0:QK, 2 * (t % 2) + h // 4, (h % 4) * P:(h % 4 + 1) * P],
                                              qk_st[:, t % 2, h, :], ident)
                    if h % 4 == 3:
                        ins.then_inc(k_turned, 1)

            for t in range(4):
                for half in range(2):
                    if t >= 2:
                        pe.wait_ge(v_evac, 2 * (t - 2) + half + 1)
                    else:
                        pe.wait_ge(q_evac, 2 * t + half + 1)
                    for kc in range(2):
                        ins = nc.tensor.matmul(ps[:, 4 + 2 * (t % 2) + half, :], ckt[:, kc, t * P:(t + 1) * P],
                                               ukv[:, kc, half * HALF:(half + 1) * HALF], start=(kc == 0),
                                               stop=(kc == 1))
                    ins.then_inc(kv_proj, 1)
                if t >= 1:
                    turn_keys(t - 1)
            turn_keys(3)
            pe.wait_ge(v_evac, 8)
            pe.wait_ge(kt_ready, 8)

            def scores(it):
                h, t = it // 2, it % 2
                if it >= 2:
                    pe.wait_ge(p_ready, it - 1)
                nc.tensor.matmul(ps[:, 4 + it % 2, :], qt_m[:, h, t * P:(t + 1) * P], kt_m[:, h, :], start=True,
                                 stop=True).then_inc(score, 1)

            def turn_probs(it):
                pe.wait_ge(p_ready, it + 1)
                if it >= 2:
                    pe.wait_ge(pt_ready, it - 1)
                for q in range(4):
                    ins = nc.tensor.transpose(ps[:, 6 + it % 2, q * P:(q + 1) * P],
                                              prob[:, it % 2, q * P:(q + 1) * P], ident)
                ins.then_inc(p_turned, 1)

            def values(it):
                h, t = it // 2, it % 2
                pe.wait_ge(pt_ready, it + 1)
                for q in range(4):
                    ins = nc.tensor.matmul(ps[:, t, h * MLA_V:(h + 1) * MLA_V], prob_t[:, it % 2, q * P:(q + 1) * P],
                                           v_m[:, q, h, :], start=(q == 0), stop=(q == 3))
                ins.then_inc(pv_done, 1)

            scores(0)
            for it in range(2 * MLA_H):
                if it + 1 < 2 * MLA_H:
                    scores(it + 1)
                turn_probs(it)
                if it >= 1:
                    values(it - 1)
            values(2 * MLA_H - 1)
            pe.wait_ge(ret_roped, 4)
            pe.wait_ge(p_ready, 2 * MLA_H)
            for q in range(2):
                for j in range(4):
                    h, t = 2 * q + j // 2, j % 2
                    ins = nc.tensor.transpose(ps[:, 4 + q, j * P:(j + 1) * P], rq[:, t, h * RDK:(h + 1) * RDK], ident)
                ins.then_inc(r_turned, 1)
            pe.wait_ge(pt_ready, 2 * MLA_H)
            for h, bank in enumerate((6, 7, 2, 3)):
                for t in range(4):
                    ins = nc.tensor.transpose(ps[:, bank, t * P:(t + 1) * P], rk[:, t, h * RDK:(h + 1) * RDK], ident)
                ins.then_inc(r_turned, 1)
            pe.wait_ge(rt_evac, 6)

            def decayed(h):
                for half in range(2):
                    if h >= 2:
                        pe.wait_ge(pr_ready, 2 * (h - 2) + half + 1)
                    for j in range(2):
                        kt = 2 * half + j
                        ins = nc.tensor.matmul(ps[:, 4 + 2 * (h % 2) + half, j * TOK:(j + 1) * TOK],
                                               rkt[:, h, kt * P:(kt + 1) * P], rqt[:, h, :], start=True, stop=True)
                    ins.then_inc(att_done, 1)

            def retained(h):
                pe.wait_ge(pr_ready, 2 * h + 2)
                for t in range(NT):
                    for kt in range(4):
                        ins = nc.tensor.matmul(ps[:, t, h * RDK:(h + 1) * RDK], pr[:, h % 2, kt, t * P:(t + 1) * P],
                                               rv[:, kt, h * RDK:(h + 1) * RDK], start=(kt == 0), stop=(kt == 3))
                ins.then_inc(y_done, 1)

            decayed(0)
            for h in range(RH):
                if h + 1 < RH:
                    decayed(h + 1)
                retained(h)
            turn(N_RET, o, 4)
            for j in range(4):
                pe.wait_ge(t_lo, 4 * N_RET + j + 1)
                acc_product(W_OUT + j, hh, hl, 2 * j, j == 0, j == 3)
            extract(2)

            def up_unit(f, u, b_in, h, i=None):
                more = 0 if i is None else 4 * i
                w_hi, w_lo = unit(u, 512, i)
                for c in range(2):
                    pp = 2 * b_in + c
                    if h == 0:
                        if f == 0:
                            pe.wait_ge(hid_pool, pp - 3 + CREDIT + more)
                        else:
                            pe.wait_ge(hid_dve, NFF * (f - 1) + pp - 3 + CREDIT + more)
                    for s in range(2):
                        to = ps[:, 4 + pp % 4, s * TOK:(s + 1) * TOK]
                        for kk in range(4):
                            k = 4 * h + kk
                            cc = slice(s * 256 + c * P, s * 256 + (c + 1) * P)
                            wh_, wl_ = w_hi[:, kk, cc], w_lo[:, kk, cc]
                            ins = three(to, wh_, wl_, hh[:, k, :], hl[:, k, :], h == 0 and s == 0 and kk == 0,
                                        h == 1 and kk == 3)
                    if h == 1 and c == 0:
                        ins.then_inc(up_done, 1)
                    elif h == 1:
                        ins.then_inc(w_used, 1)
                if h == 0:
                    ins.then_inc(w_used, 1)

            def ffn(f):
                u0 = UP[f]
                with pe.Fori(0, 4) as i:
                    for b in range(2):
                        for h in range(2):
                            pe.wait_ge(t_lo, 4 * (N_FF0, N_FF1, N_FF2)[f] + 2 * h + 2)
                            up_unit(f, u0 + 2 * b + h, b, h, i)
                for b in range(8, NBLK):
                    for h in range(2):
                        up_unit(f, u0 + 2 * b + h, b, h)
                for j in range(NBLK):
                    pe.wait_ge(gl_done, NFF * f + 2 * j + 2 + CREDIT)
                    acc_product(DOWN[f] + j, gh, gl, 2 * j, j == 0, j == NBLK - 1)
                    if f == 1 and j == 3:
                        extract(6)

            turn(N_FF0, xn, 4, 2)
            ffn(0)
            extract(3)
            turn(N_MIX1, xn, 4, 3)
            for b in range(4):
                if b >= 2:
                    pe.wait_ge(v_added, 2 * (b - 2) + 2)
                for h in range(2):
                    pe.wait_ge(t_lo, 4 * N_MIX1 + 2 * h + 2)
                    rows_product(GM_V + 2 * b + h, lat, [ps[:, 4 + 2 * (b % 2) + t, :] for t in range(2)], 512,
                                 4 * h, 4, h == 0, h == 1)
            pe.wait_ge(ws_loaded, 16)
            for q in range(4):
                for j in range(4):
                    ins = nc.tensor.transpose(ps[:, q, j * P:(j + 1) * P], wsr[:, 4 * q + j, :], ident)
                ins.then_inc(ws_turned, 1)
            pe.wait_ge(v_added, 6)
            extract(4)

            def partners(b):
                if b == 0:
                    pe.wait_ge(ex_taken, EX_BASE[5])
                else:
                    pe.wait_ge(ub_ready, 4 * b)
                for h in range(2):
                    w_hi, w_lo = unit(U_UNIT[b] + h, 512)
                    for c in range(4):
                        for kk in range(4):
                            k = 4 * h + kk
                            ins = three(ps[:, 4 + c // 2, (c % 2) * TOK:(c % 2 + 1) * TOK],
                                        w_hi[:, kk, c * P:(c + 1) * P], w_lo[:, kk, c * P:(c + 1) * P],
                                        hh[:, k, :], hl[:, k, :], h == 0 and c % 2 == 0 and kk == 0,
                                        h == 1 and kk == 3)
                    ins.then_inc(w_used, 1)

            def spatial(b):
                if b == 0:
                    pe.wait_ge(wst_ready, 4)
                    pe.wait_ge(affine, 8)
                else:
                    pe.wait_ge(yr_ready, b)
                for g in range(4):
                    for n in range(NT):
                        gg = 4 * b + g
                        ins = nc.tensor.matmul(ps[:, 6 + g // 2, (g % 2) * TOK + n * P:(g % 2) * TOK + (n + 1) * P],
                                               vg[:, n, gg * P:(gg + 1) * P], wst[:, gg, :], start=True, stop=True)
                ins.then_inc(sp_done, 1)

            def output_part(b):
                pe.wait_ge(yl_ready, b + 1)
                for j in range(2):
                    w_hi, w_lo = unit(O_UNIT[b] + j, D)
                    for kk in range(2):
                        for t in range(NT):
                            for cb in range(2):
                                cc, tt = slice(cb * HALF, (cb + 1) * HALF), slice(t * P, (t + 1) * P)
                                kq = 2 * j + kk
                                ins = three(ps[:, 2 * t + cb, :], yh[:, b % 2, kq, tt], yl[:, b % 2, kq, tt],
                                            w_hi[:, kk, cc], w_lo[:, kk, cc], b == 0 and kq == 0, b == 3 and kq == 3)
                    ins.then_inc(w_used, 1)

            partners(0)
            for b in range(5):
                if b < 3:
                    partners(b + 1)
                if b < 4:
                    spatial(b)
                if b > 0:
                    output_part(b - 1)
            extract(5)
            turn(N_FF1, xn, 4, 5)
            ffn(1)
            turn(N_KV, xn, 4, 6)
            for b in range(4):
                if b == 2:
                    pe.wait_ge(evac, EVACS + 2)
                    extract(7)
                    pe.wait_ge(ex_taken, EX_BASE[8])
                elif b == 3:
                    pe.wait_ge(evac, EVACS + 4)
                for h in range(2):
                    pe.wait_ge(t_lo, 4 * N_KV + 2 * h + 2)
                    rows_product(KV + 2 * b + h, lat, [ps[:, 2 * (b % 2) + t, :] for t in range(2)], 512,
                                 4 * h, 4, h == 0, h == 1)
            pe.wait_ge(t_raw, 2 * (4 * N_MIX2 + 1))
            w_hi, w_lo = unit(KV + 8, FH)
            for k in range(KD):
                ins = three(ps[0:FH, 4, 0:TOK], w_hi[:, k, :], w_lo[:, k, :], hh[:, k, :], hl[:, k, :], k == 0,
                            k == KD - 1)
            ins.then_inc(w_used, 1)

            def queries_gates(b):
                pe.wait_ge(evac, EVACS + 6 + 2 * b)
                for h in range(2):
                    pe.wait_ge(t_lo, 4 * N_MIX2 + 2 * h + 2)
                    rows_product(QG + 2 * b + h, [(hh2, hl2, t) for t in range(NT)],
                                 [ps[:, 2 * (b % 2) + t, :] for t in range(2)], 512, 4 * h, 4, h == 0, h == 1)

            def turn_heads(src, base):
                for q in range(8):
                    if base + q >= 4:
                        p_ = base + q - 4
                        pe.wait_ge(ft_evac if p_ % 2 else act_step, p_ // 2 + 1)
                    for j in range(4):
                        h, t = 2 * q + j // 2, j % 2
                        ins = nc.tensor.transpose(ps[0:FA, 4 + q % 4, j * P:(j + 1) * P], src[:, t, h, :], ident)
                    ins.then_inc(f_turned, 1)

            queries_gates(0)
            pe.wait_ge(f_copied, 1)
            for t in range(NT):
                ins = nc.tensor.transpose(ps[:, 4, TOK + t * FH:TOK + (t + 1) * FH], f_rows[:, t * P:(t + 1) * P],
                                          ident[0:FH, 0:FH])
            ins.then_inc(f_cols, 1)
            queries_gates(1)
            pe.wait_ge(ls_ready, 1)
            ls = fz[:, 5]
            nc.tensor.matmul(ps[:, 5, 0:FH], tri, ls[:, 0, :], start=True, stop=True)
            nc.tensor.matmul(ps[:, 5, FH:2 * FH], tri, ls[:, 1, :], start=True, stop=False)
            nc.tensor.matmul(ps[:, 5, FH:2 * FH], ones, ls[:, 0, :], start=False, stop=True).then_inc(cum_done, 1)
            queries_gates(2)
            extract(8)
            pe.wait_ge(ka_ready, 1)
            pe.wait_ge(ex_taken, EX_BASE[9])
            turn_heads(ka, 0)
            queries_gates(3)
            pe.wait_ge(qa_ready, 1)
            turn_heads(qa, 8)
            pe.wait_ge(ft_evac, 8)
            pe.wait_ge(act_step, 8)
            pe.wait_ge(evac, EVACS + 16)

            def fox_scores(h):
                if h >= 2:
                    pe.wait_ge(fp_ready, 2 * (h - 1))
                bank = 4 + h % 2
                nc.tensor.matmul(ps[:, bank, 0:P], qt_f[:, h, 0:P], kt_f[:, h, 0:P], start=True, stop=False,
                                 skip_group_check=True)
                nc.tensor.matmul(ps[:, bank, 0:P], ident, neg, start=False, stop=True, skip_group_check=True)
                nc.tensor.matmul(ps[:, bank, P:3 * P], qt_f[:, h, P:2 * P], kt_f[:, h, :], start=False, stop=False,
                                 skip_group_check=True)
                nc.tensor.matmul(ps[:, bank, 2 * P:3 * P], ident, neg, start=False, stop=True,
                                 skip_group_check=True).then_inc(fs_done, 1)

            def fox_turn(h):
                pe.wait_ge(fp_ready, 2 * h + 2)
                if h >= 2:
                    pe.wait_ge(fpt_ready, h - 1)
                for q in range(3):
                    ins = nc.tensor.transpose(ps[:, 6 + h % 2, q * P:(q + 1) * P],
                                              prob_f[:, h % 2, q * P:(q + 1) * P], ident)
                ins.then_inc(fp_turned, 1)

            def fox_values(h):
                pe.wait_ge(fpt_ready, h + 1)
                cc = slice((h % 8) * FD, (h % 8 + 1) * FD)
                vv = slice(h * FD, (h + 1) * FD)
                nc.tensor.matmul(ps[:, h // 8, cc], prob_ft[:, h % 2, 0:P], v_f[:, 0, vv], start=True, stop=True)
                nc.tensor.matmul(ps[:, 2 + h // 8, cc], prob_ft[:, h % 2, P:2 * P], v_f[:, 0, vv], start=True,
                                 stop=False)
                nc.tensor.matmul(ps[:, 2 + h // 8, cc], prob_ft[:, h % 2, 2 * P:3 * P], v_f[:, 1, vv], start=False,
                                 stop=True).then_inc(fpv_done, 1)

            fox_scores(0)
            for h in range(FH):
                if h + 1 < FH:
                    fox_scores(h + 1)
                fox_turn(h)
                if h >= 1:
                    fox_values(h - 1)
            fox_values(FH - 1)
            turn(N_FOX, o_f, 4)
            for j in range(4):
                pe.wait_ge(t_lo, 4 * N_FOX + j + 1)
                acc_product(WO + j, hh, hl, 2 * j, j == 0, j == 3)
            extract(9)
            turn(N_FF2, xn, 4, 9)
            ffn(2)

        @block.gpsimd
        def _(pool):
            steps = [0]

            def link(ins):
                steps[0] += 1
                ins.then_inc(pool_step, 1)
                pool.wait_ge(pool_step, steps[0])

            def flat(v):
                return v.rearrange("a b -> (a b)") if len(v.shape) == 2 else v

            def start_acc(g):
                if g == 1:
                    pool.wait_ge(mod1_used, 1)
                elif g > 1:
                    pool.wait_ge(ex_done, EX_BASE[g])
                nc.gpsimd.memset(acc[:, :], 0.0).then_inc(acc_zeroed, 1)
                pool.wait_ge(acc_zeroed, g + 1)
                pool.dma_start(acc[0:1, :], ada[g][1]).then_inc(acc_biased, 16)

            post_rows = [a["g_final"], a["post_mix_g_2"][0], a["post_ffn_g_2"][0], a["post_mix_g_2"][1],
                         a["post_ffn_g_2"][1]]

            def load_postg(k):
                pool.dma_start(postg[:, :], post_rows[k].partition_broadcast(P)).then_inc(postg_loaded, 16)

            a_bias, ln_g, ln_b = a["a_b_in_2"][0], a["a_ln_g_2"][0], a["a_ln_b_2"][0]
            b_s = a["a_b_s_2"][0].rearrange("g t -> (g t)")
            bc_rows = [a_bias[GW + b * HALF:GW + (b + 1) * HALF] for b in range(4)]
            for b in range(4):
                bc_rows += [ln_g[b * HALF:(b + 1) * HALF], ln_b[b * HALF:(b + 1) * HALF]]
            bc_rows += [b_s[b * HALF:(b + 1) * HALF] for b in range(4)]

            def load_bc(j):
                if 4 <= j < 8:
                    pool.wait_ge(v_added, 2 * (j - 4) + 2)
                elif j >= 8:
                    pool.wait_ge(affine, j - 7)
                pool.dma_start(bc[:, j % 4, :], bc_rows[j].partition_broadcast(P)).then_inc(bc_loaded[j % 4], 16)

            nc.gpsimd.memset(credit[:, 0:1], 0.0).then_inc(hid_pool, CREDIT)
            nc.gpsimd.memset(credit[:, 1:2], 0.0).then_inc(gl_done, CREDIT)
            start_acc(0)
            pool.dma_start(lg[:, 3, :], a["ret_decay"][0].rearrange("d h -> (d h)").partition_broadcast(P))\
                .then_inc(in_small, 16)
            pool.dma_start(bf[:, :], a["kv_b_f_2"].partition_broadcast(P)).then_inc(in_small, 16)
            pool.dma_start(gq[:, 0, :], a["b_q_norm_g_2"][0].partition_broadcast(P)).then_inc(in_small, 16)
            pool.dma_start(gq[:, 1, :], a["k_norm_g_2"].partition_broadcast(P)).then_inc(in_small, 16)
            load_postg(0)
            start_acc(1)
            pool.wait_ge(evac, 20)
            pool.wait_ge(sq_done, SQ_BASE[R_C + 1])
            rb = rtmp_pool.rearrange("p (h a c) -> p h a c", h=RH, a=2)
            for src in (rq, rk):
                for t in range(NT):
                    xv = src[:, t, :].rearrange("p (h a c) -> p h a c", h=RH, a=2)
                    s_ = bcast(sin_r[:, t, :], 1, RH)
                    c_ = bcast(bcast(cos_r[:, t, :], 1, 2), 1, RH)
                    nc.gpsimd.tensor_tensor(rb[:, :, 0, :], xv[:, :, 1, :], s_, ALU.mult)
                    link(nc.gpsimd.tensor_tensor(rb[:, :, 1, :], xv[:, :, 0, :], s_, ALU.mult))
                    link(nc.gpsimd.tensor_tensor(xv, xv, c_, ALU.mult))
                    nc.gpsimd.tensor_tensor(xv[:, :, 0, :], xv[:, :, 0, :], rb[:, :, 0, :], ALU.subtract)
                    ins = nc.gpsimd.tensor_tensor(xv[:, :, 1, :], xv[:, :, 1, :], rb[:, :, 1, :], ALU.add)
                    ins.then_inc(ret_roped, 1)
                    pool.wait_ge(ret_roped, (0 if src is rq else 2) + t + 1)
            start_acc(2)
            pool.wait_ge(pv_done, 2 * MLA_H)
            at = CONST_AT["diff"]
            pool.dma_start(diff[:, :, :], a["shape_consts"][:, at:at + NT * TOK].rearrange("p (t c) -> p t c", t=NT))\
                .then_inc(diff_loaded, 16)
            for h in range(RH):
                pool.wait_ge(mask_exp, h + 1)
                nc.gpsimd.tensor_tensor(mask[:, h, 2:4, :], mask[:, h, 2:4, :], mt[:, :, :], ALU.add)\
                    .then_inc(mask_ready, 1)
            start_acc(3)

            def pair(f, pp, i=None):
                more = 0 if i is None else 4 * i
                n, c = NFF * f + pp, pp % 2
                if f == 0:
                    pool.wait_ge(silu_done, n + 1 + more)
                    pool.wait_ge(gl_done, n - 1 + CREDIT + more)
                    nc.gpsimd.tensor_tensor(hid[:, c, :], sl[:, c, :], hu[:, c, 0, :], ALU.mult).then_inc(hid_pool, 1)
                pool.wait_ge(gh_done, n + 1 + more)
                at_ = bass.ds(pp + more, 1) if i is not None else slice(pp, pp + 1)
                nc.gpsimd.tensor_tensor(gl[:, at_, :], hid[:, c:c + 1, :], gh[:, at_, :].bitcast(F32), ALU.subtract)\
                    .then_inc(gl_done, 1)

            def ffn(f):
                with pool.Fori(0, 4) as i:
                    for j in range(4):
                        pair(f, j, i)
                for pp in range(16, NFF):
                    pair(f, pp)

            ffn(0)
            pool.wait_ge(w_used, split_no(DOWN[0] + 10) + 1)
            for j in range(4):
                load_bc(j)
            pool.dma_start(wsr[:, :, :], a["a_w_s_2"][0].rearrange("g t s -> t g s")).then_inc(ws_loaded, 16)
            start_acc(4)
            pool.wait_ge(x_ready, 6)
            load_postg(1)
            for j in range(4, 8):
                load_bc(j)
            start_acc(5)
            pool.wait_ge(ex_taken, EX_BASE[4] + 3)
            load_postg(2)
            for j in range(8, 16):
                load_bc(j)
            start_acc(6)
            pool.wait_ge(ex_taken, EX_BASE[5] + 3)
            load_postg(3)
            ffn(1)
            start_acc(7)
            start_acc(8)
            for src, sq, base in ((k_st, ksq, EVACS + 3), (q_st, qsq, EVACS + 11)):
                if src is q_st:
                    pool.wait_ge(k_scaled, NT)
                for t in range(NT):
                    pool.wait_ge(evac, base + t)
                    nc.gpsimd.tensor_tensor(sq[:, t, :], src[:, t, :], src[:, t, :], ALU.mult).then_inc(head_sq, 1)
            start_acc(9)
            pool.wait_ge(ex_taken, EX_BASE[8] + 3)
            load_postg(4)
            ffn(2)

        @block.sync
        def _(sp):
            def send(u):
                if u >= N_UNITS:
                    return
                src = units[u]
                if u >= RAW:
                    q = u - RAW
                    if q == W_UQ:
                        sp.wait_ge(q_proj, 4)
                    elif q == W_UKV:
                        sp.wait_ge(kv_proj, 8)
                    else:
                        sp.wait_ge(lo_done, split_no(q) + 1)
                dst = raw[:, u % RAW, 0:width(u)]
                if isinstance(src, tuple):
                    _, f, b, h = src
                    send_up(f, u % RAW, b, h)
                else:
                    chunks = src.shape[1]
                    dst = dst.rearrange("p (k c) -> p k c", k=chunks)
                    for part in (slice(0, chunks // 2), slice(chunks // 2, chunks)):
                        sp.dma_start(dst[:, part], src[:, part])\
                            .then_inc(raw_loaded[u % RAW], 16)

            def send_up(f, slot, b, h):
                dst = raw[:, slot, :].rearrange("p (k s c) -> p k s c", k=4, s=2)
                src = pair_blocks(up_w[f], b, h)
                for s in range(2):
                    sp.dma_start(dst[:, :, s], src[:, :, s]).then_inc(raw_loaded[slot], 16)

            def send_ada(v):
                if v >= 80:
                    return
                if v < 10:
                    sp.wait_ge(mod1_used, v - 7)
                else:
                    sp.wait_ge(acc_step, v - 9)
                k = v % 8
                sp.dma_start(au[:, v % 2, :], ada[v // 8][0][k * P:(k + 1) * P, :]).then_inc(au_loaded[v % 2], 16)

            sp.dma_start(con[:, :], a["shape_consts"][:, 0:CONST_AT["diff"]]).then_inc(in_const, 16)
            for t, rows in enumerate(VEC_TILES):
                r = 0
                for name, first, n in rows:
                    v = a[name]
                    if len(v.shape) == 2:
                        v = v.rearrange("a b -> (a b)")
                    elif len(v.shape) == 3:
                        v = v.rearrange("a b c -> (a b c)")
                    sp.dma_start(vrow[r:r + n, t, :], v[first:first + n * P].rearrange("(r c) -> r c", c=P))\
                        .then_inc(in_rows, 16)
                    r += n
            sp.wait_ge(mod1_used, 1)
            sp.dma_start(x[:, :, :], a["x"][0].rearrange("(t p) d -> p t d", p=P)).then_inc(in_x, 16)
            sp.dma_start(cx[:, :, :], a["ctx"][0].rearrange("(t p) d -> p t d", p=P)).then_inc(in_ctx, 16)
            sp.wait_ge(mod1_used, 3)
            for u in range(RAW):
                send(u)
            send_ada(8)
            send_ada(9)
            k = 0
            loops = {UP[f] + 2: f for f in range(3)}
            while k < len(taken):
                kind, n = taken[k]
                if kind == "w" and n in loops:
                    f = loops[n]
                    assert taken[k:k + 16] == [("w", n + j) for j in range(16)]
                    u0 = n + RAW
                    with sp.Fori(0, 4) as i:
                        for j in range(4):
                            sp.wait_ge(lo_done, split_no(n + j) + 1 + 4 * i)
                            send_up(f, (u0 + j) % RAW, 3 + j // 2 + 2 * i, j % 2)
                    k += 16
                    continue
                if kind == "w":
                    send(n + RAW)
                else:
                    send_ada(n + 2)
                k += 1
            for t in range(NT):
                sp.wait_ge(x_ready, 13 + t)
                sp.dma_start(out[0, t * P:(t + 1) * P, :], x[:, t, :]).then_inc(out_sent, 16)
            sp.wait_ge(out_sent, 32)


_INS = ["x", "c", "ctx", "c_ctx", "w_ada", "b_ada", "g_norm1", "w_in", "g_q", "w_uq", "g_kv", "w_ukv", "ret_decay",
        "g_ret", "w_out", "g_norm2", "w_up", "conv_w", "conv_b", "w_down", "g_final", "c_2", "ada_w_2", "ada_b_2",
        "pre_mix_g_2", "post_mix_g_2", "pre_ffn_g_2", "post_ffn_g_2", "ffn_w_gu_2", "ffn_w_down_2", "a_w_in_2",
        "a_b_in_2", "a_ln_g_2", "a_ln_b_2", "a_w_s_2", "a_b_s_2", "a_w_out_2", "kv_ada_w_2", "kv_ada_b_2",
        "kv_norm_g_2", "kv_w_2", "kv_b_f_2", "k_norm_g_2", "b_w_qg_2", "b_q_norm_g_2", "b_w_o_2"]


def kernel(**inputs):
    import concourse.bacc as bacc
    from concourse.bass_utils import run_bass_kernel_spmd as run

    nc = bacc.Bacc("TRN2", target_bir_lowering=False, num_devices=1)
    arrays, args = {}, {}
    for name in _INS:
        v = np.ascontiguousarray(inputs[name])
        arrays[f"in_{name}_dram"] = v
        args[name] = nc.dram_tensor(f"in_{name}_dram", v.shape, mybir.dt.from_np(v.dtype), kind="ExternalInput").ap()
    table = shape_constants()
    arrays["in_shape_consts_dram"] = table
    args["shape_consts"] = nc.dram_tensor("in_shape_consts_dram", table.shape, F32, kind="ExternalInput").ap()
    out = nc.dram_tensor("out_0_dram", (1, TOK, D), F32, kind="ExternalOutput").ap()
    build(nc, args, out)
    r = run(nc, [arrays], core_ids=[0])
    return r.results[0]["out_0_dram"]
```
